# Optimizing a Trainium2 kernel written in Bass

```python
import jax
import jax.numpy as jnp
from jax import lax
import numpy as np
import jax, jax.numpy as jnp

D_MODEL = 1024
BATCH = 1
SEQ = 256
DEPTH = 2

N_MEM = 256
HEAD_DIM = 64
ROPE_THETA = 500000.0
ROPE_FRACTION = 4
RMS_EPS = 1e-6
NEG_INF = -1e30
TINY = 1e-20

DSA_HEADS = 8
DSA_IDX_HEADS = 8
DSA_IDX_DIM = 32
DSA_TOPK = 256
DSA_QBLOCK = 128

MOBA_HEADS = 8
MOBA_BLOCK = 256
MOBA_TOPK = 3
MOBA_QBLOCK = 32

NSA_HEADS = 16
NSA_GROUPS = 4
NSA_CMP_LEN = 32
NSA_CMP_STRIDE = 16
NSA_SEL_LEN = 64
NSA_SEL_TOPK = 16
NSA_WINDOW = 512
NSA_QBLOCK = 32
NSA_FORCE = 1e4

MEM_HEADS = 4
MEM_HEAD_DIM = 128

D_FF = ((8 * D_MODEL + 3 * 256 - 1) // (3 * 256)) * 256

AB_SIZES = (DSA_HEADS * HEAD_DIM, HEAD_DIM, HEAD_DIM, DSA_IDX_HEADS * DSA_IDX_DIM, DSA_IDX_DIM, DSA_IDX_HEADS, MOBA_HEADS * HEAD_DIM, MOBA_HEADS * HEAD_DIM, MOBA_HEADS * HEAD_DIM)
AB_WIDTH = sum(AB_SIZES)
AB_MIX_WIDTH = (DSA_HEADS + MOBA_HEADS) * HEAD_DIM
C_SIZES = (NSA_HEADS * HEAD_DIM,) + (NSA_GROUPS * HEAD_DIM,) * 6 + (NSA_HEADS * 3,)
C_WIDTH = sum(C_SIZES)
C_MIX_WIDTH = NSA_HEADS * HEAD_DIM


def rms_norm(x, gain):
    xf = x.astype(jnp.float32)
    y = xf * lax.rsqrt(jnp.mean(xf * xf, axis=-1, keepdims=True) + RMS_EPS)
    return (y * gain.astype(jnp.float32)).astype(x.dtype)

def partial_rope(x, positions):
    dh = x.shape[-1]
    rot = dh // ROPE_FRACTION
    half = rot // 2
    inv_freq = ROPE_THETA ** (-(jnp.arange(half, dtype=jnp.float32) * 2.0 / rot))
    ang = positions.astype(jnp.float32)[:, :, None] * inv_freq
    cos = jnp.cos(ang)[:, :, None, :]
    sin = jnp.sin(ang)[:, :, None, :]
    xf = x.astype(jnp.float32)
    x1 = xf[..., :half]
    x2 = xf[..., half:rot]
    out = jnp.concatenate([x1 * cos - x2 * sin, x2 * cos + x1 * sin, xf[..., rot:]], axis=-1)
    return out.astype(x.dtype)

def masked_softmax(s, mask):
    s = jnp.where(mask, s, NEG_INF)
    m = jnp.max(s, axis=-1, keepdims=True)
    p = jnp.where(mask, jnp.exp(s - m), 0.0)
    return p / jnp.maximum(jnp.sum(p, axis=-1, keepdims=True), TINY)

def _rows(t, start, size):
    return lax.dynamic_slice_in_dim(t, start, size, axis=1)

def _split(x, sizes):
    out = []
    start = 0
    for n in sizes:
        out.append(x[..., start:start + n])
        start += n
    return out

def _sweep_queries(fn, n_blocks):
    out = lax.map(fn, jnp.arange(n_blocks, dtype=jnp.int32))
    out = jnp.moveaxis(out, 0, 1)
    return out.reshape((out.shape[0], -1) + out.shape[3:])

def dsa_attention(q, k, v, q_idx, k_idx, w_idx):
    B, S, H, Dh = q.shape
    k_top = min(DSA_TOPK, S // 4)
    key_pos = jnp.arange(S)
    b_idx = jnp.arange(B)[:, None, None]
    scale = Dh ** -0.5

    def block(c):
        t0 = c * DSA_QBLOCK
        qpos = t0 + jnp.arange(DSA_QBLOCK)
        logits = jnp.einsum('bqhd,bsd->bqhs', _rows(q_idx, t0, DSA_QBLOCK), k_idx).astype(jnp.float32)
        score = jnp.einsum('bqh,bqhs->bqs', _rows(w_idx, t0, DSA_QBLOCK).astype(jnp.float32), jax.nn.relu(logits))
        score = jnp.where(key_pos[None, None, :] <= qpos[None, :, None], score, NEG_INF)
        _, sel = lax.top_k(score, k_top)
        k_sel = k[b_idx, sel]
        v_sel = v[b_idx, sel]
        s = jnp.einsum('bqhd,bqkd->bhqk', _rows(q, t0, DSA_QBLOCK), k_sel).astype(jnp.float32) * scale
        p = masked_softmax(s, (sel <= qpos[None, :, None])[:, None])
        return jnp.einsum('bhqk,bqkd->bqhd', p.astype(v.dtype), v_sel)

    return _sweep_queries(block, S // DSA_QBLOCK)

def moba_attention(q, k, v):
    B, S, H, Dh = q.shape
    n_blk = -(-S // MOBA_BLOCK)
    pad = n_blk * MOBA_BLOCK - S
    k_pad = jnp.pad(k, ((0, 0), (0, pad), (0, 0), (0, 0)))
    v_pad = jnp.pad(v, ((0, 0), (0, pad), (0, 0), (0, 0)))
    k_blk = k_pad.reshape(B, n_blk, MOBA_BLOCK, H, Dh).transpose(0, 3, 1, 2, 4)
    v_blk = v_pad.reshape(B, n_blk, MOBA_BLOCK, H, Dh).transpose(0, 3, 1, 2, 4)
    k_mean = jnp.mean(k_blk.astype(jnp.float32), axis=3)
    n_top = max(1, min(MOBA_TOPK, n_blk - 1))
    n_past = n_top * MOBA_BLOCK
    b_idx = jnp.arange(B)[:, None, None, None]
    h_idx = jnp.arange(H)[None, :, None, None]
    blk_ids = jnp.arange(n_blk)
    scale = Dh ** -0.5

    def block(c):
        t0 = c * MOBA_QBLOCK
        qpos = t0 + jnp.arange(MOBA_QBLOCK)
        own = t0 // MOBA_BLOCK
        qc = _rows(q, t0, MOBA_QBLOCK)
        gate = jnp.einsum('bqhd,bhnd->bhqn', qc.astype(jnp.float32), k_mean)
        gate = jnp.where(blk_ids < own, gate, NEG_INF)
        _, sel = lax.top_k(gate, n_top)
        k_sel = k_blk[b_idx, h_idx, sel]
        v_sel = v_blk[b_idx, h_idx, sel]
        s_past = jnp.einsum('bqhd,bhqnkd->bhqnk', qc, k_sel).astype(jnp.float32)
        m_past = jnp.broadcast_to((sel < own)[..., None], s_past.shape)
        k_own = _rows(k_pad, own * MOBA_BLOCK, MOBA_BLOCK)
        v_own = _rows(v_pad, own * MOBA_BLOCK, MOBA_BLOCK)
        kpos = own * MOBA_BLOCK + jnp.arange(MOBA_BLOCK)
        s_own = jnp.einsum('bqhd,bkhd->bhqk', qc, k_own).astype(jnp.float32)
        m_own = jnp.broadcast_to(kpos[None, :] <= qpos[:, None], s_own.shape)
        s = jnp.concatenate([s_past.reshape(B, H, MOBA_QBLOCK, n_past), s_own], axis=-1) * scale
        m = jnp.concatenate([m_past.reshape(B, H, MOBA_QBLOCK, n_past), m_own], axis=-1)
        p = masked_softmax(s, m).astype(v.dtype)
        p_past = p[..., :n_past].reshape(B, H, MOBA_QBLOCK, n_top, MOBA_BLOCK)
        return (jnp.einsum('bhqnk,bhqnkd->bqhd', p_past, v_sel)
                + jnp.einsum('bhqk,bkhd->bqhd', p[..., n_past:], v_own))

    return _sweep_queries(block, S // MOBA_QBLOCK)

def nsa_compress(x, pos_emb, w1, w2):
    B, S, G, Dh = x.shape
    n_cmp = (S - NSA_CMP_LEN) // NSA_CMP_STRIDE + 1
    idx = jnp.arange(n_cmp)[:, None] * NSA_CMP_STRIDE + jnp.arange(NSA_CMP_LEN)[None, :]
    blk = x[:, idx] + pos_emb[None, None, :, None, :]
    blk = blk.transpose(0, 1, 3, 2, 4).reshape(B, n_cmp, G, NSA_CMP_LEN * Dh)
    return jax.nn.silu(blk @ w1) @ w2

def nsa_attention(q, q_rot, k_cmp, v_cmp, k_sel, v_sel, k_win, v_win, gates):
    B, S, H, Dh = q.shape
    G = k_sel.shape[2]
    HG = H // G
    qg = q.reshape(B, S, G, HG, Dh)
    qr = q_rot.reshape(B, S, G, HG, Dh)
    n_cmp = k_cmp.shape[1]
    cmp_start = jnp.arange(n_cmp) * NSA_CMP_STRIDE
    cmp_end = cmp_start + NSA_CMP_LEN - 1
    n_sel = S // NSA_SEL_LEN
    n_top = min(NSA_SEL_TOPK, n_sel)
    sel_start = jnp.arange(n_sel) * NSA_SEL_LEN
    cover = ((cmp_start[:, None] < sel_start[None, :] + NSA_SEL_LEN)
             & (cmp_start[:, None] + NSA_CMP_LEN > sel_start[None, :])).astype(jnp.float32)
    ks_blk = k_sel.reshape(B, n_sel, NSA_SEL_LEN, G, Dh).transpose(0, 3, 1, 2, 4)
    vs_blk = v_sel.reshape(B, n_sel, NSA_SEL_LEN, G, Dh).transpose(0, 3, 1, 2, 4)
    kw_pad = jnp.pad(k_win, ((0, 0), (NSA_WINDOW, 0), (0, 0), (0, 0)))
    vw_pad = jnp.pad(v_win, ((0, 0), (NSA_WINDOW, 0), (0, 0), (0, 0)))
    b_idx = jnp.arange(B)[:, None, None, None]
    g_idx = jnp.arange(G)[None, :, None, None]
    blk_ids = jnp.arange(n_sel)[None, :]
    scale = Dh ** -0.5
    n_gather = n_top * NSA_SEL_LEN

    def block(c):
        t0 = c * NSA_QBLOCK
        qpos = t0 + jnp.arange(NSA_QBLOCK)
        qp = _rows(qg, t0, NSA_QBLOCK)
        qrc = _rows(qr, t0, NSA_QBLOCK)
        gc = _rows(gates, t0, NSA_QBLOCK)
        s_c = jnp.einsum('bqgjd,bngd->bgjqn', qp, k_cmp).astype(jnp.float32) * scale
        p_c = masked_softmax(s_c, cmp_end[None, :] <= qpos[:, None])
        o_c = jnp.einsum('bgjqn,bngd->bqgjd', p_c.astype(v_cmp.dtype), v_cmp)
        imp = jnp.einsum('bgjqn,ns->bgqs', p_c, cover)
        cur = (qpos // NSA_SEL_LEN)[:, None]
        forced = (blk_ids == 0) | (blk_ids == cur) | (blk_ids == cur - 1)
        imp = jnp.where(forced, NSA_FORCE, imp)
        imp = jnp.where(blk_ids <= cur, imp, NEG_INF)
        _, sel = lax.top_k(imp, n_top)
        kg = ks_blk[b_idx, g_idx, sel].reshape(B, G, NSA_QBLOCK, n_gather, Dh)
        vg = vs_blk[b_idx, g_idx, sel].reshape(B, G, NSA_QBLOCK, n_gather, Dh)
        kpos = (sel[..., None] * NSA_SEL_LEN + jnp.arange(NSA_SEL_LEN)).reshape(B, G, NSA_QBLOCK, n_gather)
        s_s = jnp.einsum('bqgjd,bgqmd->bgjqm', qrc, kg).astype(jnp.float32) * scale
        p_s = masked_softmax(s_s, (kpos <= qpos[None, None, :, None])[:, :, None])
        o_s = jnp.einsum('bgjqm,bgqmd->bqgjd', p_s.astype(vg.dtype), vg)
        kw = _rows(kw_pad, t0, NSA_WINDOW + NSA_QBLOCK)
        vw = _rows(vw_pad, t0, NSA_WINDOW + NSA_QBLOCK)
        wpos = t0 - NSA_WINDOW + jnp.arange(NSA_WINDOW + NSA_QBLOCK)
        dist = qpos[:, None] - wpos[None, :]
        m_w = (dist >= 0) & (dist < NSA_WINDOW) & (wpos[None, :] >= 0)
        s_w = jnp.einsum('bqgjd,bkgd->bgjqk', qrc, kw).astype(jnp.float32) * scale
        p_w = masked_softmax(s_w, m_w)
        o_w = jnp.einsum('bgjqk,bkgd->bqgjd', p_w.astype(vw.dtype), vw)
        o = gc[..., 0:1] * o_c + gc[..., 1:2] * o_s + gc[..., 2:3] * o_w
        return o.reshape(B, NSA_QBLOCK, H, Dh)

    return _sweep_queries(block, S // NSA_QBLOCK)

def dsa_moba_mixer(h, positions, w_in, w_out, a_q_norm, a_k_norm, b_q_norm, b_k_norm):
    B, S, _ = h.shape
    aq, ak, av, iq, ik, iw, bq, bk, bv = _split(h @ w_in, AB_SIZES)
    aq = partial_rope(rms_norm(aq.reshape(B, S, DSA_HEADS, HEAD_DIM), a_q_norm), positions)
    ak = partial_rope(rms_norm(ak.reshape(B, S, 1, HEAD_DIM), a_k_norm), positions)[:, :, 0]
    iq = partial_rope(iq.reshape(B, S, DSA_IDX_HEADS, DSA_IDX_DIM), positions)
    ik = partial_rope(ik.reshape(B, S, 1, DSA_IDX_DIM), positions)[:, :, 0]
    o_a = dsa_attention(aq, ak, av, iq, ik, iw)
    bq = partial_rope(rms_norm(bq.reshape(B, S, MOBA_HEADS, HEAD_DIM), b_q_norm), positions)
    bk = partial_rope(rms_norm(bk.reshape(B, S, MOBA_HEADS, HEAD_DIM), b_k_norm), positions)
    o_b = moba_attention(bq, bk, bv.reshape(B, S, MOBA_HEADS, HEAD_DIM))
    o = jnp.concatenate([o_a.reshape(B, S, -1), o_b.reshape(B, S, -1)], axis=-1)
    return o @ w_out

def nsa_mixer(h, positions, w_in, w_out, q_norm, kcmp_norm, ksel_norm, kwin_norm,
              pos_k, pos_v, w1_k, w2_k, w1_v, w2_v):
    B, S, _ = h.shape
    G = NSA_GROUPS
    HG = NSA_HEADS // NSA_GROUPS
    q, kc, vc, ks, vs, kw, vw, gt = _split(h @ w_in, C_SIZES)
    grp = lambda t: t.reshape(B, S, G, HEAD_DIM)
    q = rms_norm(q.reshape(B, S, NSA_HEADS, HEAD_DIM), q_norm)
    q_rot = partial_rope(q, positions)
    kc = rms_norm(nsa_compress(grp(kc), pos_k, w1_k, w2_k), kcmp_norm)
    vc = nsa_compress(grp(vc), pos_v, w1_v, w2_v)
    ks = partial_rope(rms_norm(grp(ks), ksel_norm), positions)
    kw = partial_rope(rms_norm(grp(kw), kwin_norm), positions)
    gates = jax.nn.sigmoid(gt.astype(jnp.float32)).reshape(B, S, G, HG, 3).astype(h.dtype)
    o = nsa_attention(q, q_rot, kc, vc, ks, grp(vs), kw, grp(vw), gates)
    return o.reshape(B, S, C_MIX_WIDTH) @ w_out

def memory_cross_attention(h, m, w_q, w_kv, w_o, q_norm, k_norm):
    B, S, _ = h.shape
    M = m.shape[1]
    q = rms_norm((h @ w_q).reshape(B, S, MEM_HEADS, MEM_HEAD_DIM), q_norm)
    k, v = _split(m @ w_kv, (MEM_HEADS * MEM_HEAD_DIM, MEM_HEADS * MEM_HEAD_DIM))
    k = rms_norm(k.reshape(B, M, MEM_HEADS, MEM_HEAD_DIM), k_norm)
    v = v.reshape(B, M, MEM_HEADS, MEM_HEAD_DIM)
    s = jnp.einsum('bshd,bmhd->bhsm', q, k).astype(jnp.float32) * (MEM_HEAD_DIM ** -0.5)
    p = jax.nn.softmax(s, axis=-1).astype(v.dtype)
    o = jnp.einsum('bhsm,bmhd->bshd', p, v).reshape(B, S, MEM_HEADS * MEM_HEAD_DIM)
    return o @ w_o

def swiglu(h, w_in, w_out):
    g, u = _split(h @ w_in, (D_FF, D_FF))
    return (jax.nn.silu(g) * u) @ w_out

def first_inputs(seed: int = 0) -> dict:
    key = jax.random.key(seed)
    keys = jax.random.split(key, 48)
    ctr = [0]

    def nxt():
        k = keys[ctr[0]]
        ctr[0] += 1
        return k

    def nrm(shape, scale):
        return scale * jax.random.normal(nxt(), shape, jnp.float32)

    def gain(shape):
        return 1.0 + 0.02 * jax.random.normal(nxt(), shape, jnp.float32)

    n_even = (DEPTH + 1) // 2
    n_odd = DEPTH // 2
    d = D_MODEL
    x = nrm((BATCH, SEQ, d), 1.0)
    mem = nrm((BATCH, N_MEM, d), 1.0)
    offset = jax.random.randint(nxt(), (BATCH, 1), 0, SEQ)
    positions = (offset + jnp.arange(SEQ)[None, :]).astype(jnp.int32)
    cmp_in = NSA_CMP_LEN * HEAD_DIM
    return {
        'x': x,
        'mem': mem,
        'positions': positions,
        'norm_mix': gain((DEPTH, d)),
        'norm_mem': gain((DEPTH, d)),
        'norm_mem_src': gain((DEPTH, d)),
        'norm_ffn': gain((DEPTH, d)),
        'ab_w_in': nrm((n_even, d, AB_WIDTH), d ** -0.5),
        'ab_w_out': nrm((n_even, AB_MIX_WIDTH, d), AB_MIX_WIDTH ** -0.5),
        'dsa_q_norm': gain((n_even, HEAD_DIM)),
        'dsa_k_norm': gain((n_even, HEAD_DIM)),
        'moba_q_norm': gain((n_even, HEAD_DIM)),
        'moba_k_norm': gain((n_even, HEAD_DIM)),
        'nsa_w_in': nrm((n_odd, d, C_WIDTH), d ** -0.5),
        'nsa_w_out': nrm((n_odd, C_MIX_WIDTH, d), C_MIX_WIDTH ** -0.5),
        'nsa_q_norm': gain((n_odd, HEAD_DIM)),
        'nsa_kcmp_norm': gain((n_odd, HEAD_DIM)),
        'nsa_ksel_norm': gain((n_odd, HEAD_DIM)),
        'nsa_kwin_norm': gain((n_odd, HEAD_DIM)),
        'nsa_cmp_pos_k': nrm((n_odd, NSA_CMP_LEN, HEAD_DIM), 0.1),
        'nsa_cmp_pos_v': nrm((n_odd, NSA_CMP_LEN, HEAD_DIM), 0.1),
        'nsa_cmp_w1_k': nrm((n_odd, cmp_in, HEAD_DIM), cmp_in ** -0.5),
        'nsa_cmp_w2_k': nrm((n_odd, HEAD_DIM, HEAD_DIM), HEAD_DIM ** -0.5),
        'nsa_cmp_w1_v': nrm((n_odd, cmp_in, HEAD_DIM), cmp_in ** -0.5),
        'nsa_cmp_w2_v': nrm((n_odd, HEAD_DIM, HEAD_DIM), HEAD_DIM ** -0.5),
        'mem_w_q': nrm((DEPTH, d, MEM_HEADS * MEM_HEAD_DIM), d ** -0.5),
        'mem_w_kv': nrm((DEPTH, d, 2 * MEM_HEADS * MEM_HEAD_DIM), d ** -0.5),
        'mem_w_o': nrm((DEPTH, MEM_HEADS * MEM_HEAD_DIM, d), (MEM_HEADS * MEM_HEAD_DIM) ** -0.5),
        'mem_q_norm': gain((DEPTH, MEM_HEAD_DIM)),
        'mem_k_norm': gain((DEPTH, MEM_HEAD_DIM)),
        'ffn_w_in': nrm((DEPTH, d, 2 * D_FF), d ** -0.5),
        'ffn_w_out': nrm((DEPTH, D_FF, d), D_FF ** -0.5),
    }

def first_block(x, mem, positions, norm_mix, norm_mem, norm_mem_src, norm_ffn,
              ab_w_in, ab_w_out, dsa_q_norm, dsa_k_norm, moba_q_norm, moba_k_norm,
              nsa_w_in, nsa_w_out, nsa_q_norm, nsa_kcmp_norm, nsa_ksel_norm, nsa_kwin_norm,
              nsa_cmp_pos_k, nsa_cmp_pos_v, nsa_cmp_w1_k, nsa_cmp_w2_k, nsa_cmp_w1_v, nsa_cmp_w2_v,
              mem_w_q, mem_w_kv, mem_w_o, mem_q_norm, mem_k_norm, ffn_w_in, ffn_w_out):
    for i in range(DEPTH):
        j = i // 2
        h = rms_norm(x, norm_mix[i])
        if i % 2 == 0:
            x = x + dsa_moba_mixer(h, positions, ab_w_in[j], ab_w_out[j], dsa_q_norm[j], dsa_k_norm[j],
                                   moba_q_norm[j], moba_k_norm[j])
        else:
            x = x + nsa_mixer(h, positions, nsa_w_in[j], nsa_w_out[j], nsa_q_norm[j], nsa_kcmp_norm[j],
                              nsa_ksel_norm[j], nsa_kwin_norm[j], nsa_cmp_pos_k[j], nsa_cmp_pos_v[j],
                              nsa_cmp_w1_k[j], nsa_cmp_w2_k[j], nsa_cmp_w1_v[j], nsa_cmp_w2_v[j])
        x = x + memory_cross_attention(rms_norm(x, norm_mem[i]), rms_norm(mem, norm_mem_src[i]),
                                       mem_w_q[i], mem_w_kv[i], mem_w_o[i], mem_q_norm[i], mem_k_norm[i])
        x = x + swiglu(rms_norm(x, norm_ffn[i]), ffn_w_in[i], ffn_w_out[i])
    return x


DEPTH_2 = 1

POOL_WIDTH = D_MODEL // 2
POOL_GROUPS = 4
POOL_GROUP_DIM = POOL_WIDTH // POOL_GROUPS
POOL_WINDOWS = (2, 4, 8, 16)
LRU_WIDTH = D_MODEL
LRU_HEADS = 16
LRU_HEAD_DIM = LRU_WIDTH // LRU_HEADS
CONV_WIDTH = 4
RG_C = 8.0
IN_COLS = POOL_WIDTH + 2 * LRU_WIDTH + 2 * D_MODEL
N_GROUPS = 4
EXP_PER_GROUP = 4
N_EXP = N_GROUPS * EXP_PER_GROUP
TOP_K = 2
D_EXPERT = D_MODEL // 2
EPS = 1e-6


def rms_norm_2(x, g):
    xf = x.astype(jnp.float32)
    y = xf * lax.rsqrt(jnp.mean(xf * xf, axis=-1, keepdims=True) + EPS)
    return (y * g.astype(jnp.float32)).astype(x.dtype)

def pooling_mixer(u, pool_w, pool_scale):
    b_, s_, _ = u.shape
    ug = u.astype(jnp.float32).reshape(b_, s_, POOL_GROUPS, POOL_GROUP_DIM)
    c = jnp.cumsum(ug, axis=1)
    pos = jnp.arange(1, s_ + 1, dtype=jnp.float32)
    pooled = []
    for g, w in enumerate(POOL_WINDOWS):
        cg = c[:, :, g]
        prev = jnp.pad(cg[:, :s_ - w], ((0, 0), (w, 0), (0, 0)))
        cnt = jnp.minimum(pos, float(w))
        pooled.append((cg - prev) / cnt[None, :, None])
    z = (jnp.stack(pooled, axis=2) - ug).astype(u.dtype)
    y = jnp.einsum('bsgc,gcd->bsgd', z, pool_w).reshape(b_, s_, POOL_WIDTH)
    return y * pool_scale

def rglru_mixer(u, gate_in, conv_w, conv_b, w_r, b_r, w_i, b_i, lam):
    b_, s_, c_ = u.shape
    xc = lax.conv_general_dilated(
        u, conv_w[:, None, :], window_strides=(1,), padding=[(CONV_WIDTH - 1, 0)],
        dimension_numbers=('NWC', 'WIO', 'NWC'), feature_group_count=c_) + conv_b
    xh = xc.reshape(b_, s_, LRU_HEADS, LRU_HEAD_DIM)
    r = jax.nn.sigmoid(jnp.einsum('bshc,hcd->bshd', xh, w_r).reshape(b_, s_, c_) + b_r)
    i = jax.nn.sigmoid(jnp.einsum('bshc,hcd->bshd', xh, w_i).reshape(b_, s_, c_) + b_i)
    log_a = -RG_C * r.astype(jnp.float32) * jax.nn.softplus(-lam.astype(jnp.float32))
    a = jnp.exp(log_a)
    mult = jnp.sqrt(-jnp.expm1(2.0 * log_a))
    bt = mult * (i * xc).astype(jnp.float32)

    def combine(lhs, rhs):
        a1, b1 = lhs
        a2, b2 = rhs
        return a1 * a2, a2 * b1 + b2

    _, h = lax.associative_scan(combine, (a, bt), axis=1)
    return h.astype(u.dtype) * jax.nn.gelu(gate_in)

def hier_moe(h, rg_w, rg_b, re_w, re_b, e_gate, e_up, e_down):
    b_, s_, d_ = h.shape
    xt = h.reshape(b_ * s_, d_)
    g_logits = (xt @ rg_w + rg_b).astype(jnp.float32)
    g_prob = jax.nn.softmax(g_logits, axis=-1)
    p_top, g_idx = lax.top_k(g_prob, 1)
    e_logits = (xt @ re_w + re_b).astype(jnp.float32).reshape(-1, N_GROUPS, EXP_PER_GROUP)
    sel = jnp.take_along_axis(e_logits, g_idx[:, :, None], axis=1)[:, 0]
    v, e_idx = lax.top_k(sel, TOP_K)
    w2 = jax.nn.softmax(v, axis=-1) * p_top
    ids = g_idx * EXP_PER_GROUP + e_idx
    comb = jnp.einsum('tk,tke->te', w2, jax.nn.one_hot(ids, N_EXP, dtype=jnp.float32)).astype(h.dtype)
    y = jnp.zeros_like(xt)
    for e in range(N_EXP):
        he = jax.nn.silu(xt @ e_gate[e]) * (xt @ e_up[e])
        y = y + comb[:, e:e + 1] * (he @ e_down[e])
    return y.reshape(b_, s_, d_)

def second_inputs(seed: int = 0) -> dict:
    key = jax.random.key(seed)
    ks = jax.random.split(key, 24)
    f32 = jnp.float32
    L = DEPTH_2

    def nrm(k, shape, scale):
        return jax.random.normal(k, shape, f32) * scale

    u = jax.random.uniform(ks[10], (L, LRU_WIDTH), f32, 0.9, 0.999)
    s = u ** (1.0 / RG_C)
    lam = jnp.log(s) - jnp.log1p(-s)
    return {
        'x': nrm(ks[0], (BATCH, SEQ, D_MODEL), 1.0),
        'norm1_g': 1.0 + nrm(ks[1], (L, D_MODEL), 0.02),
        'w_in': nrm(ks[2], (L, D_MODEL, IN_COLS), D_MODEL ** -0.5),
        'pool_w': nrm(ks[3], (L, POOL_GROUPS, POOL_GROUP_DIM, POOL_GROUP_DIM), POOL_GROUP_DIM ** -0.5),
        'pool_scale': 1.0 + nrm(ks[4], (L, POOL_WIDTH), 0.02),
        'conv_w': nrm(ks[5], (L, CONV_WIDTH, LRU_WIDTH), CONV_WIDTH ** -0.5),
        'conv_b': nrm(ks[6], (L, LRU_WIDTH), 0.01),
        'rg_w_r': nrm(ks[7], (L, LRU_HEADS, LRU_HEAD_DIM, LRU_HEAD_DIM), LRU_HEAD_DIM ** -0.5),
        'rg_b_r': nrm(ks[8], (L, LRU_WIDTH), 0.01),
        'rg_w_i': nrm(ks[9], (L, LRU_HEADS, LRU_HEAD_DIM, LRU_HEAD_DIM), LRU_HEAD_DIM ** -0.5),
        'rg_b_i': nrm(ks[11], (L, LRU_WIDTH), 0.01),
        'rg_lambda': lam,
        'proj_a': nrm(ks[12], (L, POOL_WIDTH, D_MODEL), POOL_WIDTH ** -0.5),
        'proj_b': nrm(ks[13], (L, LRU_WIDTH, D_MODEL), LRU_WIDTH ** -0.5),
        'w_out': nrm(ks[14], (L, D_MODEL, D_MODEL), D_MODEL ** -0.5),
        'norm2_g': 1.0 + nrm(ks[15], (L, D_MODEL), 0.02),
        'router_group_w': nrm(ks[16], (L, D_MODEL, N_GROUPS), D_MODEL ** -0.5),
        'router_group_b': nrm(ks[17], (L, N_GROUPS), 0.01),
        'router_expert_w': nrm(ks[18], (L, D_MODEL, N_EXP), D_MODEL ** -0.5),
        'router_expert_b': nrm(ks[19], (L, N_EXP), 0.01),
        'exp_w_gate': nrm(ks[20], (L, N_EXP, D_MODEL, D_EXPERT), D_MODEL ** -0.5),
        'exp_w_up': nrm(ks[21], (L, N_EXP, D_MODEL, D_EXPERT), D_MODEL ** -0.5),
        'exp_w_down': nrm(ks[22], (L, N_EXP, D_EXPERT, D_MODEL), D_EXPERT ** -0.5),
        'norm_f_g': 1.0 + nrm(ks[23], (D_MODEL,), 0.02),
    }

def second_block(x, norm1_g, w_in, pool_w, pool_scale, conv_w, conv_b, rg_w_r, rg_b_r, rg_w_i, rg_b_i,
              rg_lambda, proj_a, proj_b, w_out, norm2_g, router_group_w, router_group_b,
              router_expert_w, router_expert_b, exp_w_gate, exp_w_up, exp_w_down, norm_f_g):
    o1 = POOL_WIDTH
    o2 = o1 + LRU_WIDTH
    o3 = o2 + LRU_WIDTH
    o4 = o3 + D_MODEL
    for l in range(DEPTH_2):
        h = rms_norm_2(x, norm1_g[l])
        z = h @ w_in[l]
        u_pool, u_lru, u_gate = z[..., :o1], z[..., o1:o2], z[..., o2:o3]
        g_a = jax.nn.sigmoid(z[..., o3:o4])
        g_b = jax.nn.sigmoid(z[..., o4:])
        y_a = pooling_mixer(u_pool, pool_w[l], pool_scale[l]) @ proj_a[l]
        y_b = rglru_mixer(u_lru, u_gate, conv_w[l], conv_b[l], rg_w_r[l], rg_b_r[l],
                          rg_w_i[l], rg_b_i[l], rg_lambda[l]) @ proj_b[l]
        x = x + (g_a * y_a + g_b * y_b) @ w_out[l]
        h2 = rms_norm_2(x, norm2_g[l])
        x = x + hier_moe(h2, router_group_w[l], router_group_b[l], router_expert_w[l],
                         router_expert_b[l], exp_w_gate[l], exp_w_up[l], exp_w_down[l])
    return rms_norm_2(x, norm_f_g)


def setup_inputs(seed=0):
    out = dict(first_inputs(seed))
    for name, value in second_inputs(seed + 1).items():
        if name != "x":
            out[name + "_2"] = value
    return out


def reference(
    x, mem, positions, norm_mix, norm_mem, norm_mem_src, norm_ffn, ab_w_in, ab_w_out,
    dsa_q_norm, dsa_k_norm, moba_q_norm, moba_k_norm, nsa_w_in, nsa_w_out, nsa_q_norm,
    nsa_kcmp_norm, nsa_ksel_norm, nsa_kwin_norm, nsa_cmp_pos_k, nsa_cmp_pos_v, nsa_cmp_w1_k,
    nsa_cmp_w2_k, nsa_cmp_w1_v, nsa_cmp_w2_v, mem_w_q, mem_w_kv, mem_w_o, mem_q_norm,
    mem_k_norm, ffn_w_in, ffn_w_out, norm1_g_2, w_in_2, pool_w_2, pool_scale_2, conv_w_2,
    conv_b_2, rg_w_r_2, rg_b_r_2, rg_w_i_2, rg_b_i_2, rg_lambda_2, proj_a_2, proj_b_2, w_out_2,
    norm2_g_2, router_group_w_2, router_group_b_2, router_expert_w_2, router_expert_b_2,
    exp_w_gate_2, exp_w_up_2, exp_w_down_2, norm_f_g_2,
):
    x = first_block(
        x, mem, positions, norm_mix, norm_mem, norm_mem_src, norm_ffn, ab_w_in, ab_w_out,
        dsa_q_norm, dsa_k_norm, moba_q_norm, moba_k_norm, nsa_w_in, nsa_w_out, nsa_q_norm,
        nsa_kcmp_norm, nsa_ksel_norm, nsa_kwin_norm, nsa_cmp_pos_k, nsa_cmp_pos_v, nsa_cmp_w1_k,
        nsa_cmp_w2_k, nsa_cmp_w1_v, nsa_cmp_w2_v, mem_w_q, mem_w_kv, mem_w_o, mem_q_norm,
        mem_k_norm, ffn_w_in, ffn_w_out,
    )
    return second_block(
        x, norm1_g_2, w_in_2, pool_w_2, pool_scale_2, conv_w_2, conv_b_2, rg_w_r_2, rg_b_r_2,
        rg_w_i_2, rg_b_i_2, rg_lambda_2, proj_a_2, proj_b_2, w_out_2, norm2_g_2,
        router_group_w_2, router_group_b_2, router_expert_w_2, router_expert_b_2, exp_w_gate_2,
        exp_w_up_2, exp_w_down_2, norm_f_g_2,
    )


_drawn_inputs = setup_inputs


def setup_inputs(seed=0):
    import zlib

    import numpy as np

    out = dict(_drawn_inputs(seed))
    spreads = {}
    factors = {'norm_mem': 8.0,
     'norm_mem_src': 8.0,
     'dsa_q_norm': 8.0,
     'dsa_k_norm': 8.0,
     'moba_q_norm': 8.0,
     'moba_k_norm': 6.549,
     'nsa_q_norm': 8.0,
     'nsa_kcmp_norm': 8.0,
     'nsa_ksel_norm': 8.0,
     'nsa_kwin_norm': 8.0,
     'nsa_cmp_pos_k': 8.0,
     'mem_q_norm': 8.0,
     'mem_k_norm': 8.0,
     'norm1_g_2': 3.481,
     'pool_scale_2': 8.0,
     'conv_b_2': 14.545,
     'rg_b_r_2': 44.74,
     'rg_b_i_2': 64.0,
     'norm2_g_2': 12.571,
     'router_group_b_2': 28.091,
     'router_expert_b_2': 44.747,
     'norm_f_g_2': 8.164}
    for name, (base, spread) in spreads.items():
        noise = np.random.default_rng([zlib.crc32(name.encode()), seed]).standard_normal(out[name].shape)
        drawn = base * np.exp(spread * noise) if base else spread * noise
        out[name] = jnp.asarray(drawn.astype(out[name].dtype))
    for name, factor in factors.items():
        out[name] = (out[name] * factor).astype(out[name].dtype)
    return out
```

```python
from contextlib import ExitStack
import math
import numpy as np
import concourse.bass as bass
from concourse import mybir

F32 = mybir.dt.float32
F32R = mybir.dt.float32r
I32 = mybir.dt.int32
ALU = mybir.AluOpType
ACT = mybir.ActivationFunctionType
AX = mybir.AxisListType.X

P = 128
T = 256
C = T // P
D = 1024
KC = D // P
DH = 64
FF = 2816
FB = 256
RING = 3
UNIT = 2048
LO_DVE = 768
EPS = 1e-6
NEG = -1e30
TAKEN = -3e38
TINY = 1e-20
ROPE_THETA = 500000.0
HALF = 8
N_CMP = 15
CMP_LEN, CMP_STRIDE = 32, 16
N_EXP, N_GRP, PER_GRP = 16, 4, 4
TOPK = 64
POOL_WINDOWS = (2, 4, 8, 16)

AQ, AK, AV, IQ, IK, IW, BQ, BK, BV, AB_W = 0, 512, 576, 640, 896, 928, 936, 1448, 1960, 2472
NQ, KCMP, VCMP, KSEL, VSEL, KWIN, VWIN, GT, C_W = 0, 1024, 1280, 1536, 1792, 2048, 2304, 2560, 2608
UL, UP, UG, GA, GB, IN_W = 512, 0, 1536, 2560, 3584, 4608

G_MIX, G_MEM, G_SRC, G_FFN, G_N1, G_N2 = (0, 1), (2, 3), (4, 5), (6, 7), 8, 9
R_CONV, R_CB, R_BR, R_BI, R_LAM, R_PS = 0, 32, 40, 48, 56, 64
N_AQ, N_AK, N_BQ, N_BK, N_NQ, N_KC, N_KS, N_KW = range(8)


class Chain:

    def __init__(self, eng, sem):
        self.eng, self.sem, self.n, self.turn = eng, sem, 0, 0

    def __call__(self, ins):
        self.n += 1
        ins.then_inc(self.sem, 1)
        self.eng.wait_ge(self.sem, self.n + self.turn)


class Slab:

    def __init__(self, w, c0, width, k, evac, unit, index, done_act, done_dve):
        self.w, self.c0, self.width, self.k, self.evac = w, c0, width, k, evac
        self.unit, self.units, self.index = unit, -(-k // 4), index
        self.end = unit + self.units
        self.done_act, self.done_dve = done_act, done_dve


class Plan:

    def __init__(self):
        self.slabs, self.loads, self.width, self.dmas = [], [], [], []
        self.act = self.dve = 0
        self.turns, self.turn_act, self.turn_dve = 0, [0], [0]
        self.items = self.outs = 0

    def product(self, w, width, k=KC, evac="both", first=0):
        out = []
        for c0 in range(first, first + width, 512):
            n = min(512, first + width - c0)
            self.act += evac == "both"
            self.dve += 1 if evac == "both" else 2
            s = Slab(w, c0, n, k, evac, len(self.width), len(self.slabs), self.act, self.dve)
            self.slabs.append(s)
            self.loads.append(s)
            self.width += [min(4, k) * n] * s.units
            self.dmas += [1] * s.units
            out.append(s)
        return out

    def blocks(self, n, per, dmas, load):
        b = Blocks(n, per, len(self.width), load, dmas)
        self.loads.append(b)
        self.width += [UNIT] * (3 * n)
        self.dmas += [dmas, dmas] + [dmas, dmas, 1] * (n - 1) + [1]
        return b

    def turn(self, n, act, dve):
        base = self.turns
        for _ in range(n):
            self.turn_act.append(self.turn_act[-1] + act)
            self.turn_dve.append(self.turn_dve[-1] + dve)
        self.turns += n
        return base

    def item(self, n):
        self.items += n
        return self.items - n

    def attention(self, n):
        self.outs += n
        return self.item(n), self.outs - n, self.turn(n, 0, 1)

    def landed(self, u):
        return 16 * sum(self.dmas[v] for v in range(u % RING, u + 1, RING))


class Blocks:

    def __init__(self, n, per, base, load, dmas):
        self.n, self.per, self.base, self.load, self.dmas = n, per, base, load, dmas
        self.first, self.last = 2, n - per if (n - 2) % per == 0 and per > 1 else n - 1


class Item:

    def __init__(self, q, k, nk, bias, scale, v, dv, out, weight=None, add=False):
        self.q, self.k, self.nk, self.bias, self.scale, self.v, self.dv, self.out = q, k, nk, bias, scale, v, dv, out
        self.weight, self.add = weight, add


def build(nc, a, out):
    ctx = ExitStack()
    with ctx:
        def sb(name, shape, dt=F32):
            return ctx.enter_context(nc.sbuf_tensor("t_" + name, shape, dt))

        def sem(name):
            return ctx.enter_context(nc.semaphore(name))

        flags = {}

        def flag(name):
            if name not in flags:
                flags[name] = sem(name)
            return flags[name]

        raw = [sb(f"raw{i}", [P, UNIT]) for i in range(RING)]
        whi = [sb(f"whi{i}", [P, UNIT], F32R) for i in range(RING)]
        wlo = [sb(f"wlo{i}", [P, UNIT], F32R) for i in range(RING)]
        x = sb("x", [P, C, D])
        ahi, alo = sb("ahi", [P, KC, T], F32R), sb("alo", [P, KC, T], F32R)
        bhi, blo = sb("bhi", [P, KC, T], F32R), sb("blo", [P, KC, T], F32R)
        z = sb("z", [P, 9216])
        feat = sb("feat", [P, 5120])
        memo = sb("memo", [P, 4096])
        rows = feat[0:80, 2560:2816].rearrange("r (a n) -> r a n", a=2)
        mem_k_gain = z[:, 8656:8912].rearrange("p (l n) -> p l n", l=2)
        final_gain = feat[:, 0:D]
        cols = sb("cols", [P, 2, 80])
        ident = sb("ident", [P, P])
        causal = sb("causal", [P, C, T])
        zero = sb("zero", [P, T])
        cmp_bias, cmp_keep = sb("cmp_bias", [P, C, 32]), sb("cmp_keep", [P, C, 32])
        shared = sb("shared", [P, 2600])
        dsa_bias = shared[:, 0:512].rearrange("p (c t) -> p c t", c=C)
        masked = [shared[:, 512 + T * i:512 + T * (i + 1)] for i in range(2)]
        prob = [shared[:, 1024 + T * i:1024 + T * (i + 1)] for i in range(3)]
        probt = [shared[:, 1792 + T * i:1792 + T * (i + 1)] for i in range(2)]
        best8 = shared[:, 2336:2344]
        item_max, item_neg, item_sum, item_inv = (sb(n, [P, 64]) for n in ("item_max", "item_neg", "item_sum", "item_inv"))
        s_mean, s_y, s_t, s_u = (sb(n, [P, 64]) for n in ("s_mean", "s_y", "s_t", "s_u"))
        s_bits = sb("s_bits", [P, 64], I32)
        cosine, sine = sb("cosine", [P, C, HALF]), sb("sine", [P, C, HALF])
        pos_i, pos_r, pos_f = sb("pos_i", [C, P], I32), sb("pos_r", [C, P]), sb("pos_f", [P, C])
        angle = sb("angle", [P, 4, C, HALF])
        gains = sb("gains", [P, 8, DH])
        mem_q_gain = sb("mem_q_gain", [P, 2, P])
        silu = shared[:, 0:1024].rearrange("p (c a f) -> p c a f", c=C, a=2)
        route_w = shared[:, 1024:1184].rearrange("p (k n) -> p k n", k=KC)
        rt = shared[:, 1184:1568].rearrange("p (a c n) -> p a c n", a=12, c=C)
        half_comb = shared[:, 1568:1632].rearrange("p (c n) -> p c n", c=C)
        route_b = shared[:, 1632:1652]
        rhi, rlo = sb("rhi", [P, KC, 20], F32R), sb("rlo", [P, KC, 20], F32R)
        w2 = shared[0:DH, 2344:2472].rearrange("p (a e) -> p a e", a=2)
        pos_rows = shared[0:CMP_LEN, 2472:2600]
        numbers, half, sumsq = sb("numbers", [P, 16]), sb("half", [P, 1]), sb("sumsq", [P, 2])

        psum = [ctx.enter_context(nc.psum_tensor(f"bank{i}", [P, 512], F32)) for i in range(8)]
        G, TB, SCB = psum[0:4], psum[4:6], psum[6:8]
        memk = [memo[:, 2048 * i:2048 * i + 1024].rearrange("p (h t) -> p h t", h=4) for i in range(2)]
        memk_rows = [memo[:, 2048 * i:2048 * i + 1024].rearrange("p (c n) -> p c n", c=C) for i in range(2)]
        memv = [memo[:, 2048 * i + 1024:2048 * i + 2048].rearrange("p (c n) -> p c n", c=C) for i in range(2)]

        def zv(off, width):
            return z[:, off:off + C * width].rearrange("p (c n) -> p c n", c=C)

        def heads(view, first, n, d):
            return view[:, :, first:first + n * d].rearrange("p c (h d) -> p c h d", d=d)

        raw_loaded = [sem(f"raw_loaded{i}") for i in range(RING)]
        hi_done, lo_dve, lo_pool, unit_used = (sem(n) for n in ("hi_done", "lo_dve_done", "lo_pool_done", "unit_used"))
        slab_act, slab_dve = sem("slab_emptied_act"), sem("slab_emptied_dve")
        turned, turn_act, turn_dve = sem("turned"), sem("turn_emptied_act"), sem("turn_emptied_dve")
        scored, item_masked, exped = sem("scored"), sem("item_masked"), sem("exped")
        pved, item_out = sem("pved"), sem("item_out")
        dve_step, act_step, pool_step = sem("dve_step"), sem("act_step"), sem("pool_step")
        ff_tanh, ff_silu, ff_turned, ff_hi, ff_lo = (sem(n) for n in ("ff_tanh", "ff_silu", "ff_turned", "ff_hi", "ff_lo"))

        plan = Plan()
        L = [{}, {}]
        M = [{}, {}]
        for l in range(2):
            s = L[l]
            s["hturn"] = plan.turn(4, 1, 1)
            s["in"] = plan.product(a["ab_w_in"][0], AB_W) if l == 0 else plan.product(a["nsa_w_in"][0], C_W)
            if l == 0:
                mem_turn = plan.turn(4, 1, 1)
                s["qturn"] = plan.turn(8, 0, 1)
                s["index"] = plan.item(16)
                for m in range(2):
                    M[m]["kv"] = plan.product(a["mem_w_kv"][m], 1024)
                s["heads"] = plan.attention(32)
            else:
                s["qturn"] = plan.turn(4, 0, 1)
                s["qrturn"] = plan.turn(8, 0, 1)
                s["posturn"] = plan.turn(1, 0, 1)
                s["kcturn"] = plan.turn(1, 0, 1)
                s["cmpturn"] = plan.turn(2, 0, 1)
                s["heads"] = plan.attention(64)
            s["oturn"] = plan.turn(4, 1, 1)
            s["out"] = plan.product(a["ab_w_out" if l == 0 else "nsa_w_out"][0], D, evac="dve")
            s["mturn"] = plan.turn(4, 1, 1)
            s["mq"] = plan.product(a["mem_w_q"][l], 512)
            if l == 0:
                for m in range(2):
                    M[m]["kturn"] = plan.turn(2, 1, 0)
            s["mqturn"] = plan.turn(2, 0, 1)
            s["mheads"] = plan.attention(8)
            s["moturn"] = plan.turn(2, 1, 1)
            s["mo"] = plan.product(a["mem_w_o"][l], D, k=4, evac="dve")
            s["fturn"] = plan.turn(4, 1, 1)
            s["ff"] = plan.blocks(FF // FB, 1, 2, ("ffn", l))
            s["ff"].start = sum(b["ff"].n for b in L[:l])
        N = {}
        N["hturn"] = plan.turn(4, 1, 1)
        N["in"] = plan.product(a["w_in_2"][0], 1536) + plan.product(a["w_in_2"][0], 1024, first=UG)
        N["gates"] = plan.product(a["w_in_2"][0], 2048, first=GA)
        N["uturn"] = plan.turn(10, 0, 1)
        N["gturn"] = plan.turn(8, 1, 0)
        N["yturn"] = plan.turn(2, 1, 1)
        N["pa"] = plan.product(a["proj_a_2"][0], D, k=4, evac="dve")
        N["pb"] = plan.product(a["proj_b_2"][0], D, evac="dve")
        N["oturn"] = plan.turn(4, 1, 1)
        N["out"] = plan.product(a["w_out_2"][0], D, evac="dve")
        N["h2turn"] = plan.turn(4, 1, 1)
        N["moe"] = plan.blocks(N_EXP * 2, 2, 2, ("moe", 0))
        N["moe"].start = 2 * (FF // FB)
        n_units = len(plan.width)

        XN = zv(0, D)
        SQA, SQQ, SQK = (z[:, a_:a_ + C * n * DH].rearrange("p (c h d) -> p c h d", c=C, d=DH)
                         for a_, n in ((4944, 9), (6096, 8), (7120, 8)))
        ROPET = feat[:, 4096:4672]
        COPIES = z[:, 8144:8656].rearrange("p (c n) -> p c n", c=C)
        MEMIN = feat[:, 0:2 * D].rearrange("p (c n) -> p c n", c=C)
        Z0, Z1, ZM = zv(0, AB_W), zv(0, C_W), zv(0, 512)
        KWT = z[:, 5216:5728]
        KCVT = z[:, 5728:6752].rearrange("p (g t) -> p g t", g=4)
        HIV = z[0:DH, 6752:7264].rearrange("p (g j n) -> p g j n", g=4, j=4)
        VBLK = z[:, 7264:8288].rearrange("p (g j d) -> p g j d", g=4, j=4)
        CMPW = memo[:, 0:2048].rearrange("p (j e) -> p j e", e=DH)
        POST = z[:, 8288:8320]
        HID = z[0:DH, 8320:8576].rearrange("p (a g n) -> p a g n", a=2, g=4)
        HIT = z[0:DH, 8576:8832].rearrange("p (a g n) -> p a g n", a=2, g=4)
        KCN = z[:, 8832:8960].rearrange("p (a d) -> p a d", a=2)
        KCT = z[:, 8960:9088]
        GATE = z[:, 9088:9184].rearrange("p (c n) -> p c n", c=C)
        CS, CP = shared[:, 512:1024], shared[:, 1024:1536]
        CPT = shared[:, 1536:2048]
        U = feat[:, :].rearrange("p (k t) -> p k t", t=T)
        ULT, UPT, UGT = U[:, 0:8, :], U[:, 8:12, :], U[:, 12:20, :]
        ZA = z[:, 0:5120].rearrange("p (c n) -> p c n", c=C)
        ZG = z[:, 5120:9216].rearrange("p (c n) -> p c n", c=C)
        XC = z[:, 0:2048].rearrange("p (k t) -> p k t", t=T)
        RG = z[:, 2048:4096].rearrange("p (k t) -> p k t", t=T)
        POOLT = z[:, 4096:5120].rearrange("p (k t) -> p k t", t=T)
        IG = memo[:, 0:2048].rearrange("p (k t) -> p k t", t=T)
        GATEW = memo[:, 2048:4096].rearrange("p (a k n) -> p a k n", a=2, k=8)
        POOLW = shared[:, 1664:2176].rearrange("p (g n) -> p g n", g=4)
        SP4 = shared[:, 2176:2192]
        LAM = shared[:, 2192:2256].rearrange("p (a k) -> p a k", a=8)
        HB = shared[:, 2256:2272].rearrange("p (a k) -> p a k", a=2)
        FHI, FLO = bhi[:, 0:2, :], blo[:, 0:2, :]

        def bank_of(s, c):
            return G[2 * (s.index % 2) + c][:, 0:s.width]

        def gain_of(g):
            return lambda k: cols[:, 0, 8 * g + k:8 * g + k + 1]

        def pair(view, first):
            return lambda c: view[:, c, first:first + P]

        def place1(h):
            return 4 * (h // 8) + h % 4, h // 4 % 2

        def z1_dst(s, c):
            v = Z1[:, c, s.c0:s.c0 + s.width]
            if s.c0 < KCMP:
                return v.rearrange("p (i g d) -> p g i d", g=2, d=DH)
            if s.c0 == KCMP:
                return v.rearrange("p (g a d) -> p a g d", a=2, d=DH)
            return v

        def z1_src(s, c):
            v = bank_of(s, c)
            if s.c0 < KCMP:
                return v.rearrange("p (g i d) -> p g i d", g=2, d=DH)
            if s.c0 == KCMP:
                return v.rearrange("p (a g d) -> p a g d", a=2, d=DH)
            return v

        JOBS0 = ([pair(Z0, IQ), pair(Z0, IQ + P), pair(COPIES, 0), pair(COPIES, P)]
                 + [pair(Z0, AQ + P * i) for i in range(4)] + [pair(Z0, BQ + P * i) for i in range(4)]
                 + [pair(Z0, BK + P * i) for i in range(4)])
        JOBSQ = [pair(Z1, NQ + P * i) for i in range(8)]
        JOBSR = (JOBSQ + [pair(Z1, KSEL + P * i) for i in range(2)] + [pair(Z1, KWIN + P * i) for i in range(2)]
                 + [pair(Z1, KCMP + P * g) for g in range(4)])
        JOBSM = [pair(ZM, P * i) for i in range(4)]

        def items0():
            out_ = []
            for h in range(8):
                r = slice(DH * (h % 2), DH * (h % 2) + DH)
                for c in range(C):
                    nk = P * (c + 1)
                    out_.append(Item(feat[r, 2048 + T * (h // 2) + P * c:2048 + T * (h // 2) + P * (c + 1)],
                                     feat[r, 3072 + T * (h // 2):3072 + T * (h // 2) + nk], nk, causal[:, c, 0:nk],
                                     DH ** -0.5, [Z0[:, b, BV + DH * h:BV + DH * h + DH] for b in range(c + 1)], DH,
                                     Z0[:, c, BQ + DH * h:BQ + DH * h + DH]))
            for h in range(8):
                r = slice(DH * (h % 2), DH * (h % 2) + DH)
                for c in range(C):
                    nk = P * (c + 1)
                    out_.append(Item(feat[r, 1024 + T * (h // 2) + P * c:1024 + T * (h // 2) + P * (c + 1)],
                                     feat[r, 768:768 + nk], nk, dsa_bias[:, c, 0:nk],
                                     DH ** -0.5, [Z0[:, b, AV:AV + DH] for b in range(c + 1)], DH,
                                     Z0[:, c, AQ + DH * h:AQ + DH * h + DH]))
            return out_

        def items1():
            out_ = []
            for h in range(16):
                (jq, half_), g = place1(h), h // 4
                r = slice(DH * half_, DH * half_ + DH)
                for branch, keys, v0 in ((1, feat[:, 4096:4608], VSEL), (2, KWT, VWIN)):
                    for c in range(C):
                        nk = P * (c + 1)
                        out_.append(Item(feat[r, 2048 + T * jq + P * c:2048 + T * jq + P * (c + 1)],
                                         keys[r, T * (g // 2):T * (g // 2) + nk], nk, causal[:, c, 0:nk], DH ** -0.5,
                                         [Z1[:, b, v0 + DH * g:v0 + DH * g + DH] for b in range(c + 1)], DH,
                                         Z1[:, c, DH * h:DH * h + DH],
                                         GATE[:, c, 3 * h + branch:3 * h + branch + 1], True))
            return out_

        def items_mem(l):
            return [Item(feat[:, T * h + P * c:T * h + P * (c + 1)], memk[l][:, h, :], T, zero[:, :], P ** -0.5,
                         [memv[l][:, b, P * h:P * h + P] for b in range(C)], P, ZM[:, c, P * h:P * h + P])
                    for h in range(4) for c in range(C)]

        def osrc0(c, k):
            return Z0[:, c, P * k:P * k + P] if k < 4 else Z0[:, c, BQ + P * (k - 4):BQ + P * (k - 3)]

        def osrc1(c, k):
            return Z1[:, c, P * k:P * k + P]

        def xsrc(c, k):
            return XN[:, c, P * k:P * k + P]

        def msrc(c, k):
            return ZM[:, c, P * k:P * k + P]

        def ysrc(c, k):
            return ZG[:, c, P * k:P * k + P]

        def dve_share(n):
            return LO_DVE if n == UNIT else n * 3 // 16 * 2

        def loop_turns(b):
            return b.first // b.per, b.last // b.per, b.per

        def landed_at(b, j, c):
            ref = b.base + 3 * b.first + c
            return plan.landed(ref) + 16 * plan.dmas[ref] * (j - b.first)

        block = ctx.enter_context(nc.Block())

        @block.sync
        def _(sp):
            def slot_free(u, static=True):
                if not static or u >= RING:
                    sp.wait_ge(lo_dve, u - RING + 1)
                    sp.wait_ge(lo_pool, u - RING + 1)

            def load_slab(s):
                for i in range(s.units):
                    u, nk = s.unit + i, min(4, s.k)
                    slot_free(u)
                    sp.dma_start(raw[u % RING][:, 0:nk * s.width].rearrange("p (k n) -> p k n", k=nk),
                                 s.w[512 * i:512 * i + P * nk, s.c0:s.c0 + s.width].rearrange("(k p) n -> p k n", p=P)
                                 ).then_inc(raw_loaded[u % RING], 16)

            def load_up(b, j, half, u, slot, static, e=None, h=None):
                slot_free(u, static)
                kind, l = b.load
                dst = raw[slot][:, :].rearrange("p (k a f) -> p k a f", k=4, a=2)
                if kind == "ffn":
                    for n in range(2):
                        src = a["ffn_w_in"][l, 512 * half:512 * half + 512, FF * n:FF * n + FF].rearrange("(k p) f -> p k f", p=P)
                        sp.dma_start(dst[:, :, n, :], src[:, :, bass.ds(j * FB, FB)]).then_inc(raw_loaded[slot], 16)
                else:
                    for n, w in enumerate(("exp_w_gate_2", "exp_w_up_2")):
                        src = a[w][0, bass.ds(e, 1), 512 * half:512 * half + 512, FB * h:FB * h + FB]
                        src = src.rearrange("e (k p) f -> p (e k) f", p=P)
                        sp.dma_start(dst[:, :, n, :], src).then_inc(raw_loaded[slot], 16)

            def load_down(b, j, u, slot, static):
                slot_free(u, static)
                kind, l = b.load
                w = a["ffn_w_out"][l] if kind == "ffn" else a["exp_w_down_2"][0].rearrange("e f n -> (e f) n")
                src = w[bass.ds(j * FB, FB), :].rearrange("(r p) n -> p r n", p=P)
                sp.dma_start(raw[slot][:, :].rearrange("p (r n) -> p r n", r=2), src).then_inc(raw_loaded[slot], 16)

            def load_block(b, j, static, e=None, h=None):
                u = b.base + 3 * j - 1
                s = (b.base - 1) % RING
                load_up(b, j, 0, u, s, static, e, h)
                load_up(b, j, 1, u + 1, (s + 1) % RING, static, e, h)
                load_down(b, j - 1, u + 2, (s + 2) % RING, static)

            def load_blocks(b):
                halves = 2 if b.per == 2 else 1
                where = (lambda j: (j // 2, j % 2)) if halves == 2 else (lambda j: (None, None))
                load_up(b, 0, 0, b.base, b.base % RING, True, *where(0))
                load_up(b, 0, 1, b.base + 1, (b.base + 1) % RING, True, *where(0))
                load_block(b, 1, True, *where(1))
                first, last, per = loop_turns(b)
                with sp.Fori(first, last) as i:
                    for n in range(per):
                        load_block(b, i * per + n, False, i, n)
                for j in range(b.last, b.n):
                    load_block(b, j, True, *where(j))
                load_down(b, b.n - 1, b.base + 3 * b.n - 1, (b.base + 3 * b.n - 1) % RING, True)

            sp.dma_start(x[:, :, :], a["x"][0].rearrange("(c p) n -> p c n", p=P)).then_inc(flag("x_in"), 16)
            for n, s in enumerate(plan.loads):
                if n == 1:
                    sp.dma_start(MEMIN, a["mem"][0].rearrange("(c p) n -> p c n", p=P)).then_inc(flag("mem_in"), 16)
                load_blocks(s) if isinstance(s, Blocks) else load_slab(s)
                if s is L[0]["mo"][-1]:
                    sp.wait_ge(item_out, L[0]["mheads"][1] + 8)
                    for n_, w in enumerate(("nsa_cmp_w1_k", "nsa_cmp_w1_v")):
                        sp.dma_start(CMPW[DH * n_:DH * n_ + DH], a[w][0].rearrange("(j d) e -> d j e", d=DH)
                                     ).then_inc(flag("cmp_weights_in"), 16)
                if s is L[1]["mo"][-1]:
                    sp.wait_ge(item_out, L[1]["mheads"][1] + 8)
                    sp.wait_ge(flag("gate_weights_zeroed"), 1)
                    for n_, w in enumerate(("rg_w_r_2", "rg_w_i_2")):
                        src = a[w][0].rearrange("(k h) c d -> h c k d", h=2)
                        for h in range(2):
                            r = slice(DH * h, DH * h + DH)
                            sp.dma_start(GATEW[r, n_, :, DH * h:DH * h + DH], src[h]).then_inc(flag("gate_weights_in"), 16)
                    sp.dma_start(POOLW, a["pool_w_2"][0].rearrange("g c d -> c g d")).then_inc(flag("gate_weights_in"), 16)
                if s is N["pb"][-1]:
                    sp.wait_ge(flag("lru_done"), 1)
                    wide = route_w
                    sp.dma_start(wide[:, :, 0:N_GRP], a["router_group_w_2"][0].rearrange("(k p) n -> p k n", p=P)).then_inc(flag("router_in"), 16)
                    sp.dma_start(wide[:, :, N_GRP:20], a["router_expert_w_2"][0].rearrange("(k p) n -> p k n", p=P)).then_inc(flag("router_in"), 16)
                    sp.dma_start(route_b[:, 0:N_GRP], a["router_group_b_2"].broadcast_to([P, N_GRP])).then_inc(flag("router_in"), 16)
                    sp.dma_start(route_b[:, N_GRP:20], a["router_expert_b_2"].broadcast_to([P, N_EXP])).then_inc(flag("router_in"), 16)
                    sp.dma_start(final_gain, a["norm_f_g_2"].rearrange("(a n) -> a n", a=1).broadcast_to([P, D])).then_inc(flag("final_gain_in"), 16)
            for c in range(C):
                sp.wait_ge(flag("out_ready"), c + 1)
                sp.dma_start(out[0, P * c:P * c + P, :], XN[:, c, :]).then_inc(flag("stored"), 16)
            sp.wait_ge(flag("stored"), 32)

        @block.gpsimd
        def _(pool):
            step = Chain(pool, pool_step)
            at = [0]

            def lo(u, slot, n):
                s = dve_share(n)
                pool.wait_ge(hi_done, u + 1)
                pool.tensor_tensor(wlo[slot][:, s:n], raw[slot][:, s:n], whi[slot][:, s:n].bitcast(F32),
                                   ALU.subtract).then_inc(lo_pool, 1)

            def split_to(end):
                while at[0] < min(end, n_units):
                    lo(at[0], at[0] % RING, plan.width[at[0]])
                    at[0] += 1

            def blocks(b):
                first, last, per = loop_turns(b)
                split_to(b.base + 3 * b.first + 1)
                with pool.Fori(first, last) as i:
                    for n in range(per):
                        for c in range(1, 4):
                            lo(b.base + 3 * (i * per + n) + c, (b.base + c) % RING, UNIT)
                at[0] = b.base + 3 * b.last + 1

            step(pool.memset(ident[:, :], 0.0))
            step(pool.affine_select(out=ident[:, :], in_=ident[:, :], compare_op=ALU.not_equal, fill=1.0,
                                    base=0, pattern=[[-1, P]], channel_multiplier=1))
            step(pool.memset(zero[:, :], 0.0))
            for c in range(C):
                step(pool.affine_select(out=causal[:, c, :], in_=zero[:, :], compare_op=ALU.is_ge, fill=NEG,
                                        base=P * c, pattern=[[-1, T]], channel_multiplier=1))
            for c in range(C):
                step(pool.affine_select(out=cmp_bias[:, c, :], in_=zero[:, 0:32], compare_op=ALU.is_ge, fill=NEG,
                                        base=P * c - (CMP_LEN - 1), pattern=[[-CMP_STRIDE, 32]], channel_multiplier=1))
            step(pool.memset(cmp_keep[:, :, :], 1.0))
            for c in range(C):
                step(pool.affine_select(out=cmp_keep[:, c, :], in_=cmp_keep[:, c, :], compare_op=ALU.is_ge, fill=0.0,
                                        base=P * c - (CMP_LEN - 1), pattern=[[-CMP_STRIDE, 32]], channel_multiplier=1))
            for t in range(16):
                step(pool.memset(numbers[:, t:t + 1], 1.0 / (t + 1)))
            pool.memset(half[:, :], 0.5).then_inc(flag("masks_ready"), 1)
            for l in range(2):
                split_to(L[l]["ff"].base)
                if l == 1:
                    pool.wait_ge(item_out, L[1]["mheads"][1] + 8)
                    pool.memset(GATEW, 0.0).then_inc(flag("gate_weights_zeroed"), 1)
                blocks(L[l]["ff"])
            split_to(N["moe"].base)
            blocks(N["moe"])
            split_to(n_units)

        @block.scalar
        def _(act):
            step = Chain(act, act_step)
            at = [0]

            def hi(u, slot, n, landed, static=True):
                act.wait_ge(raw_loaded[slot], landed)
                if not static or u >= RING:
                    act.wait_ge(unit_used, u - RING + 1)
                act.activation(whi[slot][:, 0:n], raw[slot][:, 0:n], ACT.Copy).then_inc(hi_done, 1)

            def split_to(end):
                while at[0] < min(end, n_units):
                    u = at[0]
                    hi(u, u % RING, plan.width[u], plan.landed(u))
                    at[0] += 1

            def product(slabs, dst, src=bank_of):
                for s in slabs:
                    split_to(s.end + 2)
                    if s.evac == "both":
                        act.wait_ge(unit_used, s.end)
                        act.activation(dst(s, 0), src(s, 0), ACT.Copy).then_inc(slab_act, 1)

            def to_t(base, nk, gain, dst):
                for b in range(nk // 2):
                    act.wait_ge(turned, base + b + 1)
                    bank = TB[(base + b) % 2]
                    for n in range(2):
                        k = 2 * b + n
                        ins = act.activation(dst[:, k, :], bank[:, T * n:T * n + T], ACT.Copy,
                                             scale=gain(k) if callable(gain) else gain)
                    ins.then_inc(turn_act, 1)

            def squares(src, tag, scratch=2048):
                for c in range(C):
                    ins = act.activation(z[:, scratch + D * c:scratch + D * c + D], src[:, c, :], ACT.Square,
                                         accum_out=sumsq[:, c:c + 1])
                ins.then_inc(flag("squared_" + tag), 1)

            def head_squares(parts, slabs, tag):
                act.wait_ge(slab_act, slabs[-1].done_act)
                act.wait_ge(slab_dve, slabs[-1].done_dve)
                for src, dst in parts:
                    ins = act.activation(dst, src, ACT.Square)
                ins.then_inc(flag("head_squares_" + tag), 1)

            def attention(items, first, batch):
                for i, it in enumerate(items):
                    g = first + i
                    act.wait_ge(item_masked, g + 1)
                    if i >= 3:
                        act.wait_ge(turned, batch + i - 2)
                    act.activation(prob[g % 3][:, 0:it.nk], masked[g % 2][:, 0:it.nk], ACT.Exp,
                                   bias=item_neg[:, i:i + 1], accum_out=item_sum[:, i:i + 1]).then_inc(exped, 1)

            def ff_up_out(j, static=True):
                for c in range(C):
                    if c == 0:
                        act.wait_ge(unit_used, ff_gu_unit(j))
                        if not static or ff_n(j) >= 1:
                            act.wait_ge(ff_silu, ff_n(j))
                    act.activation(silu[:, c, 0, :], TB[c][:, 0:FB], ACT.Tanh, scale=0.5).then_inc(ff_tanh, 1)

            def ff_hidden(j):
                act.wait_ge(ff_turned, ff_n(j) + 1)
                act.activation(FHI, SCB[0][:, :].rearrange("p (f t) -> p f t", f=2), ACT.Copy).then_inc(ff_hi, 1)

            def blocks(b):
                nonlocal ff_n, ff_gu_unit
                ff_n = lambda j: b.start + j
                ff_gu_unit = lambda j: b.base + 2 if isinstance(j, int) and j == 0 else b.base + 3 * j + 1
                split_to(b.base + 3)
                ff_up_out(0)
                split_to(b.base + 4)
                ff_hidden(0)
                split_to(b.base + 6)
                ff_up_out(1)
                split_to(b.base + 7)
                first, last, per = loop_turns(b)
                with act.Fori(first, last) as i:
                    for n in range(per):
                        j = i * per + n
                        ff_hidden(j - 1)
                        for c in (1, 2):
                            hi(b.base + 3 * j + c, (b.base + c) % RING, UNIT, landed_at(b, j, c), False)
                        ff_up_out(j, False)
                        hi(b.base + 3 * j + 3, (b.base + 3) % RING, UNIT, landed_at(b, j, 3), False)
                at[0] = b.base + 3 * b.last + 1
                for j in range(b.last, b.n):
                    ff_hidden(j - 1)
                    split_to(b.base + min(3 * j + 3, 3 * b.n))
                    ff_up_out(j)
                    split_to(b.base + min(3 * j + 4, 3 * b.n))
                ff_hidden(b.n - 1)

            ff_n = ff_gu_unit = None

            def load(dst, src, name):
                act.dma_start(dst, src).then_inc(flag(name), 16)

            for l in range(2):
                for g, name in ((G_MIX, "norm_mix"), (G_MEM, "norm_mem"), (G_SRC, "norm_mem_src"), (G_FFN, "norm_ffn")):
                    load(rows[8 * g[l]:8 * g[l] + 8, 0, :], a[name][l].rearrange("(k p) -> k p", p=P), "rows_in")
            for g, name in ((G_N1, "norm1_g_2"), (G_N2, "norm2_g_2")):
                load(rows[8 * g:8 * g + 8, 0, :], a[name][0].rearrange("(k p) -> k p", p=P), "rows_in")
            load(rows[0:32, 1, :], a["conv_w_2"][0].rearrange("w (k p) -> (w k) p", p=P), "rows_in")
            for r, name in ((R_CB, "conv_b_2"), (R_BR, "rg_b_r_2"), (R_BI, "rg_b_i_2"), (R_LAM, "rg_lambda_2")):
                load(rows[r:r + 8, 1, :], a[name][0].rearrange("(k p) -> k p", p=P), "rows_in")
            load(rows[R_PS:R_PS + 4, 1, :], a["pool_scale_2"][0].rearrange("(k p) -> k p", p=P), "rows_in")
            load(pos_i[:, :], a["positions"].rearrange("a (c p) -> (a c) p", p=P), "positions_in")
            act.wait_ge(flag("x_in"), 16)
            squares(x, "mix0")
            for n, name in enumerate(("dsa_q_norm", "dsa_k_norm", "moba_q_norm", "moba_k_norm", "nsa_q_norm",
                                      "nsa_kcmp_norm", "nsa_ksel_norm", "nsa_kwin_norm")):
                load(gains[:, n, :], a[name].broadcast_to([P, DH]), "gains_in")
            for l in range(2):
                load(mem_q_gain[:, l, :], a["mem_q_norm"][l:l + 1, :].broadcast_to([P, P]), "gains_in")
                load(mem_k_gain[:, l, :], a["mem_k_norm"][l:l + 1, :].broadcast_to([P, P]), "gains_in")
            load(pos_rows[:, 0:DH], a["nsa_cmp_pos_k"][0], "gains_in")
            load(pos_rows[:, DH:P], a["nsa_cmp_pos_v"][0], "gains_in")
            load(w2[:, 0, :], a["nsa_cmp_w2_k"][0], "gains_in")
            load(w2[:, 1, :], a["nsa_cmp_w2_v"][0], "gains_in")

            for l in range(2):
                s = L[l]
                if l:
                    act.wait_ge(flag("ff_added0"), 1)
                    squares(x, "mix1")
                to_t(s["hturn"], KC, gain_of(G_MIX[l]), ahi)
                if l == 0:
                    act.wait_ge(flag("mem_in"), 16)
                    squares(MEMIN, "mem", 4944)
                    act.wait_ge(flag("angles"), 1)
                    act.activation(sine[:, :, :], angle[:, 2], ACT.Sin)
                    act.activation(cosine[:, :, :], angle[:, 3], ACT.Sin).then_inc(flag("rotation"), 1)

                    def z0(s_, c):
                        return Z0[:, c, s_.c0:s_.c0 + s_.width]

                    product(s["in"][0:2], z0)
                    head_squares([(heads(Z0, AQ, 9, DH), SQA)], s["in"][0:2], "a")
                    product(s["in"][2:3], z0)
                    head_squares([(heads(Z0, BQ, 8, DH), SQQ)], s["in"][0:3], "bq")
                    product(s["in"][3:4], z0)
                    head_squares([(heads(Z0, BK, 8, DH), SQK)], s["in"][0:4], "bk")
                    product(s["in"][4:5], z0)
                    for b in range(4):
                        act.wait_ge(turned, mem_turn + b + 1)
                        for m, dst in enumerate((bhi, ahi)):
                            for n in range(2):
                                ins = act.activation(dst[:, 2 * b + n, :], TB[(mem_turn + b) % 2][:, T * n:T * n + T],
                                                     ACT.Copy, scale=gain_of(G_SRC[m])(2 * b + n))
                        ins.then_inc(turn_act, 1)
                    for n, s_ in enumerate(M[0]["kv"]):
                        for v in range(s_.units):
                            split_to(s_.unit + v + RING)
                            for i in range(8 * n + 4 * v, 8 * n + 4 * v + 4):
                                g, nk = s["index"] + i, P * (i // 8 + 1)
                                act.wait_ge(scored, g + 1)
                                if i >= 3:
                                    act.wait_ge(item_masked, g - 2)
                                act.activation(prob[g % 3][:, 0:nk], SCB[g % 2][:, 0:nk], ACT.Relu).then_inc(exped, 1)
                        act.wait_ge(unit_used, s_.end)
                        act.activation((memk_rows if n == 0 else memv)[0][:, 0, :], bank_of(s_, 0), ACT.Copy).then_inc(slab_act, 1)
                    product(M[1]["kv"], lambda s_, c: (memk_rows if s_.c0 == 0 else memv)[1][:, c, :])
                    attention(items0(), *s["heads"][::2])
                    to_t(s["oturn"], KC, 1.0, ahi)
                else:
                    product(s["in"], z1_dst, z1_src)
                    SQ1 = z[:, 5216:9216]
                    head_squares([(heads(Z1, NQ, 16, DH), SQ1[:, 0:2048].rearrange("p (c h d) -> p c h d", c=C, d=DH)),
                                  (heads(Z1, KSEL, 4, DH), SQ1[:, 2048:2560].rearrange("p (c h d) -> p c h d", c=C, d=DH)),
                                  (heads(Z1, KWIN, 4, DH), SQ1[:, 2560:3072].rearrange("p (c h d) -> p c h d", c=C, d=DH))],
                                 s["in"], "qk1")
                    act.activation(GATE, Z1[:, :, GT:C_W], ACT.Tanh, scale=0.5).then_inc(flag("gates_tanh"), 1)
                    split_to(s["in"][-1].end + RING)
                    act.wait_ge(flag("cmp_hidden"), 1)
                    act.activation(HIT, HID, ACT.Tanh, scale=0.5).then_inc(flag("cmp_tanh"), 1)
                    for c in range(C):
                        act.wait_ge(flag("cmp_shifted"), c + 1)
                        act.activation(CP, CS, ACT.Exp).then_inc(flag("cmp_exp"), 1)
                    attention(items1(), *s["heads"][::2])
                    to_t(s["oturn"], KC, 1.0, ahi)
                if l == 0:
                    act.wait_ge(slab_dve, M[1]["kv"][-1].done_dve)
                    for m in range(2):
                        ins = act.activation(zv(4944 + 1024 * m, 512), memk_rows[m], ACT.Square)
                    ins.then_inc(flag("head_squares_mk"), 1)
                product(s["out"], None)
                act.wait_ge(slab_dve, s["out"][-1].done_dve)
                squares(x, f"memq{l}")
                to_t(s["mturn"], KC, gain_of(G_MEM[l]), ahi)
                product(s["mq"], lambda s_, c: ZM[:, c, :])
                head_squares([(heads(ZM, 0, 4, P), heads(zv(2048, 512), 0, 4, P))], s["mq"], f"memq{l}")
                if l == 0:
                    for m in range(2):
                        act.wait_ge(turned, M[m]["kturn"] + 2)
                        for b in range(2):
                            act.activation(memo[:, 2048 * m + 512 * b:2048 * m + 512 * b + 512],
                                           TB[(M[m]["kturn"] + b) % 2][:, :], ACT.Copy).then_inc(turn_act, 1)
                split_to(s["mo"][-1].end)
                attention(items_mem(l), *s["mheads"][::2])
                to_t(s["moturn"], 4, 1.0, ahi)
                product(s["mo"], None)
                act.wait_ge(slab_dve, s["mo"][-1].done_dve)
                squares(x, f"ffn{l}")
                to_t(s["fturn"], KC, gain_of(G_FFN[l]), ahi)
                blocks(s["ff"])

            act.wait_ge(flag("ff_added1"), 1)
            squares(x, "mix2")
            to_t(N["hturn"], KC, gain_of(G_N1), ahi)
            act.wait_ge(flag("minus_abs_lambda"), 1)
            act.activation(LAM[:, 1, :], LAM[:, 1, :], ACT.Exp).then_inc(flag("exp_lambda"), 1)
            product(N["in"], lambda s_, c: ZA[:, c, s_.c0:s_.c0 + s_.width])
            product(N["gates"][0:2], lambda s_, c: ZG[:, c, s_.c0 - GA:s_.c0 - GA + 512])
            for k in range(8):
                act.wait_ge(turned, N["gturn"] + k + 1)
                bank = TB[(N["gturn"] + k) % 2]
                act.activation(RG[:, k, :], bank[:, 0:T], ACT.Tanh, scale=0.5, bias=HB[:, 0, k:k + 1])
                act.activation(IG[:, k, :], bank[:, T:2 * T], ACT.Tanh, scale=0.5, bias=HB[:, 1, k:k + 1]).then_inc(turn_act, 1)
            split_to(N["gates"][1].end + RING)
            act.wait_ge(flag("log_decay"), 1)
            act.activation(ULT, RG, ACT.Exp, scale=-1.0).then_inc(flag("decay"), 1)
            act.wait_ge(flag("decay"), 1)
            act.activation(RG, RG, ACT.Tanh).then_inc(flag("decay_tanh"), 1)
            act.wait_ge(flag("gelu_inner"), 1)
            act.activation(IG, IG, ACT.Tanh, scale=math.sqrt(2 / math.pi)).then_inc(flag("gelu_tanh"), 1)
            product(N["gates"][2:4], lambda s_, c: ZG[:, c, s_.c0 - GA:s_.c0 - GA + 512])
            act.wait_ge(slab_act, N["gates"][-1].done_act)
            act.wait_ge(slab_dve, N["gates"][-1].done_dve)
            act.activation(ZG, ZG, ACT.Tanh, scale=0.5).then_inc(flag("mix_gates"), 1)
            to_t(N["yturn"], 4, lambda k: cols[:, 1, R_PS + k:R_PS + k + 1], ahi)
            act.wait_ge(flag("drive_squared"), 1)
            act.activation(RG, RG, ACT.Sqrt, scale=0.25).then_inc(flag("drive_scale"), 1)
            act.wait_ge(flag("lru_out"), 1)
            act.activation(bhi[:, :, :], ULT, ACT.Copy).then_inc(flag("lru_hi"), 1)
            product(N["pa"], None)
            product(N["pb"], None)
            to_t(N["oturn"], KC, 0.5, ahi)
            product(N["out"], None)
            act.wait_ge(slab_dve, N["out"][-1].done_dve)
            squares(x, "moe")
            to_t(N["h2turn"], KC, gain_of(G_N2), ahi)
            act.wait_ge(flag("router_in"), 64)
            act.activation(rhi[:, :, :], route_w, ACT.Copy).then_inc(flag("router_hi"), 1)
            split_to(N["moe"].base + RING)
            act.wait_ge(flag("group_shifted"), 1)
            act.activation(rt[:, 1, :, 0:N_GRP], rt[:, 0, :, 0:N_GRP], ACT.Exp).then_inc(flag("group_exp"), 1)
            act.wait_ge(flag("expert_gap"), 1)
            act.activation(rt[:, 9, :, 0:1], rt[:, 8, :, 0:1], ACT.Exp).then_inc(flag("expert_exp"), 1)
            blocks(N["moe"])
            act.wait_ge(flag("ff_added2"), 1)
            squares(x, "final")

        @block.vector
        def _(dve):
            step = Chain(dve, dve_step)
            at = [0]

            def lo(u, slot, n):
                s = dve_share(n)
                dve.wait_ge(hi_done, u + 1)
                dve.tensor_tensor(wlo[slot][:, 0:s], raw[slot][:, 0:s], whi[slot][:, 0:s].bitcast(F32),
                                  ALU.subtract).then_inc(lo_dve, 1)

            def split_to(end):
                while at[0] < min(end, n_units):
                    lo(at[0], at[0] % RING, plan.width[at[0]])
                    at[0] += 1

            def product(slabs, dst, src=bank_of):
                for s in slabs:
                    split_to(s.end + 2)
                    dve.wait_ge(unit_used, s.end)
                    if s.evac == "both":
                        dve.tensor_copy(dst(s, 1), src(s, 1)).then_inc(slab_dve, 1)
                    else:
                        for c in range(C):
                            if dst is None:
                                xs = x[:, c, s.c0:s.c0 + s.width]
                                dve.tensor_tensor(xs, xs, bank_of(s, c), ALU.add).then_inc(slab_dve, 1)
                            else:
                                dst(s, c)
                if slabs[-1].evac == "dve":
                    dve.wait_ge(slab_dve, slabs[-1].done_dve)

            def rsqrt(n, d):
                m, y, t, u = (s_[:, 0:n] for s_ in (s_mean, s_y, s_t, s_u))
                step(dve.tensor_scalar(m, m, 1.0 / d, EPS, ALU.mult, ALU.add))
                step(dve.tensor_scalar(s_bits[:, 0:n], m.bitcast(I32), 1, None, ALU.logical_shift_right))
                step(dve.tensor_scalar(y.bitcast(I32), s_bits[:, 0:n], -1.0, 1597463007.0, ALU.mult, ALU.add))
                for _ in range(3):
                    step(dve.tensor_tensor(t, y, y, ALU.mult))
                    step(dve.tensor_tensor(u, t, m, ALU.mult))
                    step(dve.tensor_scalar(t, u, -0.5, 1.5, ALU.mult, ALU.add))
                    step(dve.tensor_tensor(y, y, t, ALU.mult))

            def norm(src, tag, dst=XN):
                dve.wait_ge(flag("squared_" + tag), 1)
                step(dve.tensor_copy(s_mean[:, 0:C], sumsq[:, :]))
                rsqrt(C, D)
                for c in range(C):
                    ins = dve.tensor_scalar(dst[:, c, :], src[:, c, :], s_y[:, c:c + 1], None, ALU.mult)
                ins.then_inc(flag("normed_" + tag), 1)

            def to_t(base, nk, gain, hi_, dst):
                for b in range(nk // 2):
                    dve.wait_ge(turn_act, plan.turn_act[base + b + 1])
                    bank = TB[(base + b) % 2]
                    for n in range(2):
                        k = 2 * b + n
                        ins = dve.scalar_tensor_tensor(out=dst[:, k, :], in0=bank[:, T * n:T * n + T],
                                                       scalar=gain(k) if callable(gain) else gain,
                                                       in1=hi_[:, k, :].bitcast(F32), op0=ALU.mult, op1=ALU.subtract)
                    ins.then_inc(turn_dve, 1)

            def turns(base, n, dst):
                for b in range(n):
                    dve.wait_ge(turned, base + b + 1)
                    dve.tensor_copy(dst(b), TB[(base + b) % 2][:, :]).then_inc(turn_dve, 1)
                dve.wait_ge(turn_dve, plan.turn_dve[base + n])

            def head_norm(parts, d, tag):
                dve.wait_ge(flag("head_squares_" + tag), 1)
                at_ = 0
                for sq, v, _ in parts:
                    n = v.shape[2]
                    step(dve.tensor_reduce(s_mean[:, at_:at_ + C * n].rearrange("p (c h) -> p c h", c=C), sq, AX, ALU.add))
                    at_ += C * n
                rsqrt(at_, d)
                at_ = 0
                for _, v, _ in parts:
                    n = v.shape[2]
                    r = s_y[:, at_:at_ + C * n].rearrange("p (c h) -> p c h", c=C).unsqueeze(3).broadcast_to([P, C, n, d])
                    ins = dve.tensor_tensor(v, v, r, ALU.mult)
                    at_ += C * n
                step(ins)
                for _, _, gs in parts:
                    for v, g in gs:
                        n = v.shape[2]
                        ins = dve.tensor_tensor(v, v, g.unsqueeze(1).unsqueeze(1).broadcast_to([P, C, n, d]), ALU.mult)
                step(ins)

            def rope(v, hf, scratch):
                n = v.shape[2]
                w = C * n * hf
                v1, v2 = v[:, :, :, 0:hf], v[:, :, :, hf:2 * hf]
                co, si = (t_[:, :, 0:HALF:HALF // hf].unsqueeze(2).broadcast_to([P, C, n, hf]) for t_ in (cosine, sine))
                t = [scratch[:, w * i:w * i + w].rearrange("p (c h d) -> p c h d", c=C, h=n) for i in range(4)]
                dve.tensor_tensor(t[0], v1, co, ALU.mult)
                dve.tensor_tensor(t[1], v2, si, ALU.mult)
                dve.tensor_tensor(t[2], v2, co, ALU.mult)
                step(dve.tensor_tensor(t[3], v1, si, ALU.mult))
                dve.tensor_tensor(v1, t[0], t[1], ALU.subtract)
                step(dve.tensor_tensor(v2, t[2], t[3], ALU.add))

            def attention(items, first, outs, batch):
                n = len(items)
                for t in range(n + 3):
                    if t < n:
                        it, g = items[t], first + t
                        dve.wait_ge(scored, g + 1)
                        if t >= 2:
                            dve.wait_ge(exped, g - 1)
                        step(dve.tensor_tensor_reduce(masked[g % 2][:, 0:it.nk], SCB[g % 2][:, 0:it.nk], it.bias, it.scale,
                                                      TAKEN, ALU.add, ALU.max, item_max[:, t:t + 1]))
                        dve.tensor_scalar(item_neg[:, t:t + 1], item_max[:, t:t + 1], -1.0, None, ALU.mult
                                          ).then_inc(item_masked, 1)
                    if 0 <= t - 2 < n:
                        i = t - 2
                        dve.wait_ge(turned, batch + i + 1)
                        if i >= 2:
                            dve.wait_ge(pved, outs + i - 1)
                        dve.tensor_copy(probt[i % 2][:, 0:items[i].nk], TB[(batch + i) % 2][:, 0:items[i].nk]
                                        ).then_inc(turn_dve, 1)
                    if 0 <= t - 3 < n:
                        i = t - 3
                        it = items[i]
                        dve.wait_ge(pved, outs + i + 1)
                        inv = item_inv[:, i:i + 1]
                        step(dve.reciprocal(inv, item_sum[:, i:i + 1]))
                        if it.weight is not None:
                            step(dve.tensor_tensor(inv, inv, it.weight, ALU.mult))
                        o = G[i % 2][:, 0:it.dv]
                        if it.add:
                            if i:
                                dve.wait_ge(item_out, outs + i)
                            dve.scalar_tensor_tensor(out=it.out, in0=o, scalar=inv, in1=it.out, op0=ALU.mult,
                                                     op1=ALU.add).then_inc(item_out, 1)
                        else:
                            dve.tensor_scalar(it.out, o, inv, None, ALU.mult).then_inc(item_out, 1)

            def ff_silu_(b, j, static=True):
                n = b.start + j
                for c in range(C):
                    dve.wait_ge(ff_tanh, 2 * n + c + 1)
                    if c == 0 and (not static or n >= 1):
                        dve.wait_ge(ff_turned, n)
                    gate, up, t1 = TB[c][:, 0:FB], TB[c][:, FB:2 * FB], silu[:, c, 1, :]
                    dve.scalar_tensor_tensor(out=t1, in0=silu[:, c, 0, :], scalar=1.0, in1=gate, op0=ALU.add,
                                             op1=ALU.mult).then_inc(flag("silu_half"), 1)
                    dve.wait_ge(flag("silu_half"), 2 * n + c + 1)
                    w = half[:, 0:1] if b.load[0] == "ffn" else half_comb[:, c, bass.ds(j, 1)]
                    ins = dve.scalar_tensor_tensor(out=t1, in0=t1, scalar=w, in1=up, op0=ALU.mult, op1=ALU.mult)
                ins.then_inc(ff_silu, 1)

            def ff_hidden(b, j):
                dve.wait_ge(ff_hi, b.start + j + 1)
                dve.tensor_tensor(FLO, SCB[0][:, :].rearrange("p (f t) -> p f t", f=2), FHI.bitcast(F32),
                                  ALU.subtract).then_inc(ff_lo, 1)

            def blocks(b):
                split_to(b.base + 3)
                ff_silu_(b, 0)
                split_to(b.base + 4)
                ff_hidden(b, 0)
                split_to(b.base + 6)
                ff_silu_(b, 1)
                split_to(b.base + 7)
                first, last, per = loop_turns(b)
                with dve.Fori(first, last) as i:
                    for n in range(per):
                        j = i * per + n
                        ff_hidden(b, j - 1)
                        for c in (1, 2):
                            lo(b.base + 3 * j + c, (b.base + c) % RING, UNIT)
                        ff_silu_(b, j, False)
                        lo(b.base + 3 * j + 3, (b.base + 3) % RING, UNIT)
                at[0] = b.base + 3 * b.last + 1
                for j in range(b.last, b.n):
                    ff_hidden(b, j - 1)
                    split_to(b.base + min(3 * j + 3, 3 * b.n))
                    ff_silu_(b, j)
                    split_to(b.base + min(3 * j + 4, 3 * b.n))
                ff_hidden(b, b.n - 1)

            def add_blocks(b, l):
                dve.wait_ge(unit_used, b.base + 3 * b.n)
                for c in range(C):
                    for n in range(2):
                        xs = x[:, c, 512 * n:512 * n + 512]
                        ins = dve.tensor_tensor(xs, xs, G[2 * c + n][:, :], ALU.add)
                ins.then_inc(flag(f"ff_added{l}"), 1)
                dve.wait_ge(flag(f"ff_added{l}"), 1)

            dve.wait_ge(flag("positions_in"), 16)
            dve.tensor_copy(pos_r[:, :], pos_i[:, :]).then_inc(flag("positions_float"), 1)
            dve.wait_ge(flag("positions_turned"), 1)
            step(dve.tensor_copy(pos_f[:, :], SCB[0][:, 0:C]))
            dve.tensor_copy(cols[:, 0, :], SCB[0][:, 128:208])
            dve.tensor_copy(cols[:, 1, 0:68], SCB[0][:, 256:324]).then_inc(flag("cols_ready"), 1)

            def angles():
                raw_angle = angle[:, 0]
                for i in range(HALF):
                    freq = float(np.float32(ROPE_THETA) ** np.float32(-2.0 * i / (2 * HALF)))
                    ins = dve.tensor_scalar(raw_angle[:, :, i], pos_f[:, :], freq, None, ALU.mult)
                step(ins)
                two_pi = 2 * math.pi
                part1 = 6.28125
                part2 = round((two_pi - part1) * 2 ** 20) / 2 ** 20
                part3 = two_pi - part1 - part2
                for n, quarter in ((2, 0.0), (3, 0.25)):
                    turn_, r = angle[:, 1], angle[:, n]
                    step(dve.tensor_scalar(turn_, raw_angle, 1 / two_pi, quarter, ALU.mult, ALU.add))
                    step(dve.tensor_scalar(turn_, turn_, 12582912.0, None, ALU.add))
                    step(dve.tensor_scalar(turn_, turn_, -12582912.0, None, ALU.add))
                    step(dve.scalar_tensor_tensor(out=r, in0=turn_, scalar=-part1, in1=raw_angle, op0=ALU.mult, op1=ALU.add))
                    step(dve.scalar_tensor_tensor(out=r, in0=turn_, scalar=-part2, in1=r, op0=ALU.mult, op1=ALU.add))
                    step(dve.scalar_tensor_tensor(out=r, in0=turn_, scalar=-part3, in1=r, op0=ALU.mult, op1=ALU.add))
                    step(dve.tensor_scalar(r, r, quarter * two_pi, None, ALU.add))
                    ins = dve.tensor_scalar(r, r, 3.1415925, -3.1415925, ALU.min, ALU.max)
                    step(ins) if n == 2 else ins.then_inc(flag("angles"), 1)

            for l in range(2):
                s = L[l]
                norm(x, f"mix{l}")
                to_t(s["hturn"], KC, gain_of(G_MIX[l]), ahi, alo)
                if l == 0:
                    angles()
                    dve.wait_ge(flag("mem_in"), 16)
                    norm(MEMIN, "mem", MEMIN)
                    dve.wait_ge(flag("gains_in"), 16 * 16)
                    dve.wait_ge(flag("masks_ready"), 1)
                    dve.wait_ge(flag("rotation"), 1)

                    def z0(s_, c):
                        return Z0[:, c, s_.c0:s_.c0 + s_.width]

                    in_ = s["in"]
                    va, vq, vk = heads(Z0, AQ, 9, DH), heads(Z0, BQ, 8, DH), heads(Z0, BK, 8, DH)
                    product(in_[0:2], z0)
                    head_norm([(SQA, va, [(va[:, :, 0:8, :], gains[:, N_AQ, :]), (va[:, :, 8:9, :], gains[:, N_AK, :])])],
                              DH, "a")
                    split_to(in_[1].end + RING)
                    rope(heads(Z0, IQ, 9, 32), 4, ROPET)
                    rope(va, HALF, ROPET)
                    product(in_[2:3], z0)
                    head_norm([(SQQ, vq, [(vq, gains[:, N_BQ, :])])], DH, "bq")
                    split_to(in_[2].end + RING)
                    rope(vq, HALF, ROPET)
                    for n in range(4):
                        dve.tensor_copy(COPIES[:, :, 32 * n:32 * n + 32], Z0[:, :, IK:IW])
                    for n in range(2):
                        dve.tensor_copy(COPIES[:, :, P + DH * n:P + DH * n + DH], Z0[:, :, AK:AV])
                    product(in_[3:4], z0)
                    head_norm([(SQK, vk, [(vk, gains[:, N_BK, :])])], DH, "bk")
                    split_to(in_[3].end + RING)
                    rope(vk, HALF, ROPET)
                    dve.sem_inc(flag("qk_ready0"), 1)
                    product(in_[4:5], z0)
                    for b in range(4):
                        dve.wait_ge(turn_act, plan.turn_act[mem_turn + b + 1])
                        for m, (hi_, dst) in enumerate(((bhi, blo), (ahi, alo))):
                            for n in range(2):
                                k = 2 * b + n
                                ins = dve.scalar_tensor_tensor(out=dst[:, k, :], in0=TB[(mem_turn + b) % 2][:, T * n:T * n + T],
                                                               scalar=gain_of(G_SRC[m])(k), in1=hi_[:, k, :].bitcast(F32),
                                                               op0=ALU.mult, op1=ALU.subtract)
                        ins.then_inc(turn_dve, 1)
                    turns(s["qturn"], 8, lambda b: feat[:, 512 * b:512 * b + 512])
                    for n, s_ in enumerate(M[0]["kv"]):
                        for v in range(s_.units):
                            split_to(s_.unit + v + RING)
                            for i in range(8 * n + 4 * v, 8 * n + 4 * v + 4):
                                c, h, g = i // 8, i % 8, s["index"] + i
                                nk = P * (c + 1)
                                dve.wait_ge(exped, g + 1)
                                sc, w = dsa_bias[:, c, 0:nk], Z0[:, c, IW + h:IW + h + 1]
                                if h == 0:
                                    dve.tensor_scalar(sc, prob[g % 3][:, 0:nk], w, None, ALU.mult).then_inc(item_masked, 1)
                                else:
                                    dve.scalar_tensor_tensor(out=sc, in0=prob[g % 3][:, 0:nk], scalar=w, in1=sc, op0=ALU.mult,
                                                             op1=ALU.add).then_inc(item_masked, 1)
                                dve.wait_ge(item_masked, g + 1)
                        dve.wait_ge(unit_used, s_.end)
                        dve.tensor_copy((memk_rows if n == 0 else memv)[0][:, 1, :], bank_of(s_, 1)).then_inc(slab_dve, 1)

                    def best_keys(c):
                        nk = P * (c + 1)
                        sc = dsa_bias[:, c, 0:nk]
                        step(dve.tensor_tensor(sc, sc, causal[:, c, 0:nk], ALU.add))
                        for _ in range(TOPK // 8):
                            step(dve.max(best8, sc))
                            step(dve.match_replace(out=sc, in_to_replace=best8, in_values=sc, imm_value=TAKEN))
                        step(dve.tensor_scalar(sc, sc, TAKEN, NEG, ALU.not_equal, ALU.mult))
                        step(dve.tensor_tensor(sc, sc, causal[:, c, 0:nk], ALU.add))

                    split_to(M[0]["kv"][-1].end + RING)
                    for c in range(C):
                        best_keys(c)
                        product(M[1]["kv"][c:c + 1], lambda s_, c_: (memk_rows if s_.c0 == 0 else memv)[1][:, c_, :])
                    attention(items0(), *s["heads"])
                    to_t(s["oturn"], KC, 1.0, ahi, alo)
                else:
                    product(s["in"], z1_dst, z1_src)
                    SQ1 = z[:, 5216:9216]
                    vq, vks, vkw = heads(Z1, NQ, 16, DH), heads(Z1, KSEL, 4, DH), heads(Z1, KWIN, 4, DH)
                    head_norm([(SQ1[:, 0:2048].rearrange("p (c h d) -> p c h d", c=C, d=DH), vq, [(vq, gains[:, N_NQ, :])]),
                               (SQ1[:, 2048:2560].rearrange("p (c h d) -> p c h d", c=C, d=DH), vks, [(vks, gains[:, N_KS, :])]),
                               (SQ1[:, 2560:3072].rearrange("p (c h d) -> p c h d", c=C, d=DH), vkw, [(vkw, gains[:, N_KW, :])])],
                              DH, "qk1")
                    dve.sem_inc(flag("q_plain1"), 1)
                    turns(s["qturn"], 4, lambda b: feat[:, 512 * b:512 * b + 512])
                    rope(vq, HALF, SQ1)
                    rope(vks, HALF, SQ1)
                    rope(vkw, HALF, SQ1)
                    dve.sem_inc(flag("qk_ready1"), 1)
                    turns(s["qrturn"], 8, lambda b: feat[:, 2048 + 512 * b:2560 + 512 * b] if b < 5 else
                          z[:, 5216 + 512 * (b - 5):5728 + 512 * (b - 5)])
                    dve.wait_ge(turned, s["posturn"] + 1)
                    dve.tensor_copy(POST, TB[s["posturn"] % 2][:, 0:CMP_LEN]).then_inc(turn_dve, 1)
                    dve.memset(VBLK, 0.0)
                    dve.memset(HID, 0.0)
                    dve.wait_ge(flag("gates_tanh"), 1)
                    step(dve.tensor_scalar(GATE, GATE, 0.5, 0.5, ALU.mult, ALU.add))
                    split_to(s["in"][-1].end + RING)
                    dve.wait_ge(flag("cmp_w1_done"), 1)
                    dve.tensor_copy(s_t[0:DH, 0:1], SCB[0][0:DH, 256:257])
                    step(dve.tensor_copy(s_t[0:DH, 1:2], SCB[1][0:DH, 257:258]))
                    for n in range(2):
                        ins = dve.tensor_scalar(HID[:, n, :, 0:N_CMP],
                                                SCB[n][0:DH, 64 * n:64 * n + 60].rearrange("p (g n) -> p g n", g=4),
                                                s_t[0:DH, n:n + 1], None, ALU.add)
                    ins.then_inc(flag("cmp_hidden"), 1)
                    dve.wait_ge(flag("cmp_tanh"), 1)
                    step(dve.scalar_tensor_tensor(out=HIT, in0=HIT, scalar=1.0, in1=HID, op0=ALU.add, op1=ALU.mult))
                    step(dve.tensor_scalar(HIT, HIT, 0.5, None, ALU.mult))
                    for j in range(4):
                        ins = dve.tensor_copy(HIV[:, :, j, :], HIT[:, 1, :, :])
                    ins.then_inc(flag("cmp_silu"), 1)
                    dve.wait_ge(flag("cmp_w2_done"), 1)
                    bank = SCB[1]
                    step(dve.tensor_copy(KCN[:, 0, :], bank[:, 0:DH]))
                    step(dve.tensor_tensor(KCN[:, 1, :], KCN[:, 0, :], KCN[:, 0, :], ALU.mult))
                    step(dve.tensor_reduce(s_mean[:, 0:1], KCN[:, 1, :], AX, ALU.add))
                    rsqrt(1, DH)
                    step(dve.tensor_scalar(KCN[:, 0, :], KCN[:, 0, :], s_y[:, 0:1], None, ALU.mult))
                    step(dve.tensor_tensor(KCN[:, 0, :], KCN[:, 0, :], gains[:, N_KC, :], ALU.mult))
                    step(dve.tensor_copy(KCN[:, 1, :], KCN[:, 0, :]))
                    for j in range(4):
                        r = slice(32 * j, 32 * j + 32)
                        ins = dve.tensor_copy(VBLK[r, :, j, :], bank[r, 128:384].rearrange("p (g d) -> p g d", g=4))
                    ins.then_inc(flag("cmp_kv_ready"), 1)
                    dve.wait_ge(turned, s["kcturn"] + 1)
                    dve.tensor_copy(KCT, TB[s["kcturn"] % 2][:, 0:P]).then_inc(turn_dve, 1)
                    for c in range(C):
                        dve.wait_ge(flag("cmp_scored"), c + 1)
                        cs4, cp4 = (b_.rearrange("p (h n) -> p h n", h=16) for b_ in (CS, CP))
                        bias = cmp_bias[:, c, :].unsqueeze(1).broadcast_to([P, 16, 32])
                        keep = cmp_keep[:, c, :].unsqueeze(1).broadcast_to([P, 16, 32])
                        for n in range(2):
                            ins = dve.tensor_scalar(CS.rearrange("p (b a m) -> p b a m", b=2, a=2)[:, :, n, :],
                                                    SCB[n][:, 0:T].rearrange("p (b m) -> p b m", b=2), DH ** -0.5, None, ALU.mult)
                        step(ins)
                        step(dve.tensor_tensor(cs4, cs4, bias, ALU.add))
                        step(dve.tensor_reduce(s_t[:, 0:16], cs4, AX, ALU.max))
                        dve.tensor_tensor(cs4, cs4, s_t[:, 0:16].unsqueeze(2).broadcast_to([P, 16, 32]), ALU.subtract
                                          ).then_inc(flag("cmp_shifted"), 1)
                        dve.wait_ge(flag("cmp_exp"), c + 1)
                        step(dve.tensor_tensor(cp4, cp4, keep, ALU.mult))
                        step(dve.tensor_reduce(s_t[:, 0:16], cp4, AX, ALU.add))
                        step(dve.tensor_scalar(s_t[:, 0:16], s_t[:, 0:16], TINY, None, ALU.max))
                        step(dve.reciprocal(s_u[:, 0:16], s_t[:, 0:16]))
                        gate = GATE[:, c, :].rearrange("p (h b) -> p h b", b=3)[:, :, 0]
                        step(dve.tensor_tensor(s_u[:, 0:16], s_u[:, 0:16], gate, ALU.mult))
                        dve.tensor_tensor(cp4, cp4, s_u[:, 0:16].unsqueeze(2).broadcast_to([P, 16, 32]), ALU.mult
                                          ).then_inc(flag("cmp_prob"), 1)
                        dve.wait_ge(turned, s["cmpturn"] + c + 1)
                        dve.tensor_copy(CPT, TB[(s["cmpturn"] + c) % 2][:, :]).then_inc(turn_dve, 1)
                        dve.wait_ge(flag("cmp_out"), c + 1)
                        dve.tensor_copy(Z1[:, c, 0:512], G[0][:, :])
                        step(dve.tensor_copy(Z1[:, c, 512:1024], G[1][:, :]))
                    dve.sem_inc(flag("cmp_added"), 1)
                    attention(items1(), *s["heads"])
                    to_t(s["oturn"], KC, 1.0, ahi, alo)
                product(s["out"][0:1], None)
                if l == 0:
                    mk = [heads(memk_rows[m], 0, 4, P) for m in range(2)]
                    head_norm([(heads(zv(4944 + 1024 * m, 512), 0, 4, P), mk[m], [(mk[m], mem_k_gain[:, m, :])])
                               for m in range(2)], P, "mk")
                    dve.sem_inc(flag("mem_k_normed"), 1)
                product(s["out"][1:2], None)
                norm(x, f"memq{l}")
                to_t(s["mturn"], KC, gain_of(G_MEM[l]), ahi, alo)
                product(s["mq"], lambda s_, c: ZM[:, c, :])
                vm = heads(ZM, 0, 4, P)
                head_norm([(heads(zv(2048, 512), 0, 4, P), vm, [(vm, mem_q_gain[:, l, :])])], P, f"memq{l}")
                dve.sem_inc(flag(f"mem_q_ready{l}"), 1)
                turns(s["mqturn"], 2, lambda b: feat[:, 512 * b:512 * b + 512])
                split_to(s["mo"][-1].end)
                attention(items_mem(l), *s["mheads"])
                to_t(s["moturn"], 4, 1.0, ahi, alo)
                product(s["mo"], None)
                norm(x, f"ffn{l}")
                to_t(s["fturn"], KC, gain_of(G_FFN[l]), ahi, alo)
                blocks(s["ff"])
                add_blocks(s["ff"], l)

            norm(x, "mix2")
            to_t(N["hturn"], KC, gain_of(G_N1), ahi, alo)
            lam = cols[:, 1, R_LAM:R_LAM + 8]
            l0, l1, l2, l3 = (LAM[:, i, :] for i in range(4))
            step(dve.tensor_scalar(l0, lam, -1.0, None, ALU.mult))
            dve.tensor_tensor(l1, l0, lam, ALU.min).then_inc(flag("minus_abs_lambda"), 1)
            dve.wait_ge(flag("exp_lambda"), 1)
            step(dve.tensor_scalar(l2, l1, 2.0, None, ALU.add))
            step(dve.reciprocal(l2, l2))
            step(dve.tensor_tensor(l1, l1, l2, ALU.mult))
            step(dve.tensor_tensor(l2, l1, l1, ALU.mult))
            step(dve.tensor_scalar(l3, l2, 1 / 17, 1 / 15, ALU.mult, ALU.add))
            for n in (13, 11, 9, 7, 5, 3, 1):
                step(dve.tensor_tensor(l3, l3, l2, ALU.mult))
                step(dve.tensor_scalar(l3, l3, 1 / n, None, ALU.add))
            step(dve.tensor_tensor(l3, l3, l1, ALU.mult))
            step(dve.tensor_scalar(l0, l0, 0.0, 0.5, ALU.max, ALU.mult))
            step(dve.tensor_tensor(l3, l3, l0, ALU.add))
            step(dve.tensor_scalar(SP4[:, 0:8], l3, 8.0, None, ALU.mult))
            for n, r in enumerate((R_BR, R_BI)):
                step(dve.tensor_scalar(HB[:, n, :], cols[:, 1, r:r + 8], 0.5, None, ALU.mult))
            product(N["in"], lambda s_, c: ZA[:, c, s_.c0:s_.c0 + s_.width])
            dve.sem_inc(flag("z_copied2"), 1)
            turns(N["uturn"], 10, lambda b: feat[:, 512 * b:512 * b + 512])
            split_to(N["in"][-1].end + RING)
            for k in range(8):
                wc = [cols[:, 1, 8 * n + k:8 * n + k + 1] for n in range(4)]
                step(dve.tensor_scalar(XC[:, k, :], ULT[:, k, :], wc[3], cols[:, 1, R_CB + k:R_CB + k + 1], ALU.mult, ALU.add))
                for n in (2, 1, 0):
                    back = 3 - n
                    ins = dve.scalar_tensor_tensor(out=XC[:, k, back:T], in0=ULT[:, k, 0:T - back], scalar=wc[n],
                                                   in1=XC[:, k, back:T], op0=ALU.mult, op1=ALU.add)
                    step(ins) if n else ins.then_inc(flag("convolved"), 1)
            product(N["gates"][0:2], lambda s_, c: ZG[:, c, s_.c0 - GA:s_.c0 - GA + 512])
            dve.wait_ge(turn_act, plan.turn_act[N["gturn"] + 8])
            for k in range(8):
                ins = dve.tensor_scalar(RG[:, k, :], RG[:, k, :], SP4[:, k:k + 1], SP4[:, k:k + 1], ALU.mult, ALU.add)
            ins.then_inc(flag("log_decay"), 1)
            dve.wait_ge(flag("convolved"), 8)
            step(dve.scalar_tensor_tensor(out=XC, in0=IG, scalar=1.0, in1=XC, op0=ALU.add, op1=ALU.mult))
            step(dve.tensor_tensor(IG, UGT, UGT, ALU.mult))
            step(dve.tensor_scalar(IG, IG, 0.044715, 1.0, ALU.mult, ALU.add))
            dve.tensor_tensor(IG, IG, UGT, ALU.mult).then_inc(flag("gelu_inner"), 1)
            product(N["gates"][2:4], lambda s_, c: ZG[:, c, s_.c0 - GA:s_.c0 - GA + 512])
            for g, w in enumerate(POOL_WINDOWS):
                p_, src, span = POOLT[:, g, :], UPT[:, g, :], 1
                tmp = [masked[0], masked[1]]
                cur = src
                while span < w:
                    nxt = tmp[0] if cur is not tmp[0] else tmp[1]
                    dve.tensor_copy(nxt[:, 0:span], cur[:, 0:span])
                    step(dve.tensor_tensor(nxt[:, span:T], cur[:, span:T], cur[:, 0:T - span], ALU.add))
                    cur, span = nxt, 2 * span
                dve.tensor_tensor(p_[:, 0:w - 1], cur[:, 0:w - 1], numbers[:, 0:w - 1], ALU.mult)
                step(dve.tensor_scalar(p_[:, w - 1:T], cur[:, w - 1:T], 1.0 / w, None, ALU.mult))
                ins = dve.tensor_tensor(p_, p_, src, ALU.subtract)
                step(ins) if g < 3 else ins.then_inc(flag("pooled"), 1)
            dve.wait_ge(flag("gelu_tanh"), 1)
            step(dve.scalar_tensor_tensor(out=UGT, in0=IG, scalar=1.0, in1=UGT, op0=ALU.add, op1=ALU.mult))
            dve.wait_ge(flag("decay_tanh"), 1)
            step(dve.tensor_tensor(IG, ULT, ULT, ALU.mult))
            dve.scalar_tensor_tensor(out=RG, in0=IG, scalar=1.0, in1=RG, op0=ALU.add, op1=ALU.mult).then_inc(flag("drive_squared"), 1)
            to_t(N["yturn"], 4, lambda k: cols[:, 1, R_PS + k:R_PS + k + 1], ahi, alo)
            dve.wait_ge(flag("drive_scale"), 1)
            step(dve.tensor_tensor(XC, XC, RG, ALU.mult))
            for k in range(8):
                ins = dve.tensor_tensor_scan(IG[:, k, :], ULT[:, k, :], XC[:, k, :], 0.0, ALU.mult, ALU.add)
            step(ins)
            dve.scalar_tensor_tensor(out=ULT, in0=IG, scalar=0.5, in1=UGT, op0=ALU.mult, op1=ALU.mult).then_inc(flag("lru_out"), 1)
            dve.wait_ge(flag("lru_hi"), 1)
            dve.tensor_tensor(blo[:, :, :], ULT, bhi[:, :, :].bitcast(F32), ALU.subtract).then_inc(flag("lru_done"), 1)
            dve.wait_ge(flag("mix_gates"), 1)

            def mix_a(s_, c):
                g_ = ZG[:, c, s_.c0:s_.c0 + 512]
                dve.scalar_tensor_tensor(out=g_, in0=g_, scalar=1.0, in1=bank_of(s_, c), op0=ALU.add, op1=ALU.mult
                                         ).then_inc(slab_dve, 1)

            def mix_b(s_, c):
                g_, y_ = ZG[:, c, D + s_.c0:D + s_.c0 + 512], ZG[:, c, s_.c0:s_.c0 + 512]
                step(dve.scalar_tensor_tensor(out=g_, in0=g_, scalar=1.0, in1=bank_of(s_, c), op0=ALU.add, op1=ALU.mult))
                dve.tensor_tensor(y_, y_, g_, ALU.add).then_inc(slab_dve, 1)

            product(N["pa"], mix_a)
            product(N["pb"], mix_b)
            to_t(N["oturn"], KC, 0.5, ahi, alo)
            product(N["out"], None)
            norm(x, "moe")
            to_t(N["h2turn"], KC, gain_of(G_N2), ahi, alo)

            dve.wait_ge(flag("router_hi"), 1)
            dve.tensor_tensor(rlo[:, :, :], route_w, rhi[:, :, :].bitcast(F32), ALU.subtract).then_inc(flag("router_lo"), 1)
            split_to(N["moe"].base + RING)
            dve.wait_ge(flag("routed"), 1)
            gl, el = rt[:, 0, :, 0:N_GRP], rt[:, 2, :, :]
            lg = SCB[1][:, 0:40].rearrange("p (c n) -> p c n", c=C)
            dve.tensor_tensor(gl, lg[:, :, 0:N_GRP], route_b[:, 0:N_GRP].unsqueeze(1).broadcast_to([P, C, N_GRP]), ALU.add)
            step(dve.tensor_tensor(el, lg[:, :, N_GRP:20], route_b[:, N_GRP:20].unsqueeze(1).broadcast_to([P, C, N_EXP]), ALU.add))
            iota = rt[:, 3, :, :]
            for e in range(N_EXP):
                ins = dve.memset(iota[:, :, e:e + 1], float(e - N_EXP))
            step(ins)

            def first_best(v, n, best, hot, t_):
                step(dve.tensor_reduce(best, v, AX, ALU.max))
                step(dve.tensor_tensor(t_, v, best.broadcast_to([P, C, n]), ALU.is_equal))
                step(dve.tensor_tensor(t_, t_, iota[:, :, 0:n], ALU.mult))
                step(dve.tensor_reduce(rt[:, 11, :, 0:1], t_, AX, ALU.min))
                step(dve.tensor_tensor(hot, iota[:, :, 0:n], rt[:, 11, :, 0:1].broadcast_to([P, C, n]), ALU.is_equal))

            gbest, ghot = rt[:, 4, :, 0:1], rt[:, 5, :, 0:N_GRP]
            first_best(gl, N_GRP, gbest, ghot, rt[:, 10, :, 0:N_GRP])
            dve.tensor_tensor(gl, gl, gbest.broadcast_to([P, C, N_GRP]), ALU.subtract).then_inc(flag("group_shifted"), 1)
            dve.wait_ge(flag("group_exp"), 1)
            step(dve.tensor_reduce(rt[:, 4, :, 1:2], rt[:, 1, :, 0:N_GRP], AX, ALU.add))
            p_top = rt[:, 4, :, 2:3]
            step(dve.reciprocal(p_top, rt[:, 4, :, 1:2]))
            g16 = rt[:, 6, :, :]
            for g in range(N_GRP):
                ins = dve.tensor_copy(g16[:, :, PER_GRP * g:PER_GRP * g + PER_GRP], ghot[:, :, g:g + 1].broadcast_to([P, C, PER_GRP]))
            step(ins)
            step(dve.tensor_tensor(el, el, g16, ALU.mult))
            step(dve.tensor_scalar(g16, g16, -NEG, NEG, ALU.mult, ALU.add))
            step(dve.tensor_tensor(el, el, g16, ALU.add))
            best1, hot1, best2, hot2 = rt[:, 4, :, 3:4], rt[:, 7, :, :], rt[:, 4, :, 4:5], rt[:, 6, :, :]
            first_best(el, N_EXP, best1, hot1, rt[:, 10, :, :])
            step(dve.tensor_scalar(hot2, hot1, 3 * NEG, None, ALU.mult))
            step(dve.tensor_tensor(el, el, hot2, ALU.add))
            first_best(el, N_EXP, best2, hot2, rt[:, 10, :, :])
            dve.tensor_tensor(rt[:, 8, :, 0:1], best2, best1, ALU.subtract).then_inc(flag("expert_gap"), 1)
            dve.wait_ge(flag("expert_exp"), 1)
            e_, w1, w2_ = rt[:, 9, :, 0:1], rt[:, 9, :, 1:2], rt[:, 9, :, 2:3]
            step(dve.tensor_scalar(w1, e_, 1.0, None, ALU.add))
            step(dve.reciprocal(w1, w1))
            step(dve.tensor_tensor(w1, w1, p_top, ALU.mult))
            step(dve.tensor_tensor(w2_, w1, e_, ALU.mult))
            step(dve.tensor_tensor(hot1, hot1, w1.broadcast_to([P, C, N_EXP]), ALU.mult))
            step(dve.tensor_tensor(hot2, hot2, w2_.broadcast_to([P, C, N_EXP]), ALU.mult))
            step(dve.tensor_tensor(hot1, hot1, hot2, ALU.add))
            for n in range(2):
                ins = dve.tensor_scalar(half_comb.rearrange("p c (e n) -> p c e n", n=2)[:, :, :, n], hot1, 0.5, None, ALU.mult)
            step(ins)
            blocks(N["moe"])
            add_blocks(N["moe"], 2)
            norm(x, "final")
            dve.wait_ge(flag("normed_final"), 1)
            dve.wait_ge(flag("final_gain_in"), 16)
            for c in range(C):
                dve.tensor_tensor(XN[:, c, :], XN[:, c, :], final_gain, ALU.mult).then_inc(flag("out_ready"), 1)

        @block.tensor
        def _(pe):
            def mm3(dst, lhi, llo, rhi_, rlo_, start, stop):
                pe.matmul(dst, lhi, rhi_, start=start, stop=False)
                pe.matmul(dst, lhi, rlo_, start=False, stop=False)
                return pe.matmul(dst, llo, rhi_, start=False, stop=stop)

            def unit_ready(u):
                pe.wait_ge(lo_dve, u + 1)
                pe.wait_ge(lo_pool, u + 1)

            def product(slabs, lhi, llo, between=None):
                for s in slabs:
                    if s.index >= 2:
                        before = plan.slabs[s.index - 2]
                        pe.wait_ge(slab_act, before.done_act)
                        pe.wait_ge(slab_dve, before.done_dve)
                    for i in range(s.units):
                        u, nk = s.unit + i, min(4, s.k)
                        unit_ready(u)
                        wh, wl = (w[u % RING][:, 0:nk * s.width].rearrange("p (k n) -> p k n", k=nk) for w in (whi, wlo))
                        for c in range(C):
                            if between:
                                between()
                            for k in range(nk):
                                kk = 4 * i + k
                                ins = mm3(bank_of(s, c), lhi[:, kk, P * c:P * c + P], llo[:, kk, P * c:P * c + P],
                                          wh[:, k, :], wl[:, k, :], kk == 0, kk == s.k - 1)
                        ins.then_inc(unit_used, 1)

            def turn_free(n):
                if n >= 2:
                    if plan.turn_act[n - 1]:
                        pe.wait_ge(turn_act, plan.turn_act[n - 1])
                    if plan.turn_dve[n - 1]:
                        pe.wait_ge(turn_dve, plan.turn_dve[n - 1])
                return TB[n % 2]

            def emptied(n):
                pe.wait_ge(turn_act, plan.turn_act[n]) if plan.turn_act[n] else None
                pe.wait_ge(turn_dve, plan.turn_dve[n]) if plan.turn_dve[n] else None

            def to_t(base, nk, src):
                for b in range(nk // 2):
                    bank = turn_free(base + b)
                    for n in range(2):
                        for c in range(C):
                            ins = pe.transpose(bank[:, T * n + P * c:T * n + P * c + P], src(c, 2 * b + n), ident[:, :])
                    ins.then_inc(turned, 1)
                emptied(base + nk // 2)

            def turns(base, jobs):
                for b in range(len(jobs) // 2):
                    bank = turn_free(base + b)
                    for n in range(2):
                        for c in range(C):
                            ins = pe.transpose(bank[:, T * n + P * c:T * n + P * c + P], jobs[2 * b + n](c), ident[:, :])
                    ins.then_inc(turned, 1)
                emptied(base + len(jobs) // 2)

            def attention(items, first, outs, batch):
                n = len(items)
                for t in range(n + 3):
                    if t < n:
                        it, g = items[t], first + t
                        if g >= 2:
                            pe.wait_ge(item_masked, g - 1)
                        pe.matmul(SCB[g % 2][:, 0:it.nk], it.q, it.k, start=True, stop=True).then_inc(scored, 1)
                    if 0 <= t - 2 < n:
                        i = t - 2
                        g = first + i
                        pe.wait_ge(exped, g + 1)
                        bank = turn_free(batch + i)
                        for b in range(items[i].nk // P):
                            ins = pe.transpose(bank[:, P * b:P * b + P], prob[g % 3][:, P * b:P * b + P], ident[:, :])
                        ins.then_inc(turned, 1)
                    if 0 <= t - 3 < n:
                        i = t - 3
                        it = items[i]
                        pe.wait_ge(turn_dve, plan.turn_dve[batch + i + 1])
                        if i >= 2:
                            pe.wait_ge(item_out, outs + i - 1)
                        nb = it.nk // P
                        for b in range(nb):
                            ins = pe.matmul(G[i % 2][:, 0:it.dv], probt[i % 2][:, P * b:P * b + P], it.v[b],
                                            start=b == 0, stop=b == nb - 1)
                        ins.then_inc(pved, 1)
                pe.wait_ge(item_out, outs + n)

            def ff_up(b, j, static=True):
                u0 = b.base + 3 * j - (0 if isinstance(j, int) and j == 0 else 1)
                s0 = b.base % RING if isinstance(j, int) and j == 0 else (b.base - 1) % RING
                if not static or b.start + j >= 1:
                    pe.wait_ge(ff_silu, b.start + j)
                for half_ in range(2):
                    unit_ready(u0 + half_)
                    slot = (s0 + half_) % RING
                    for c in range(C):
                        for k in range(4):
                            kk = 4 * half_ + k
                            ins = mm3(TB[c][:, :], ahi[:, kk, P * c:P * c + P], alo[:, kk, P * c:P * c + P],
                                      whi[slot][:, 512 * k:512 * k + 512], wlo[slot][:, 512 * k:512 * k + 512],
                                      kk == 0, kk == KC - 1)
                    ins.then_inc(unit_used, 1)

            def ff_turn(b, j, static=True):
                n = b.start + j
                pe.wait_ge(ff_silu, n + 1)
                if not static or n >= 1:
                    pe.wait_ge(ff_lo, n)
                for f in range(2):
                    for c in range(C):
                        ins = pe.transpose(SCB[0][:, T * f + P * c:T * f + P * c + P], silu[:, c, 1, P * f:P * f + P], ident[:, :])
                ins.then_inc(ff_turned, 1)

            def ff_down(b, j, slot, first=False, last=False, u=None):
                pe.wait_ge(ff_lo, b.start + j + 1)
                unit_ready(u)
                for c in range(C):
                    for f in range(2):
                        for n in range(2):
                            w = slice(D * f + 512 * n, D * f + 512 * n + 512)
                            ins = mm3(G[2 * c + n][:, :], bhi[:, f, P * c:P * c + P], blo[:, f, P * c:P * c + P],
                                      whi[slot][:, w], wlo[slot][:, w], first and f == 0, last and f == 1)
                ins.then_inc(unit_used, 1)

            def blocks(b):
                s = (b.base + 1) % RING
                ff_up(b, 0)
                ff_turn(b, 0)
                ff_up(b, 1)
                ff_down(b, 0, s, first=True, u=b.base + 4)
                first, last, per = loop_turns(b)
                with pe.Fori(first, last) as i:
                    for n in range(per):
                        j = i * per + n
                        ff_turn(b, j - 1, False)
                        ff_up(b, j, False)
                        ff_down(b, j - 1, s, u=b.base + 3 * j + 1)
                for j in range(b.last, b.n):
                    ff_turn(b, j - 1)
                    ff_up(b, j)
                    ff_down(b, j - 1, s, u=b.base + 3 * j + 1)
                ff_turn(b, b.n - 1)
                ff_down(b, b.n - 1, (b.base + 3 * b.n - 1) % RING, last=True, u=b.base + 3 * b.n - 1)

            pe.wait_ge(flag("masks_ready"), 1)
            pe.wait_ge(flag("positions_float"), 1)
            pe.wait_ge(flag("rows_in"), 16 * 16)
            pe.transpose(SCB[0][:, 0:C], pos_r[:, :], ident[0:C, 0:C])
            pe.transpose(SCB[0][:, 128:208], rows[:, 0, :], ident[0:80, 0:80])
            pe.transpose(SCB[0][:, 256:324], rows[0:68, 1, :], ident[0:68, 0:68]).then_inc(flag("positions_turned"), 1)

            for l in range(2):
                s = L[l]
                pe.wait_ge(flag(f"normed_mix{l}"), 1)
                to_t(s["hturn"], KC, xsrc)
                product(s["in"], ahi, alo)
                if l == 0:
                    pe.wait_ge(flag("normed_mem"), 1)
                    to_t(mem_turn, KC, lambda c, k: MEMIN[:, c, P * k:P * k + P])
                    pe.wait_ge(flag("qk_ready0"), 1)
                    turns(s["qturn"], JOBS0)
                    index_item = [0]

                    def two_logits():
                        for i in range(index_item[0], index_item[0] + 2):
                            c, h, g = i // 8, i % 8, s["index"] + i
                            r = slice(32 * (h % 4), 32 * (h % 4) + 32)
                            if i >= 2:
                                pe.wait_ge(exped, g - 1)
                            pe.matmul(SCB[g % 2][:, 0:P * (c + 1)], feat[r, T * (h // 4) + P * c:T * (h // 4) + P * c + P],
                                      feat[r, 512:512 + P * (c + 1)], start=True, stop=True,
                                      tile_position=(32 * (h % 4), 0)).then_inc(scored, 1)
                        index_item[0] += 2

                    product(M[0]["kv"], bhi, blo, two_logits)
                    product(M[1]["kv"], ahi, alo)
                    attention(items0(), *s["heads"])
                    to_t(s["oturn"], KC, osrc0)
                else:
                    pe.wait_ge(flag("q_plain1"), 1)
                    turns(s["qturn"], JOBSQ)
                    pe.wait_ge(flag("qk_ready1"), 1)
                    turns(s["qrturn"], JOBSR)
                    bank = turn_free(s["posturn"])
                    pe.transpose(bank[:, 0:CMP_LEN], pos_rows[:, :], ident[0:CMP_LEN, 0:CMP_LEN]).then_inc(turned, 1)
                    emptied(s["posturn"] + 1)
                    pe.wait_ge(flag("cmp_weights_in"), 32)
                    for n in range(2):
                        r = slice(DH * n, DH * n + DH)
                        for j in range(CMP_LEN):
                            pe.matmul(SCB[n][0:DH, 64 * n:64 * n + 60].rearrange("p (g n) -> p g n", g=4), CMPW[r, j, :],
                                      KCVT[r, :, j:j + CMP_STRIDE * (N_CMP - 1) + 1:CMP_STRIDE], start=j == 0, stop=j == CMP_LEN - 1)
                    for n in range(2):
                        r = slice(DH * n, DH * n + DH)
                        for j in range(CMP_LEN):
                            ins = pe.matmul(SCB[n][0:DH, 256 + n:257 + n], CMPW[r, j, :], POST[r, j:j + 1],
                                            start=j == 0, stop=j == CMP_LEN - 1)
                    ins.then_inc(flag("cmp_w1_done"), 1)
                    pe.wait_ge(flag("cmp_silu"), 1)
                    pe.matmul(SCB[1][:, 0:DH], HIT[:, 0, :, :].rearrange("p g n -> p (g n)"), w2[:, 0, :], start=True, stop=True)
                    for g in range(4):
                        ins = pe.matmul(SCB[1][:, 128 + DH * g:128 + DH * g + DH],
                                        HIV[:, g, :, :].rearrange("p j n -> p (j n)"), w2[:, 1, :], start=True, stop=True)
                    ins.then_inc(flag("cmp_w2_done"), 1)
                    pe.wait_ge(flag("cmp_kv_ready"), 1)
                    bank = turn_free(s["kcturn"])
                    pe.transpose(bank[:, 0:P], KCN.rearrange("p a d -> p (a d)"), ident[:, :]).then_inc(turned, 1)
                    emptied(s["kcturn"] + 1)
                    for c in range(C):
                        if c:
                            pe.wait_ge(flag("cmp_shifted"), c)
                        for h in range(16):
                            (jq, half_), g = place1(h), h // 4
                            r = slice(DH * half_, DH * half_ + DH)
                            at_ = P * (g // 2) + 32 * (h % 4)
                            ins = pe.matmul(SCB[half_][:, at_:at_ + 32], feat[r, T * jq + P * c:T * jq + P * c + P],
                                            KCT[r, 32 * g:32 * g + 32], start=True, stop=True)
                        ins.then_inc(flag("cmp_scored"), 1)
                        pe.wait_ge(flag("cmp_prob"), c + 1)
                        bank = turn_free(s["cmpturn"] + c)
                        for g in range(4):
                            ins = pe.transpose(bank[:, P * g:P * g + P], CP[:, P * g:P * g + P], ident[:, :])
                        ins.then_inc(turned, 1)
                        emptied(s["cmpturn"] + c + 1)
                        for g in range(4):
                            ins = pe.matmul(G[g // 2][:, T * (g % 2):T * (g % 2) + T], CPT[:, P * g:P * g + P],
                                            VBLK[:, g, :, :].rearrange("p j d -> p (j d)"), start=True, stop=True)
                        ins.then_inc(flag("cmp_out"), 1)
                    pe.wait_ge(flag("cmp_added"), 1)
                    attention(items1(), *s["heads"])
                    to_t(s["oturn"], KC, osrc1)
                product(s["out"], ahi, alo)
                pe.wait_ge(flag(f"normed_memq{l}"), 1)
                to_t(s["mturn"], KC, xsrc)
                product(s["mq"], ahi, alo)
                if l == 0:
                    pe.wait_ge(flag("mem_k_normed"), 1)
                    for m in range(2):
                        turns(M[m]["kturn"], [lambda c, h=h: memk_rows[m][:, c, P * h:P * h + P] for h in range(4)])
                pe.wait_ge(flag(f"mem_q_ready{l}"), 1)
                turns(s["mqturn"], JOBSM)
                attention(items_mem(l), *s["mheads"])
                to_t(s["moturn"], 4, msrc)
                product(s["mo"], ahi, alo)
                pe.wait_ge(flag(f"normed_ffn{l}"), 1)
                to_t(s["fturn"], KC, xsrc)
                blocks(s["ff"])

            pe.wait_ge(flag("normed_mix2"), 1)
            to_t(N["hturn"], KC, xsrc)
            product(N["in"], ahi, alo)
            pe.wait_ge(flag("z_copied2"), 1)
            pe.wait_ge(slab_act, N["in"][-1].done_act)
            turns(N["uturn"], [lambda c, k=k: ZA[:, c, P * k:P * k + P] for k in [4, 5, 6, 7, 8, 9, 10, 11, 0, 1, 2, 3] + list(range(12, 20))])
            product(N["gates"][0:2], ahi, alo)
            pe.wait_ge(flag("gate_weights_in"), 80)
            for k in range(8):
                pe.wait_ge(flag("convolved"), k + 1)
                bank = turn_free(N["gturn"] + k)
                for n in range(2):
                    ins = pe.matmul(bank[:, T * n:T * n + T], GATEW[:, n, k, :], XC[:, k, :], start=True, stop=True)
                ins.then_inc(turned, 1)
            product(N["gates"][2:4], ahi, alo)
            pe.wait_ge(flag("pooled"), 1)
            for b in range(2):
                bank = turn_free(N["yturn"] + b)
                for n in range(2):
                    ins = pe.matmul(bank[:, T * n:T * n + T], POOLW[:, 2 * b + n, :], POOLT[:, 2 * b + n, :], start=True, stop=True)
                ins.then_inc(turned, 1)
            emptied(N["yturn"] + 2)
            product(N["pa"], ahi, alo)
            pe.wait_ge(flag("lru_done"), 1)
            product(N["pb"], bhi, blo)
            pe.wait_ge(slab_dve, N["pb"][-1].done_dve)
            to_t(N["oturn"], KC, ysrc)
            product(N["out"], ahi, alo)
            pe.wait_ge(flag("normed_moe"), 1)
            to_t(N["h2turn"], KC, xsrc)
            pe.wait_ge(flag("router_lo"), 1)
            for c in range(C):
                for k in range(KC):
                    ins = mm3(SCB[1][:, 20 * c:20 * c + 20], ahi[:, k, P * c:P * c + P], alo[:, k, P * c:P * c + P],
                              rhi[:, k, :], rlo[:, k, :], k == 0, k == KC - 1)
            ins.then_inc(flag("routed"), 1)
            blocks(N["moe"])


_INS = ["x", "mem", "positions", "norm_mix", "norm_mem", "norm_mem_src", "norm_ffn", "ab_w_in", "ab_w_out",
        "dsa_q_norm", "dsa_k_norm", "moba_q_norm", "moba_k_norm", "nsa_w_in", "nsa_w_out", "nsa_q_norm",
        "nsa_kcmp_norm", "nsa_ksel_norm", "nsa_kwin_norm", "nsa_cmp_pos_k", "nsa_cmp_pos_v", "nsa_cmp_w1_k",
        "nsa_cmp_w2_k", "nsa_cmp_w1_v", "nsa_cmp_w2_v", "mem_w_q", "mem_w_kv", "mem_w_o", "mem_q_norm",
        "mem_k_norm", "ffn_w_in", "ffn_w_out", "norm1_g_2", "w_in_2", "pool_w_2", "pool_scale_2", "conv_w_2",
        "conv_b_2", "rg_w_r_2", "rg_b_r_2", "rg_w_i_2", "rg_b_i_2", "rg_lambda_2", "proj_a_2", "proj_b_2",
        "w_out_2", "norm2_g_2", "router_group_w_2", "router_group_b_2", "router_expert_w_2",
        "router_expert_b_2", "exp_w_gate_2", "exp_w_up_2", "exp_w_down_2", "norm_f_g_2"]


def kernel(**inputs):
    import concourse.bacc as bacc
    from concourse.bass_utils import run_bass_kernel_spmd

    nc = bacc.Bacc("TRN2", target_bir_lowering=False, num_devices=1)
    arrays, aps = {}, {}
    for name in _INS:
        v = np.ascontiguousarray(inputs[name])
        arrays[f"in_{name}"] = v
        aps[name] = nc.dram_tensor(f"in_{name}", v.shape, mybir.dt.from_np(v.dtype), kind="ExternalInput").ap()
    out = nc.dram_tensor("out_0", (1, T, D), F32, kind="ExternalOutput").ap()
    build(nc, aps, out)
    r = run_bass_kernel_spmd(nc, [arrays], core_ids=[0])
    return r.results[0]["out_0"]
```

```python
from contextlib import ExitStack
import math
import numpy as np
import concourse.bass as bass
from concourse import mybir

F32 = mybir.dt.float32
F32R = mybir.dt.float32r
I32 = mybir.dt.int32
ALU = mybir.AluOpType
ACT = mybir.ActivationFunctionType
AX = mybir.AxisListType.X

P = 128
T = 256
C = T // P
D = 1024
KC = D // P
DH = 64
FF = 2816
FB = 256
RING = 3
UNIT = 2048
LO_DVE = 768
EPS = 1e-6
NEG = -1e30
TAKEN = -3e38
TINY = 1e-20
ROPE_THETA = 500000.0
HALF = 8
N_CMP = 15
CMP_LEN, CMP_STRIDE = 32, 16
N_EXP, N_GRP, PER_GRP = 16, 4, 4
TOPK = 64
POOL_WINDOWS = (2, 4, 8, 16)

AQ, AK, AV, IQ, IK, IW, BQ, BK, BV, AB_W = 0, 512, 576, 640, 896, 928, 936, 1448, 1960, 2472
NQ, KCMP, VCMP, KSEL, VSEL, KWIN, VWIN, GT, C_W = 0, 1024, 1280, 1536, 1792, 2048, 2304, 2560, 2608
UL, UP, UG, GA, GB, IN_W = 512, 0, 1536, 2560, 3584, 4608

G_MIX, G_MEM, G_SRC, G_FFN, G_N1, G_N2 = (0, 1), (2, 3), (4, 5), (6, 7), 8, 9
R_CONV, R_CB, R_BR, R_BI, R_LAM, R_PS = 0, 32, 40, 48, 56, 64
N_AQ, N_AK, N_BQ, N_BK, N_NQ, N_KC, N_KS, N_KW = range(8)


class Chain:

    def __init__(self, eng, sem):
        self.eng, self.sem, self.n, self.turn = eng, sem, 0, 0

    def __call__(self, ins):
        self.n += 1
        ins.then_inc(self.sem, 1)
        self.eng.wait_ge(self.sem, self.n + self.turn)


class Slab:

    def __init__(self, w, c0, width, k, evac, unit, index, done_act, done_dve):
        self.w, self.c0, self.width, self.k, self.evac = w, c0, width, k, evac
        self.unit, self.units, self.index = unit, -(-k // 4), index
        self.end = unit + self.units
        self.done_act, self.done_dve = done_act, done_dve


class Plan:

    def __init__(self):
        self.slabs, self.loads, self.width, self.dmas = [], [], [], []
        self.act = self.dve = 0
        self.turns, self.turn_act, self.turn_dve = 0, [0], [0]
        self.turn_in_scores = set()
        self.items = self.outs = self.emptied = 0

    def product(self, w, width, k=KC, evac="both", first=0):
        out = []
        for c0 in range(first, first + width, 512):
            n = min(512, first + width - c0)
            self.act += evac == "both"
            self.dve += 1 if evac == "both" else 2
            s = Slab(w, c0, n, k, evac, len(self.width), len(self.slabs), self.act, self.dve)
            self.slabs.append(s)
            self.loads.append(s)
            self.width += [min(4, k) * n] * s.units
            self.dmas += [1] * s.units
            out.append(s)
        return out

    def blocks(self, n, per, dmas, load):
        b = Blocks(n, per, len(self.width), load, dmas)
        self.loads.append(b)
        self.width += [UNIT] * (3 * n)
        self.dmas += [dmas, dmas] + [dmas, dmas, 1] * (n - 1) + [1]
        return b

    def turn(self, n, act, dve):
        base = self.turns
        for _ in range(n):
            self.turn_act.append(self.turn_act[-1] + act)
            self.turn_dve.append(self.turn_dve[-1] + dve)
        self.turns += n
        return base

    def item(self, n):
        self.items += n
        return self.items - n

    def attention(self, n, per, tiles):
        run = Run(n, per, self.item(n), self.outs, self.turn(n, 0, 1), self.emptied, tiles)
        self.outs += n
        self.emptied += n // per
        return run

    def landed(self, u):
        return 16 * sum(self.dmas[v] for v in range(u % RING, u + 1, RING))


class Blocks:

    def __init__(self, n, per, base, load, dmas):
        self.n, self.per, self.base, self.load, self.dmas = n, per, base, load, dmas
        self.first, self.last = 2, n - per if (n - 2) % per == 0 and per > 1 else n - 1


class Run:

    def __init__(self, n, per, first, outs, batch, banks, tiles):
        self.prob, self.masked, self.probt = tiles
        self.n, self.per, self.first, self.outs, self.batch, self.banks = n, per, first, outs, batch, banks


class Branch:

    def __init__(self, q, k, nk, bias, v, out):
        self.q, self.k, self.nk, self.bias, self.v, self.out = q, k, nk, bias, v, out


class Item:

    def __init__(self, branches, scale, weight=None, first=None):
        self.branches, self.scale, self.weight, self.first = branches, scale, weight, first
        self.at = (0, branches[0].nk)
        self.width = branches[0].nk + branches[1].nk


def build(nc, a, out):
    ctx = ExitStack()
    with ctx:
        def sb(name, shape, dt=F32):
            return ctx.enter_context(nc.sbuf_tensor("t_" + name, shape, dt))

        def sem(name):
            return ctx.enter_context(nc.semaphore(name))

        flags = {}

        def flag(name):
            if name not in flags:
                flags[name] = sem(name)
            return flags[name]

        raw = [sb(f"raw{i}", [P, UNIT]) for i in range(RING)]
        whi = [sb(f"whi{i}", [P, UNIT], F32R) for i in range(RING)]
        wlo = [sb(f"wlo{i}", [P, UNIT], F32R) for i in range(RING)]
        x = sb("x", [P, C, D])
        ahi, alo = sb("ahi", [P, KC, T], F32R), sb("alo", [P, KC, T], F32R)
        bhi, blo = sb("bhi", [P, KC, T], F32R), sb("blo", [P, KC, T], F32R)
        z = sb("z", [P, 9216])
        feat = sb("feat", [P, 5120])
        memo = sb("memo", [P, 4096])
        rows = feat[0:80, 2560:2816].rearrange("r (a n) -> r a n", a=2)
        mem_k_gain = z[:, 8656:8912].rearrange("p (l n) -> p l n", l=2)
        final_gain = feat[:, 0:D]
        cols = sb("cols", [P, 2, 80])
        ident = sb("ident", [P, P])
        causal = sb("causal", [P, C, T])
        zero = sb("zero", [P, T])
        cmp_bias, cmp_keep = sb("cmp_bias", [P, C, 32]), sb("cmp_keep", [P, C, 32])
        shared = sb("shared", [P, 2600])
        dsa_bias = shared[:, 0:512].rearrange("p (c t) -> p c t", c=C)
        relu_out = [shared[:, 1024 + T * i:1024 + T * (i + 1)] for i in range(3)]
        pool_sum = [shared[:, 512 + T * i:512 + T * (i + 1)] for i in range(2)]

        def tiles(buffer, first, n):
            return [buffer[:, first + 512 * i:first + 512 * i + 512] for i in range(n)]

        TILES = (tiles(z, 4944, 4), tiles(z, 6992, 2), tiles(feat, 4096, 2))
        TILES1 = (tiles(feat, 0, 4), tiles(z, 5728, 2), tiles(shared, 512, 2))
        best8 = shared[:, 2336:2344]
        item_min, item_sum, item_inv = (sb(n, [P, 64]) for n in ("item_min", "item_sum", "item_inv"))
        s_mean, s_y, s_t, s_u = (sb(n, [P, 64]) for n in ("s_mean", "s_y", "s_t", "s_u"))
        row_scale, half_scale, half_scale2 = (sb(n, [P, C]) for n in ("row_scale", "half_scale", "half_scale2"))
        s_bits = sb("s_bits", [P, 64], I32)
        cosine, sine = sb("cosine", [P, C, HALF]), sb("sine", [P, C, HALF])
        pos_i, pos_r, pos_f = sb("pos_i", [C, P], I32), sb("pos_r", [C, P]), sb("pos_f", [P, C])
        angle = sb("angle", [P, 4, C, HALF])
        gains = sb("gains", [P, 8, DH])
        mem_q_gain = sb("mem_q_gain", [P, 2, P])
        silu = shared[:, 0:1024].rearrange("p (c a f) -> p c a f", c=C, a=2)
        route_w = shared[:, 1024:1184].rearrange("p (k n) -> p k n", k=KC)
        rt = shared[:, 1184:1568].rearrange("p (a c n) -> p a c n", a=12, c=C)
        half_comb = shared[:, 1568:1632].rearrange("p (c n) -> p c n", c=C)
        route_b = shared[:, 1632:1652]
        rhi, rlo = sb("rhi", [P, KC, 20], F32R), sb("rlo", [P, KC, 20], F32R)
        w2 = shared[0:DH, 2344:2472].rearrange("p (a e) -> p a e", a=2)
        pos_rows = shared[0:CMP_LEN, 2472:2600]
        numbers, half, sumsq = sb("numbers", [P, 16]), sb("half", [P, 1]), sb("sumsq", [P, 2])

        psum = [ctx.enter_context(nc.psum_tensor(f"bank{i}", [P, 512], F32)) for i in range(8)]
        G, TB, SCB = psum[0:4], psum[4:6], psum[6:8]
        memk = [memo[:, 2048 * i:2048 * i + 1024].rearrange("p (h t) -> p h t", h=4) for i in range(2)]
        memk_rows = [memo[:, 2048 * i:2048 * i + 1024].rearrange("p (c n) -> p c n", c=C) for i in range(2)]
        memv = [memo[:, 2048 * i + 1024:2048 * i + 2048].rearrange("p (c n) -> p c n", c=C) for i in range(2)]

        def zv(off, width):
            return z[:, off:off + C * width].rearrange("p (c n) -> p c n", c=C)

        def heads(view, first, n, d):
            return view[:, :, first:first + n * d].rearrange("p c (h d) -> p c h d", d=d)

        raw_loaded = [sem(f"raw_loaded{i}") for i in range(RING)]
        hi_done, lo_dve, lo_pool, unit_used = (sem(n) for n in ("hi_done", "lo_dve_done", "lo_pool_done", "unit_used"))
        slab_act, slab_dve = sem("slab_emptied_act"), sem("slab_emptied_dve")
        turned, turn_act, turn_dve = sem("turned"), sem("turn_emptied_act"), sem("turn_emptied_dve")
        scored, item_masked, exped = sem("scored"), sem("item_masked"), sem("exped")
        item_weighed, prob_scaled, pved = sem("item_weighed"), sem("prob_scaled"), sem("pved")
        heads_hi, heads_lo = sem("heads_hi"), sem("heads_lo")
        dve_step, act_step, pool_step = sem("dve_step"), sem("act_step"), sem("pool_step")
        ff_tanh, ff_silu, ff_turned, ff_hi, ff_lo = (sem(n) for n in ("ff_tanh", "ff_silu", "ff_turned", "ff_hi", "ff_lo"))

        plan = Plan()
        L = [{}, {}]
        M = [{}, {}]
        for l in range(2):
            s = L[l]
            s["hturn"] = plan.turn(4, 1, 1)
            if l == 0:
                s["in"] = plan.product(a["ab_w_in"][0], AB_W)
            else:
                w = a["nsa_w_in"][0]
                s["cmp"], s["gt"] = plan.product(w, 512, first=KCMP), plan.product(w, C_W - GT, first=GT)
                s["q0"], s["q1"] = plan.product(w, 512), plan.product(w, 512, first=512)
                s["sel"], s["win"] = plan.product(w, 512, first=KSEL), plan.product(w, 512, first=KWIN)
            if l == 0:
                mem_turn = plan.turn(4, 1, 1)
                s["qturn"] = plan.turn(8, 0, 1)
                s["index"] = plan.item(16)
                for m in range(2):
                    M[m]["kv"] = plan.product(a["mem_w_kv"][m], 1024)
                s["heads"] = plan.attention(16, 4, TILES)
            else:
                s["cmpkvturn"] = plan.turn(2, 0, 1)
                s["posturn"] = plan.turn(1, 0, 1)
                s["q0turn"], s["q1turn"] = plan.turn(2, 0, 1), plan.turn(2, 0, 1)
                s["kcturn"] = plan.turn(1, 0, 1)
                s["qrturn"] = plan.turn(6, 0, 1)
                s["cmpturn"] = plan.turn(2, 0, 1)
                s["heads"] = plan.attention(32, 8, TILES1)
            s["out"] = plan.product(a["ab_w_out" if l == 0 else "nsa_w_out"][0], D, evac="dve")
            s["mturn"] = plan.turn(4, 1, 1)
            s["mq"] = plan.product(a["mem_w_q"][l], 512)
            if l == 0:
                for m in range(2):
                    M[m]["kturn"] = plan.turn(2, 1, 0)
            s["mqturn"] = plan.turn(2, 0, 1)
            s["mheads"] = plan.attention(4, 2, TILES)
            s["mo"] = plan.product(a["mem_w_o"][l], D, k=4, evac="dve")
            s["fturn"] = plan.turn(4, 1, 1)
            plan.turn_in_scores |= {s["fturn"] + 2, s["fturn"] + 3}
            s["ff"] = plan.blocks(FF // FB, 1, 2, ("ffn", l))
            s["ff"].start = sum(b["ff"].n for b in L[:l])
        N = {}
        N["hturn"] = plan.turn(4, 1, 1)
        N["in"] = plan.product(a["w_in_2"][0], 1536) + plan.product(a["w_in_2"][0], 1024, first=UG)
        N["gates"] = plan.product(a["w_in_2"][0], 2048, first=GA)
        N["uturn"] = plan.turn(10, 0, 1)
        N["gturn"] = plan.turn(8, 1, 0)
        N["yturn"] = plan.turn(2, 1, 1)
        N["pa"] = plan.product(a["proj_a_2"][0], D, k=4, evac="dve")
        N["pb"] = plan.product(a["proj_b_2"][0], D, evac="dve")
        N["oturn"] = plan.turn(4, 1, 1)
        N["out"] = plan.product(a["w_out_2"][0], D, evac="dve")
        N["h2turn"] = plan.turn(4, 1, 1)
        N["moe"] = plan.blocks(N_EXP * 2, 2, 2, ("moe", 0))
        N["moe"].start = 2 * (FF // FB)
        n_units = len(plan.width)

        XN = zv(0, D)
        SQA, SQQ, SQK = (z[:, a_:a_ + C * n * DH].rearrange("p (c h d) -> p c h d", c=C, d=DH)
                         for a_, n in ((4944, 9), (6096, 8), (7120, 8)))
        ROPET = feat[:, 4096:4672]
        COPIES = z[:, 8144:8656].rearrange("p (c n) -> p c n", c=C)
        MEMIN = feat[:, 0:2 * D].rearrange("p (c n) -> p c n", c=C)
        Z0, Z1, ZM = zv(0, AB_W), zv(0, C_W), zv(0, 512)
        KWT = z[:, 5216:5728]
        KCVT = z[:, 5728:7008].rearrange("p (g t) -> p g t", g=5)
        POST_GROUP, POST = z[:, 6752:7008], z[:, 6752:6784]
        HIV = z[0:DH, 6752:7264].rearrange("p (g j n) -> p g j n", g=4, j=4)
        VBLK = z[:, 7264:8288].rearrange("p (g j d) -> p g j d", g=4, j=4)
        CMPW = memo[:, 0:2048].rearrange("p (j e) -> p j e", e=DH)
        HID = z[0:DH, 8320:8576].rearrange("p (a g n) -> p a g n", a=2, g=4)
        HIT = z[0:DH, 8576:8832].rearrange("p (a g n) -> p a g n", a=2, g=4)
        KCN = z[:, 8832:8960].rearrange("p (a d) -> p a d", a=2)
        KCT = z[:, 8960:9088]
        GATE = z[:, 9088:9184].rearrange("p (c n) -> p c n", c=C)
        CS, CP = shared[:, 512:1024], shared[:, 1024:1536]
        CPT = [shared[:, 1536:2048], shared[:, 0:512]]
        U = feat[:, :].rearrange("p (k t) -> p k t", t=T)
        ULT, UPT, UGT = U[:, 0:8, :], U[:, 8:12, :], U[:, 12:20, :]
        ZA = z[:, 0:5120].rearrange("p (c n) -> p c n", c=C)
        ZG = z[:, 5120:9216].rearrange("p (c n) -> p c n", c=C)
        XC = z[:, 0:2048].rearrange("p (k t) -> p k t", t=T)
        RG = z[:, 2048:4096].rearrange("p (k t) -> p k t", t=T)
        POOLT = z[:, 4096:5120].rearrange("p (k t) -> p k t", t=T)
        IG = memo[:, 0:2048].rearrange("p (k t) -> p k t", t=T)
        GATEW = memo[:, 2048:4096].rearrange("p (a k n) -> p a k n", a=2, k=8)
        POOLW = shared[:, 1664:2176].rearrange("p (g n) -> p g n", g=4)
        SP4 = shared[:, 2176:2192]
        LAM = shared[:, 2192:2256].rearrange("p (a k) -> p a k", a=8)
        HB = shared[:, 2256:2272].rearrange("p (a k) -> p a k", a=2)
        FHI, FLO = ahi[:, 0:2, :], alo[:, 0:2, :]

        def bank_of(s, c):
            return G[2 * (s.index % 2) + c][:, 0:s.width]

        def turn_bank(n):
            return (SCB if n in plan.turn_in_scores else TB)[n % 2]

        def gain_of(g):
            return lambda k: cols[:, 0, 8 * g + k:8 * g + k + 1]

        def pair(view, first):
            return lambda c: view[:, c, first:first + P]

        def place1(h):
            return 4 * (h // 8) + h % 4, h // 4 % 2

        def z1_dst(s, c):
            v = Z1[:, c, s.c0:s.c0 + s.width]
            if s.c0 < KCMP:
                return v.rearrange("p (i g d) -> p g i d", g=2, d=DH)
            if s.c0 == KCMP:
                return v.rearrange("p (g a d) -> p a g d", a=2, d=DH)
            return v

        def z1_src(s, c):
            v = bank_of(s, c)
            if s.c0 < KCMP:
                return v.rearrange("p (g i d) -> p g i d", g=2, d=DH)
            if s.c0 == KCMP:
                return v.rearrange("p (a g d) -> p a g d", a=2, d=DH)
            return v

        JOBS0 = ([pair(Z0, IQ), pair(Z0, IQ + P), pair(COPIES, 0), pair(COPIES, P)]
                 + [pair(Z0, AQ + P * i) for i in range(4)] + [pair(Z0, BQ + P * i) for i in range(4)]
                 + [pair(Z0, BK + P * i) for i in range(4)])
        JOBSQ = [pair(Z1, NQ + P * i) for i in range(8)]
        JOBSR = JOBSQ + [pair(Z1, KSEL + P * i) for i in range(2)] + [pair(Z1, KWIN + P * i) for i in range(2)]
        JOBSC = [pair(Z1, KCMP + P * g) for g in range(4)]
        SQ1 = {name: feat[:, a_:a_ + C * n * DH].rearrange("p (c h d) -> p c h d", c=C, d=DH)
               for name, a_, n in (("q0", 2048, 8), ("q1", 3072, 8), ("sel", 2048, 4), ("win", 2560, 4))}
        ROPET1 = feat[:, 4608:5120]
        JOBSM = [pair(ZM, P * i) for i in range(4)]

        def head_out(k, half_, c):
            return G[k // 2][DH * half_:DH * half_ + DH, T * (k % 2) + P * c:T * (k % 2) + P * c + P]

        def items0():
            out_ = []
            for q0, k0, one_key, bias, v0, dv, chunk in ((2048, 3072, False, causal, BV, DH, 4), (1024, 768, True, dsa_bias, AV, 0, 0)):
                for h in range(8):
                    r = slice(DH * (h % 2), DH * (h % 2) + DH)
                    branches = []
                    for c in range(C):
                        nk = P * (c + 1)
                        q, k = q0 + T * (h // 2) + P * c, k0 + (0 if one_key else T * (h // 2))
                        branches.append(Branch(feat[r, q:q + P], feat[r, k:k + nk], nk, bias[:, c, 0:nk],
                                               [Z0[:, b, v0 + dv * h:v0 + dv * h + DH] for b in range(c + 1)],
                                               head_out(chunk + h // 2, h % 2, c)))
                    out_.append(Item(branches, DH ** -0.5))
            return out_

        def items1():
            out_ = []
            for h in range(16):
                (jq, half_), g = place1(h), h // 4
                r = slice(DH * half_, DH * half_ + DH)
                for c in range(C):
                    nk, q = P * (c + 1), 2048 + T * jq + P * c
                    branches = [Branch(feat[r, q:q + P], keys[r, T * (g // 2):T * (g // 2) + nk], nk, causal[:, c, 0:nk],
                                       [Z1[:, b, v0 + DH * g:v0 + DH * g + DH] for b in range(c + 1)],
                                       head_out(h // 2, h % 2, c))
                                for keys, v0 in ((feat[:, 4096:4608], VSEL), (KWT, VWIN))]
                    out_.append(Item(branches, DH ** -0.5, GATE[:, c, 3 * h + 1:3 * h + 3],
                                     (VBLK[:, g, h % 4, :], CPT[c][:, P * g:P * g + P])))
            return out_

        def items_mem(l):
            return [Item([Branch(feat[:, T * h + P * c:T * h + P * (c + 1)], memk[l][:, h, :], T, zero[:, :],
                                 [memv[l][:, b, P * h:P * h + P] for b in range(C)],
                                 G[h // 2][:, T * (h % 2) + P * c:T * (h % 2) + P * c + P]) for c in range(C)], P ** -0.5)
                    for h in range(4)]

        def xsrc(c, k):
            return x[:, c, P * k:P * k + P]

        def ysrc(c, k):
            return ZG[:, c, P * k:P * k + P]

        def dve_share(n):
            return LO_DVE if n == UNIT else n * 3 // 16 * 2

        def loop_turns(b):
            return b.first // b.per, b.last // b.per, b.per

        def landed_at(b, j, c):
            ref = b.base + 3 * b.first + c
            return plan.landed(ref) + 16 * plan.dmas[ref] * (j - b.first)

        block = ctx.enter_context(nc.Block())

        @block.sync
        def _(sp):
            def slot_free(u, static=True):
                if not static or u >= RING:
                    sp.wait_ge(lo_dve, u - RING + 1)
                    sp.wait_ge(lo_pool, u - RING + 1)

            def load_slab(s):
                for i in range(s.units):
                    u, nk = s.unit + i, min(4, s.k)
                    slot_free(u)
                    sp.dma_start(raw[u % RING][:, 0:nk * s.width].rearrange("p (k n) -> p k n", k=nk),
                                 s.w[512 * i:512 * i + P * nk, s.c0:s.c0 + s.width].rearrange("(k p) n -> p k n", p=P)
                                 ).then_inc(raw_loaded[u % RING], 16)

            def load_up(b, j, half, u, slot, static, e=None, h=None):
                slot_free(u, static)
                kind, l = b.load
                dst = raw[slot][:, :].rearrange("p (k a f) -> p k a f", k=4, a=2)
                if kind == "ffn":
                    for n in range(2):
                        src = a["ffn_w_in"][l, 512 * half:512 * half + 512, FF * n:FF * n + FF].rearrange("(k p) f -> p k f", p=P)
                        sp.dma_start(dst[:, :, n, :], src[:, :, bass.ds(j * FB, FB)]).then_inc(raw_loaded[slot], 16)
                else:
                    for n, w in enumerate(("exp_w_gate_2", "exp_w_up_2")):
                        src = a[w][0, bass.ds(e, 1), 512 * half:512 * half + 512, FB * h:FB * h + FB]
                        src = src.rearrange("e (k p) f -> p (e k) f", p=P)
                        sp.dma_start(dst[:, :, n, :], src).then_inc(raw_loaded[slot], 16)

            def load_down(b, j, u, slot, static):
                slot_free(u, static)
                kind, l = b.load
                w = a["ffn_w_out"][l] if kind == "ffn" else a["exp_w_down_2"][0].rearrange("e f n -> (e f) n")
                src = w[bass.ds(j * FB, FB), :].rearrange("(r p) n -> p r n", p=P)
                sp.dma_start(raw[slot][:, :].rearrange("p (r n) -> p r n", r=2), src).then_inc(raw_loaded[slot], 16)

            def load_block(b, j, static, e=None, h=None):
                u = b.base + 3 * j - 1
                s = (b.base - 1) % RING
                load_up(b, j, 0, u, s, static, e, h)
                load_up(b, j, 1, u + 1, (s + 1) % RING, static, e, h)
                load_down(b, j - 1, u + 2, (s + 2) % RING, static)

            def load_blocks(b):
                halves = 2 if b.per == 2 else 1
                where = (lambda j: (j // 2, j % 2)) if halves == 2 else (lambda j: (None, None))
                load_up(b, 0, 0, b.base, b.base % RING, True, *where(0))
                load_up(b, 0, 1, b.base + 1, (b.base + 1) % RING, True, *where(0))
                load_block(b, 1, True, *where(1))
                first, last, per = loop_turns(b)
                with sp.Fori(first, last) as i:
                    for n in range(per):
                        load_block(b, i * per + n, False, i, n)
                for j in range(b.last, b.n):
                    load_block(b, j, True, *where(j))
                load_down(b, b.n - 1, b.base + 3 * b.n - 1, (b.base + 3 * b.n - 1) % RING, True)

            sp.dma_start(x[:, :, :], a["x"][0].rearrange("(c p) n -> p c n", p=P)).then_inc(flag("x_in"), 16)
            for n, s in enumerate(plan.loads):
                if n == 1:
                    sp.dma_start(MEMIN, a["mem"][0].rearrange("(c p) n -> p c n", p=P)).then_inc(flag("mem_in"), 16)
                load_blocks(s) if isinstance(s, Blocks) else load_slab(s)
                if s is L[0]["mo"][-1]:
                    sp.wait_ge(pved, L[0]["mheads"].outs + 4)
                    for n_, w in enumerate(("nsa_cmp_w1_k", "nsa_cmp_w1_v")):
                        sp.dma_start(CMPW[DH * n_:DH * n_ + DH], a[w][0].rearrange("(j d) e -> d j e", d=DH)
                                     ).then_inc(flag("cmp_weights_in"), 16)
                if s is L[1]["mo"][-1]:
                    sp.wait_ge(pved, L[1]["mheads"].outs + 4)
                    sp.wait_ge(flag("gate_weights_zeroed"), 1)
                    for n_, w in enumerate(("rg_w_r_2", "rg_w_i_2")):
                        src = a[w][0].rearrange("(k h) c d -> h c k d", h=2)
                        for h in range(2):
                            r = slice(DH * h, DH * h + DH)
                            sp.dma_start(GATEW[r, n_, :, DH * h:DH * h + DH], src[h]).then_inc(flag("gate_weights_in"), 16)
                    sp.dma_start(POOLW, a["pool_w_2"][0].rearrange("g c d -> c g d")).then_inc(flag("gate_weights_in"), 16)
                if s is N["pb"][-1]:
                    sp.wait_ge(flag("lru_done"), 1)
                    wide = route_w
                    sp.dma_start(wide[:, :, 0:N_GRP], a["router_group_w_2"][0].rearrange("(k p) n -> p k n", p=P)).then_inc(flag("router_in"), 16)
                    sp.dma_start(wide[:, :, N_GRP:20], a["router_expert_w_2"][0].rearrange("(k p) n -> p k n", p=P)).then_inc(flag("router_in"), 16)
                    sp.dma_start(route_b[:, 0:N_GRP], a["router_group_b_2"].broadcast_to([P, N_GRP])).then_inc(flag("router_in"), 16)
                    sp.dma_start(route_b[:, N_GRP:20], a["router_expert_b_2"].broadcast_to([P, N_EXP])).then_inc(flag("router_in"), 16)
                    sp.dma_start(final_gain, a["norm_f_g_2"].rearrange("(a n) -> a n", a=1).broadcast_to([P, D])).then_inc(flag("final_gain_in"), 16)
            for c in range(C):
                sp.wait_ge(flag("out_ready"), c + 1)
                sp.dma_start(out[0, P * c:P * c + P, :], XN[:, c, :]).then_inc(flag("stored"), 16)
            sp.wait_ge(flag("stored"), 32)

        @block.gpsimd
        def _(pool):
            step = Chain(pool, pool_step)
            at = [0]

            def lo(u, slot, n):
                s = dve_share(n)
                pool.wait_ge(hi_done, u + 1)
                pool.tensor_tensor(wlo[slot][:, s:n], raw[slot][:, s:n], whi[slot][:, s:n].bitcast(F32),
                                   ALU.subtract).then_inc(lo_pool, 1)

            def split_to(end):
                while at[0] < min(end, n_units):
                    lo(at[0], at[0] % RING, plan.width[at[0]])
                    at[0] += 1

            def blocks(b):
                first, last, per = loop_turns(b)
                split_to(b.base + 3 * b.first + 1)
                with pool.Fori(first, last) as i:
                    for n in range(per):
                        for c in range(1, 4):
                            lo(b.base + 3 * (i * per + n) + c, (b.base + c) % RING, UNIT)
                at[0] = b.base + 3 * b.last + 1

            step(pool.memset(ident[:, :], 0.0))
            step(pool.affine_select(out=ident[:, :], in_=ident[:, :], compare_op=ALU.not_equal, fill=1.0,
                                    base=0, pattern=[[-1, P]], channel_multiplier=1))
            step(pool.memset(zero[:, :], 0.0))
            for c in range(C):
                step(pool.affine_select(out=causal[:, c, :], in_=zero[:, :], compare_op=ALU.is_ge, fill=NEG,
                                        base=P * c, pattern=[[-1, T]], channel_multiplier=1))
            for c in range(C):
                step(pool.affine_select(out=cmp_bias[:, c, :], in_=zero[:, 0:32], compare_op=ALU.is_ge, fill=NEG,
                                        base=P * c - (CMP_LEN - 1), pattern=[[-CMP_STRIDE, 32]], channel_multiplier=1))
            step(pool.memset(cmp_keep[:, :, :], 1.0))
            for c in range(C):
                step(pool.affine_select(out=cmp_keep[:, c, :], in_=cmp_keep[:, c, :], compare_op=ALU.is_ge, fill=0.0,
                                        base=P * c - (CMP_LEN - 1), pattern=[[-CMP_STRIDE, 32]], channel_multiplier=1))
            for t in range(16):
                step(pool.memset(numbers[:, t:t + 1], 1.0 / (t + 1)))
            pool.memset(half[:, :], 0.5).then_inc(flag("masks_ready"), 1)

            def scale_probs(items, run):
                for t, it in enumerate(items):
                    p_ = run.prob[(run.first + t) % 4]
                    pool.wait_ge(item_weighed, run.outs + t + 1)
                    for n in range(2):
                        nk = it.branches[n].nk
                        pn = p_[:, it.at[n]:it.at[n] + nk]
                        ins = pool.tensor_tensor(pn, pn, item_inv[:, 2 * t + n:2 * t + n + 1].broadcast_to([P, nk]), ALU.mult)
                    ins.then_inc(prob_scaled, 1)

            for l in range(2):
                split_to(L[l]["out"][0].unit + 2)
                scale_probs(items1() if l else items0(), L[l]["heads"])
                split_to(L[l]["mo"][0].unit + 2)
                scale_probs(items_mem(l), L[l]["mheads"])
                split_to(L[l]["ff"].base)
                if l == 1:
                    pool.wait_ge(pved, L[1]["mheads"].outs + 4)
                    pool.memset(GATEW, 0.0).then_inc(flag("gate_weights_zeroed"), 1)
                blocks(L[l]["ff"])
            split_to(N["moe"].base)
            blocks(N["moe"])
            split_to(n_units)

        @block.scalar
        def _(act):
            step = Chain(act, act_step)
            at = [0]

            def hi(u, slot, n, landed, static=True):
                act.wait_ge(raw_loaded[slot], landed)
                if not static or u >= RING:
                    act.wait_ge(unit_used, u - RING + 1)
                act.activation(whi[slot][:, 0:n], raw[slot][:, 0:n], ACT.Copy).then_inc(hi_done, 1)

            def split_to(end):
                while at[0] < min(end, n_units):
                    u = at[0]
                    hi(u, u % RING, plan.width[u], plan.landed(u))
                    at[0] += 1

            def product(slabs, dst, src=bank_of, scale=True):
                for s in slabs:
                    split_to(s.end + 2)
                    if s.evac == "both":
                        act.wait_ge(unit_used, s.end)
                        act.activation(dst(s, 0), src(s, 0), ACT.Copy, scale=row_scale[:, 0:1] if scale else 1.0
                                       ).then_inc(slab_act, 1)

            def to_t(base, batches, gain, dst):
                for b in batches:
                    act.wait_ge(turned, base + b + 1)
                    bank = turn_bank(base + b)
                    for n in range(2):
                        k = 2 * b + n
                        ins = act.activation(dst[:, k, :], bank[:, T * n:T * n + T], ACT.Copy,
                                             scale=gain(k) if callable(gain) else gain)
                    ins.then_inc(turn_act, 1)

            def squares(src, tag, scratch=2048):
                for c in range(C):
                    ins = act.activation(z[:, scratch + D * c:scratch + D * c + D], src[:, c, :], ACT.Square,
                                         accum_out=sumsq[:, c:c + 1])
                ins.then_inc(flag("squared_" + tag), 1)

            def head_squares(parts, slabs, tag):
                act.wait_ge(slab_act, slabs[-1].done_act)
                act.wait_ge(slab_dve, slabs[-1].done_dve)
                for src, dst in parts:
                    ins = act.activation(dst, src, ACT.Square)
                ins.then_inc(flag("head_squares_" + tag), 1)

            def attention(items, run, banks):
                n, per = run.n, run.per
                for t in range(n + 5 + 1):
                    if t < n:
                        it, g = items[t], run.first + t
                        act.wait_ge(item_masked, g + 1)
                        if t >= 4:
                            act.wait_ge(turned, run.batch + t - 3)
                        for m in range(2):
                            a_, b_ = it.at[m], it.at[m] + it.branches[m].nk
                            ins = act.activation(run.prob[g % 4][:, a_:b_], run.masked[g % 2][:, a_:b_], ACT.Exp, scale=-1.0,
                                                 bias=item_min[:, 2 * t + m:2 * t + m + 1],
                                                 accum_out=item_sum[:, 2 * t + m:2 * t + m + 1])
                        ins.then_inc(exped, 1)
                    if t >= 5 and (t - 4) % per == 0:
                        k = banks[(t - 4) // per - 1]
                        act.wait_ge(pved, run.outs + t - 4)
                        act.activation(ahi[:, 2 * k:2 * k + 2, :], G[k][:, :].rearrange("p (k t) -> p k t", k=2),
                                       ACT.Copy).then_inc(heads_hi, 1)

            def ff_up_out(j, static=True):
                for c in range(C):
                    if c == 0:
                        act.wait_ge(unit_used, ff_gu_unit(j))
                        if not static or ff_n(j) >= 1:
                            act.wait_ge(ff_silu, ff_n(j))
                    act.activation(silu[:, c, 0, :], TB[c][:, 0:FB], ACT.Tanh, scale=half_scale[:, c:c + 1]).then_inc(ff_tanh, 1)

            def ff_hidden(j):
                act.wait_ge(ff_turned, ff_n(j) + 1)
                act.activation(FHI, SCB[0][:, :].rearrange("p (f t) -> p f t", f=2), ACT.Copy).then_inc(ff_hi, 1)

            def blocks(b):
                nonlocal ff_n, ff_gu_unit
                ff_n = lambda j: b.start + j
                ff_gu_unit = lambda j: b.base + 2 if isinstance(j, int) and j == 0 else b.base + 3 * j + 1
                split_to(b.base + 3)
                ff_up_out(0)
                split_to(b.base + 4)
                ff_hidden(0)
                split_to(b.base + 6)
                ff_up_out(1)
                split_to(b.base + 7)
                first, last, per = loop_turns(b)
                with act.Fori(first, last) as i:
                    for n in range(per):
                        j = i * per + n
                        ff_hidden(j - 1)
                        for c in (1, 2):
                            hi(b.base + 3 * j + c, (b.base + c) % RING, UNIT, landed_at(b, j, c), False)
                        ff_up_out(j, False)
                        hi(b.base + 3 * j + 3, (b.base + 3) % RING, UNIT, landed_at(b, j, 3), False)
                at[0] = b.base + 3 * b.last + 1
                for j in range(b.last, b.n):
                    ff_hidden(j - 1)
                    split_to(b.base + min(3 * j + 3, 3 * b.n))
                    ff_up_out(j)
                    split_to(b.base + min(3 * j + 4, 3 * b.n))
                ff_hidden(b.n - 1)

            ff_n = ff_gu_unit = None

            def load(dst, src, name):
                act.dma_start(dst, src).then_inc(flag(name), 16)

            for l in range(2):
                for g, name in ((G_MIX, "norm_mix"), (G_MEM, "norm_mem"), (G_SRC, "norm_mem_src"), (G_FFN, "norm_ffn")):
                    load(rows[8 * g[l]:8 * g[l] + 8, 0, :], a[name][l].rearrange("(k p) -> k p", p=P), "rows_in")
            for g, name in ((G_N1, "norm1_g_2"), (G_N2, "norm2_g_2")):
                load(rows[8 * g:8 * g + 8, 0, :], a[name][0].rearrange("(k p) -> k p", p=P), "rows_in")
            load(rows[0:32, 1, :], a["conv_w_2"][0].rearrange("w (k p) -> (w k) p", p=P), "rows_in")
            for r, name in ((R_CB, "conv_b_2"), (R_BR, "rg_b_r_2"), (R_BI, "rg_b_i_2"), (R_LAM, "rg_lambda_2")):
                load(rows[r:r + 8, 1, :], a[name][0].rearrange("(k p) -> k p", p=P), "rows_in")
            load(rows[R_PS:R_PS + 4, 1, :], a["pool_scale_2"][0].rearrange("(k p) -> k p", p=P), "rows_in")
            load(pos_i[:, :], a["positions"].rearrange("a (c p) -> (a c) p", p=P), "positions_in")
            act.wait_ge(flag("x_in"), 16)
            squares(x, "mix0")
            for n, name in enumerate(("dsa_q_norm", "dsa_k_norm", "moba_q_norm", "moba_k_norm", "nsa_q_norm",
                                      "nsa_kcmp_norm", "nsa_ksel_norm", "nsa_kwin_norm")):
                load(gains[:, n, :], a[name].broadcast_to([P, DH]), "gains_in")
            for l in range(2):
                load(mem_q_gain[:, l, :], a["mem_q_norm"][l:l + 1, :].broadcast_to([P, P]), "gains_in")
                load(mem_k_gain[:, l, :], a["mem_k_norm"][l:l + 1, :].broadcast_to([P, P]), "gains_in")
            load(pos_rows[:, 0:DH], a["nsa_cmp_pos_k"][0], "gains_in")
            load(pos_rows[:, DH:P], a["nsa_cmp_pos_v"][0], "gains_in")
            load(w2[:, 0, :], a["nsa_cmp_w2_k"][0], "gains_in")
            load(w2[:, 1, :], a["nsa_cmp_w2_v"][0], "gains_in")

            for l in range(2):
                s = L[l]
                act.wait_ge(flag("cols_ready"), 1)
                to_t(s["hturn"], range(4), gain_of(G_MIX[l]), ahi)
                if l:
                    act.wait_ge(flag("ff_added0"), 2)
                    squares(x, "mix1")
                act.wait_ge(flag(f"row_scale_mix{l}"), 1)
                if l == 0:
                    act.wait_ge(flag("mem_in"), 16)
                    squares(MEMIN, "mem", 4944)
                    act.wait_ge(flag("angles"), 1)
                    act.activation(sine[:, :, :], angle[:, 2], ACT.Sin)
                    act.activation(cosine[:, :, :], angle[:, 3], ACT.Sin).then_inc(flag("rotation"), 1)

                    def z0(s_, c):
                        return Z0[:, c, s_.c0:s_.c0 + s_.width]

                    product(s["in"][0:2], z0)
                    head_squares([(heads(Z0, AQ, 9, DH), SQA)], s["in"][0:2], "a")
                    product(s["in"][2:3], z0)
                    head_squares([(heads(Z0, BQ, 8, DH), SQQ)], s["in"][0:3], "bq")
                    product(s["in"][3:4], z0)
                    head_squares([(heads(Z0, BK, 8, DH), SQK)], s["in"][0:4], "bk")
                    product(s["in"][4:5], z0)
                    for b in range(4):
                        act.wait_ge(turned, mem_turn + b + 1)
                        for m, dst in enumerate((bhi, ahi)):
                            for n in range(2):
                                ins = act.activation(dst[:, 2 * b + n, :], TB[(mem_turn + b) % 2][:, T * n:T * n + T],
                                                     ACT.Copy, scale=gain_of(G_SRC[m])(2 * b + n))
                        ins.then_inc(turn_act, 1)
                    for n, s_ in enumerate(M[0]["kv"]):
                        for v in range(s_.units):
                            split_to(s_.unit + v + RING)
                            for i in range(8 * n + 4 * v, 8 * n + 4 * v + 4):
                                g, nk = s["index"] + i, P * (i // 8 + 1)
                                act.wait_ge(scored, g + 1)
                                if i >= 3:
                                    act.wait_ge(item_masked, g - 2)
                                act.activation(relu_out[g % 3][:, 0:nk], SCB[g % 2][:, 0:nk], ACT.Relu).then_inc(exped, 1)
                        act.wait_ge(unit_used, s_.end)
                        act.activation((memk_rows if n == 0 else memv)[0][:, 0, :], bank_of(s_, 0), ACT.Copy).then_inc(slab_act, 1)
                    product(M[1]["kv"], lambda s_, c: (memk_rows if s_.c0 == 0 else memv)[1][:, c, :], scale=False)
                    attention(items0(), s["heads"], (2, 3, 0, 1))
                else:
                    product(s["cmp"] + s["gt"], z1_dst, z1_src)
                    act.wait_ge(slab_act, s["gt"][-1].done_act)
                    act.wait_ge(slab_dve, s["gt"][-1].done_dve)
                    act.activation(GATE, Z1[:, :, GT:C_W], ACT.Tanh, scale=0.5).then_inc(flag("gates_tanh"), 1)
                    for name, first, n in (("q0", NQ, 8), ("q1", NQ + 512, 8), ("sel", KSEL, 4), ("win", KWIN, 4)):
                        product(s[name], z1_dst, z1_src)
                        head_squares([(heads(Z1, first, n, DH), SQ1[name])], s[name], name)
                        if name == "q1":
                            split_to(s["q1"][-1].end + RING)
                            act.wait_ge(flag("cmp_hidden"), 1)
                            act.activation(HIT, HID, ACT.Tanh, scale=0.5).then_inc(flag("cmp_tanh"), 1)
                    split_to(s["win"][-1].end + RING)
                    for c in range(C):
                        act.wait_ge(flag("cmp_shifted"), c + 1)
                        act.activation(CP, CS, ACT.Exp).then_inc(flag("cmp_exp"), 1)
                    attention(items1(), s["heads"], (0, 1, 2, 3))
                if l == 0:
                    act.wait_ge(slab_dve, M[1]["kv"][-1].done_dve)
                    for m in range(2):
                        ins = act.activation(zv(4944 + 1024 * m, 512), memk_rows[m], ACT.Square)
                    ins.then_inc(flag("head_squares_mk"), 1)
                product(s["out"][0:1], None)
                to_t(s["mturn"], range(2), gain_of(G_MEM[l]), bhi)
                product(s["out"][1:2], None)
                to_t(s["mturn"], range(2, 4), gain_of(G_MEM[l]), bhi)
                act.wait_ge(slab_dve, s["out"][-1].done_dve)
                squares(x, f"memq{l}")
                act.wait_ge(flag(f"row_scale_memq{l}"), 1)
                product(s["mq"], lambda s_, c: ZM[:, c, :])
                head_squares([(heads(ZM, 0, 4, P), heads(zv(2048, 512), 0, 4, P))], s["mq"], f"memq{l}")
                if l == 0:
                    for m in range(2):
                        act.wait_ge(turned, M[m]["kturn"] + 2)
                        for b in range(2):
                            act.activation(memo[:, 2048 * m + 512 * b:2048 * m + 512 * b + 512],
                                           TB[(M[m]["kturn"] + b) % 2][:, :], ACT.Copy).then_inc(turn_act, 1)
                split_to(s["mo"][-1].end)
                attention(items_mem(l), s["mheads"], (0, 1))
                product(s["mo"][0:1], None)
                to_t(s["fturn"], range(2), gain_of(G_FFN[l]), bhi)
                product(s["mo"][1:2], None)
                to_t(s["fturn"], range(2, 4), gain_of(G_FFN[l]), bhi)
                act.wait_ge(slab_dve, s["mo"][-1].done_dve)
                squares(x, f"ffn{l}")
                act.wait_ge(flag(f"row_scale_ffn{l}"), 1)
                blocks(s["ff"])
                split_to(s["ff"].base + 3 * s["ff"].n + 2)

            to_t(N["hturn"], range(4), gain_of(G_N1), ahi)
            act.wait_ge(flag("ff_added1"), 2)
            squares(x, "mix2")
            act.wait_ge(flag("minus_abs_lambda"), 1)
            act.activation(LAM[:, 1, :], LAM[:, 1, :], ACT.Exp).then_inc(flag("exp_lambda"), 1)
            act.wait_ge(flag("row_scale_mix2"), 1)
            product(N["in"], lambda s_, c: ZA[:, c, s_.c0:s_.c0 + s_.width])
            product(N["gates"][0:2], lambda s_, c: ZG[:, c, s_.c0 - GA:s_.c0 - GA + 512])
            for k in range(8):
                act.wait_ge(turned, N["gturn"] + k + 1)
                bank = TB[(N["gturn"] + k) % 2]
                act.activation(RG[:, k, :], bank[:, 0:T], ACT.Tanh, scale=0.5, bias=HB[:, 0, k:k + 1])
                act.activation(IG[:, k, :], bank[:, T:2 * T], ACT.Tanh, scale=0.5, bias=HB[:, 1, k:k + 1]).then_inc(turn_act, 1)
            split_to(N["gates"][1].end + RING)
            act.wait_ge(flag("log_decay"), 1)
            act.activation(ULT, RG, ACT.Exp, scale=-1.0).then_inc(flag("decay"), 1)
            act.wait_ge(flag("decay"), 1)
            act.activation(RG, RG, ACT.Tanh).then_inc(flag("decay_tanh"), 1)
            act.wait_ge(flag("gelu_inner"), 1)
            act.activation(IG, IG, ACT.Tanh, scale=math.sqrt(2 / math.pi)).then_inc(flag("gelu_tanh"), 1)
            product(N["gates"][2:4], lambda s_, c: ZG[:, c, s_.c0 - GA:s_.c0 - GA + 512])
            act.wait_ge(slab_act, N["gates"][-1].done_act)
            act.wait_ge(slab_dve, N["gates"][-1].done_dve)
            act.activation(ZG, ZG, ACT.Tanh, scale=0.5).then_inc(flag("mix_gates"), 1)
            to_t(N["yturn"], range(2), lambda k: cols[:, 1, R_PS + k:R_PS + k + 1], ahi)
            act.wait_ge(flag("drive_squared"), 1)
            act.activation(RG, RG, ACT.Sqrt, scale=0.25).then_inc(flag("drive_scale"), 1)
            act.wait_ge(flag("lru_out"), 1)
            act.activation(bhi[:, :, :], ULT, ACT.Copy).then_inc(flag("lru_hi"), 1)
            product(N["pa"], None)
            product(N["pb"][0:1], None)
            to_t(N["oturn"], range(2), 0.5, ahi)
            product(N["pb"][1:2], None)
            to_t(N["oturn"], range(2, 4), 0.5, ahi)
            product(N["out"][0:1], None)
            to_t(N["h2turn"], range(2), gain_of(G_N2), bhi)
            product(N["out"][1:2], None)
            to_t(N["h2turn"], range(2, 4), gain_of(G_N2), bhi)
            act.wait_ge(slab_dve, N["out"][-1].done_dve)
            squares(x, "moe")
            act.wait_ge(flag("row_scale_moe"), 1)
            act.wait_ge(flag("router_in"), 64)
            act.activation(rhi[:, :, :], route_w, ACT.Copy).then_inc(flag("router_hi"), 1)
            split_to(N["moe"].base + RING)
            act.wait_ge(flag("group_shifted"), 1)
            act.activation(rt[:, 1, :, 0:N_GRP], rt[:, 0, :, 0:N_GRP], ACT.Exp).then_inc(flag("group_exp"), 1)
            act.wait_ge(flag("expert_gap"), 1)
            act.activation(rt[:, 9, :, 0:1], rt[:, 8, :, 0:1], ACT.Exp).then_inc(flag("expert_exp"), 1)
            blocks(N["moe"])
            act.wait_ge(flag("ff_added2"), 2)
            squares(x, "final")

        @block.vector
        def _(dve):
            step = Chain(dve, dve_step)
            at = [0]

            def lo(u, slot, n):
                s = dve_share(n)
                dve.wait_ge(hi_done, u + 1)
                dve.tensor_tensor(wlo[slot][:, 0:s], raw[slot][:, 0:s], whi[slot][:, 0:s].bitcast(F32),
                                  ALU.subtract).then_inc(lo_dve, 1)

            def split_to(end):
                while at[0] < min(end, n_units):
                    lo(at[0], at[0] % RING, plan.width[at[0]])
                    at[0] += 1

            def product(slabs, dst, src=bank_of, scale=True):
                for s in slabs:
                    split_to(s.end + 2)
                    dve.wait_ge(unit_used, s.end)
                    if s.evac == "both":
                        if scale:
                            dve.tensor_scalar(dst(s, 1), src(s, 1), row_scale[:, 1:2], None, ALU.mult).then_inc(slab_dve, 1)
                        else:
                            dve.tensor_copy(dst(s, 1), src(s, 1)).then_inc(slab_dve, 1)
                    else:
                        for c in range(C):
                            if dst is None:
                                xs = x[:, c, s.c0:s.c0 + s.width]
                                dve.tensor_tensor(xs, xs, bank_of(s, c), ALU.add).then_inc(slab_dve, 1)
                            else:
                                dst(s, c)
                if slabs[-1].evac == "dve":
                    dve.wait_ge(slab_dve, slabs[-1].done_dve)

            def rsqrt(n, d):
                m, y, t, u = (s_[:, 0:n] for s_ in (s_mean, s_y, s_t, s_u))
                step(dve.tensor_scalar(m, m, 1.0 / d, EPS, ALU.mult, ALU.add))
                step(dve.tensor_scalar(s_bits[:, 0:n], m.bitcast(I32), 1, None, ALU.logical_shift_right))
                step(dve.tensor_scalar(y.bitcast(I32), s_bits[:, 0:n], -1.0, 1597463007.0, ALU.mult, ALU.add))
                dve.tensor_scalar(m, m, -0.5, None, ALU.mult)
                for _ in range(3):
                    step(dve.tensor_tensor(t, y, y, ALU.mult))
                    step(dve.tensor_tensor(u, t, m, ALU.mult))
                    step(dve.scalar_tensor_tensor(out=y, in0=u, scalar=1.5, in1=y, op0=ALU.add, op1=ALU.mult))

            def norm(src, tag, dst=XN):
                dve.wait_ge(flag("squared_" + tag), 1)
                step(dve.tensor_copy(s_mean[:, 0:C], sumsq[:, :]))
                rsqrt(C, D)
                for c in range(C):
                    ins = dve.tensor_scalar(dst[:, c, :], src[:, c, :], s_y[:, c:c + 1], None, ALU.mult)
                ins.then_inc(flag("normed_" + tag), 1)

            def row_scales(tag):
                dve.wait_ge(flag("squared_" + tag), 1)
                step(dve.tensor_copy(s_mean[:, 0:C], sumsq[:, :]))
                rsqrt(C, D)
                dve.tensor_scalar(half_scale[:, :], s_y[:, 0:C], 0.5, None, ALU.mult)
                step(dve.tensor_copy(row_scale[:, :], s_y[:, 0:C]))
                step(dve.tensor_tensor(half_scale2[:, :], half_scale[:, :], row_scale[:, :], ALU.mult))
                dve.sem_inc(flag("row_scale_" + tag), 1)

            def to_t(base, batches, gain, hi_, dst):
                for b in batches:
                    dve.wait_ge(turn_act, plan.turn_act[base + b + 1])
                    bank = turn_bank(base + b)
                    for n in range(2):
                        k = 2 * b + n
                        ins = dve.scalar_tensor_tensor(out=dst[:, k, :], in0=bank[:, T * n:T * n + T],
                                                       scalar=gain(k) if callable(gain) else gain,
                                                       in1=hi_[:, k, :].bitcast(F32), op0=ALU.mult, op1=ALU.subtract)
                    ins.then_inc(turn_dve, 1)

            def turns(base, n, dst):
                for b in range(n):
                    dve.wait_ge(turned, base + b + 1)
                    dve.tensor_copy(dst(b), turn_bank(base + b)[:, :]).then_inc(turn_dve, 1)
                dve.wait_ge(turn_dve, plan.turn_dve[base + n])

            def head_norm(parts, d, tag):
                dve.wait_ge(flag("head_squares_" + tag), 1)
                at_ = 0
                for sq, v, _ in parts:
                    n = v.shape[2]
                    step(dve.tensor_reduce(s_mean[:, at_:at_ + C * n].rearrange("p (c h) -> p c h", c=C), sq, AX, ALU.add))
                    at_ += C * n
                rsqrt(at_, d)
                at_ = 0
                for _, v, _ in parts:
                    n = v.shape[2]
                    r = s_y[:, at_:at_ + C * n].rearrange("p (c h) -> p c h", c=C).unsqueeze(3).broadcast_to([P, C, n, d])
                    ins = dve.tensor_tensor(v, v, r, ALU.mult)
                    at_ += C * n
                step(ins)
                for _, _, gs in parts:
                    for v, g in gs:
                        n = v.shape[2]
                        ins = dve.tensor_tensor(v, v, g.unsqueeze(1).unsqueeze(1).broadcast_to([P, C, n, d]), ALU.mult)
                step(ins)

            def rope(v, hf, scratch):
                n = v.shape[2]
                w = C * n * hf
                v1, v2 = v[:, :, :, 0:hf], v[:, :, :, hf:2 * hf]
                co, si = (t_[:, :, 0:HALF:HALF // hf].unsqueeze(2).broadcast_to([P, C, n, hf]) for t_ in (cosine, sine))
                t = [scratch[:, w * i:w * i + w].rearrange("p (c h d) -> p c h d", c=C, h=n) for i in range(4)]
                dve.tensor_tensor(t[0], v1, co, ALU.mult)
                dve.tensor_tensor(t[1], v2, si, ALU.mult)
                dve.tensor_tensor(t[2], v2, co, ALU.mult)
                step(dve.tensor_tensor(t[3], v1, si, ALU.mult))
                dve.tensor_tensor(v1, t[0], t[1], ALU.subtract)
                step(dve.tensor_tensor(v2, t[2], t[3], ALU.add))

            def attention(items, run, banks):
                n, per = run.n, run.per
                for t in range(n + 5 + 1):
                    if t < n:
                        it, g = items[t], run.first + t
                        dve.wait_ge(scored, g + 1)
                        if t >= 2:
                            dve.wait_ge(exped, g - 1)
                        for m, b_ in enumerate(it.branches):
                            s_ = slice(it.at[m], it.at[m] + b_.nk)
                            ins = dve.tensor_tensor_reduce(run.masked[g % 2][:, s_], SCB[g % 2][:, s_], b_.bias, -it.scale,
                                                           -TAKEN, ALU.add, ALU.min, item_min[:, 2 * t + m:2 * t + m + 1])
                        ins.then_inc(item_masked, 1)
                    if 0 <= t - 1 < n:
                        i = t - 1
                        inv = item_inv[:, 2 * i:2 * i + 2]
                        dve.wait_ge(exped, run.first + i + 1)
                        ins = dve.reciprocal(inv, item_sum[:, 2 * i:2 * i + 2])
                        if items[i].weight is not None:
                            step(ins)
                            ins = dve.tensor_tensor(inv, inv, items[i].weight, ALU.mult)
                        ins.then_inc(item_weighed, 1)
                    if 0 <= t - 3 < n:
                        i = t - 3
                        dve.wait_ge(turned, run.batch + i + 1)
                        if i >= 2:
                            dve.wait_ge(pved, run.outs + i - 1)
                        w = items[i].width
                        dve.tensor_copy(run.probt[i % 2][:, 0:w], TB[(run.batch + i) % 2][:, 0:w]).then_inc(turn_dve, 1)
                    if t >= 5 and (t - 4) % per == 0:
                        bank_ = (t - 4) // per
                        k = banks[bank_ - 1]
                        dve.wait_ge(heads_hi, run.banks + bank_)
                        dve.tensor_tensor(alo[:, 2 * k:2 * k + 2, :], G[k][:, :].rearrange("p (k t) -> p k t", k=2),
                                          ahi[:, 2 * k:2 * k + 2, :].bitcast(F32), ALU.subtract).then_inc(heads_lo, 1)

            def ff_silu_(b, j, static=True):
                n = b.start + j
                for c in range(C):
                    dve.wait_ge(ff_tanh, 2 * n + c + 1)
                    if c == 0 and (not static or n >= 1):
                        dve.wait_ge(ff_turned, n)
                    gate, up, t1 = TB[c][:, 0:FB], TB[c][:, FB:2 * FB], silu[:, c, 1, :]
                    dve.scalar_tensor_tensor(out=t1, in0=silu[:, c, 0, :], scalar=1.0, in1=gate, op0=ALU.add,
                                             op1=ALU.mult).then_inc(flag("silu_half"), 1)
                    dve.wait_ge(flag("silu_half"), 2 * n + c + 1)
                    w = half_scale2[:, c:c + 1] if b.load[0] == "ffn" else half_comb[:, c, bass.ds(j, 1)]
                    ins = dve.scalar_tensor_tensor(out=t1, in0=t1, scalar=w, in1=up, op0=ALU.mult, op1=ALU.mult)
                ins.then_inc(ff_silu, 1)

            def ff_hidden(b, j):
                dve.wait_ge(ff_hi, b.start + j + 1)
                dve.tensor_tensor(FLO, SCB[0][:, :].rearrange("p (f t) -> p f t", f=2), FHI.bitcast(F32),
                                  ALU.subtract).then_inc(ff_lo, 1)

            def blocks(b):
                split_to(b.base + 3)
                ff_silu_(b, 0)
                split_to(b.base + 4)
                ff_hidden(b, 0)
                split_to(b.base + 6)
                ff_silu_(b, 1)
                split_to(b.base + 7)
                first, last, per = loop_turns(b)
                with dve.Fori(first, last) as i:
                    for n in range(per):
                        j = i * per + n
                        ff_hidden(b, j - 1)
                        for c in (1, 2):
                            lo(b.base + 3 * j + c, (b.base + c) % RING, UNIT)
                        ff_silu_(b, j, False)
                        lo(b.base + 3 * j + 3, (b.base + 3) % RING, UNIT)
                at[0] = b.base + 3 * b.last + 1
                for j in range(b.last, b.n):
                    ff_hidden(b, j - 1)
                    split_to(b.base + min(3 * j + 3, 3 * b.n))
                    ff_silu_(b, j)
                    split_to(b.base + min(3 * j + 4, 3 * b.n))
                ff_hidden(b, b.n - 1)

            def add_blocks(b, l):
                split_to(b.base + 3 * b.n + 1)
                dve.wait_ge(unit_used, b.base + 3 * b.n)
                for n in range(2):
                    for c in range(C):
                        xs = x[:, c, 512 * n:512 * n + 512]
                        ins = dve.tensor_tensor(xs, xs, G[2 * c + n][:, :], ALU.add)
                    ins.then_inc(flag(f"ff_added{l}"), 1)
                split_to(b.base + 3 * b.n + 2)

            dve.wait_ge(flag("positions_in"), 16)
            dve.tensor_copy(pos_r[:, :], pos_i[:, :]).then_inc(flag("positions_float"), 1)
            dve.wait_ge(flag("positions_turned"), 1)
            step(dve.tensor_copy(pos_f[:, :], SCB[0][:, 0:C]))
            dve.tensor_copy(cols[:, 0, :], SCB[0][:, 128:208])
            dve.tensor_copy(cols[:, 1, 0:68], SCB[0][:, 256:324]).then_inc(flag("cols_ready"), 1)

            def angles():
                raw_angle = angle[:, 0]
                for i in range(HALF):
                    freq = float(np.float32(ROPE_THETA) ** np.float32(-2.0 * i / (2 * HALF)))
                    ins = dve.tensor_scalar(raw_angle[:, :, i], pos_f[:, :], freq, None, ALU.mult)
                step(ins)
                two_pi = 2 * math.pi
                part1 = 6.28125
                part2 = round((two_pi - part1) * 2 ** 20) / 2 ** 20
                part3 = two_pi - part1 - part2
                for n, quarter in ((2, 0.0), (3, 0.25)):
                    turn_, r = angle[:, 1], angle[:, n]
                    step(dve.tensor_scalar(turn_, raw_angle, 1 / two_pi, quarter, ALU.mult, ALU.add))
                    step(dve.tensor_scalar(turn_, turn_, 12582912.0, None, ALU.add))
                    step(dve.tensor_scalar(turn_, turn_, -12582912.0, None, ALU.add))
                    step(dve.scalar_tensor_tensor(out=r, in0=turn_, scalar=-part1, in1=raw_angle, op0=ALU.mult, op1=ALU.add))
                    step(dve.scalar_tensor_tensor(out=r, in0=turn_, scalar=-part2, in1=r, op0=ALU.mult, op1=ALU.add))
                    step(dve.scalar_tensor_tensor(out=r, in0=turn_, scalar=-part3, in1=r, op0=ALU.mult, op1=ALU.add))
                    step(dve.tensor_scalar(r, r, quarter * two_pi, None, ALU.add))
                    ins = dve.tensor_scalar(r, r, 3.1415925, -3.1415925, ALU.min, ALU.max)
                    step(ins) if n == 2 else ins.then_inc(flag("angles"), 1)

            for l in range(2):
                s = L[l]
                to_t(s["hturn"], range(4), gain_of(G_MIX[l]), ahi, alo)
                row_scales(f"mix{l}")
                if l == 0:
                    angles()
                    dve.wait_ge(flag("mem_in"), 16)
                    norm(MEMIN, "mem", MEMIN)
                    dve.wait_ge(flag("gains_in"), 16 * 16)
                    dve.wait_ge(flag("masks_ready"), 1)
                    dve.wait_ge(flag("rotation"), 1)

                    def z0(s_, c):
                        return Z0[:, c, s_.c0:s_.c0 + s_.width]

                    in_ = s["in"]
                    va, vq, vk = heads(Z0, AQ, 9, DH), heads(Z0, BQ, 8, DH), heads(Z0, BK, 8, DH)
                    product(in_[0:2], z0)
                    head_norm([(SQA, va, [(va[:, :, 0:8, :], gains[:, N_AQ, :]), (va[:, :, 8:9, :], gains[:, N_AK, :])])],
                              DH, "a")
                    split_to(in_[1].end + RING)
                    rope(heads(Z0, IQ, 9, 32), 4, ROPET)
                    rope(va, HALF, ROPET)
                    product(in_[2:3], z0)
                    head_norm([(SQQ, vq, [(vq, gains[:, N_BQ, :])])], DH, "bq")
                    split_to(in_[2].end + RING)
                    rope(vq, HALF, ROPET)
                    for n in range(4):
                        dve.tensor_copy(COPIES[:, :, 32 * n:32 * n + 32], Z0[:, :, IK:IW])
                    for n in range(2):
                        dve.tensor_copy(COPIES[:, :, P + DH * n:P + DH * n + DH], Z0[:, :, AK:AV])
                    product(in_[3:4], z0)
                    head_norm([(SQK, vk, [(vk, gains[:, N_BK, :])])], DH, "bk")
                    split_to(in_[3].end + RING)
                    rope(vk, HALF, ROPET)
                    dve.sem_inc(flag("qk_ready0"), 1)
                    product(in_[4:5], z0)
                    for b in range(4):
                        dve.wait_ge(turn_act, plan.turn_act[mem_turn + b + 1])
                        for m, (hi_, dst) in enumerate(((bhi, blo), (ahi, alo))):
                            for n in range(2):
                                k = 2 * b + n
                                ins = dve.scalar_tensor_tensor(out=dst[:, k, :], in0=TB[(mem_turn + b) % 2][:, T * n:T * n + T],
                                                               scalar=gain_of(G_SRC[m])(k), in1=hi_[:, k, :].bitcast(F32),
                                                               op0=ALU.mult, op1=ALU.subtract)
                        ins.then_inc(turn_dve, 1)
                    turns(s["qturn"], 8, lambda b: feat[:, 512 * b:512 * b + 512])
                    for n, s_ in enumerate(M[0]["kv"]):
                        for v in range(s_.units):
                            split_to(s_.unit + v + RING)
                            for i in range(8 * n + 4 * v, 8 * n + 4 * v + 4):
                                c, h, g = i // 8, i % 8, s["index"] + i
                                nk = P * (c + 1)
                                dve.wait_ge(exped, g + 1)
                                sc, w = dsa_bias[:, c, 0:nk], Z0[:, c, IW + h:IW + h + 1]
                                if h == 0:
                                    dve.tensor_scalar(sc, relu_out[g % 3][:, 0:nk], w, None, ALU.mult).then_inc(item_masked, 1)
                                else:
                                    dve.scalar_tensor_tensor(out=sc, in0=relu_out[g % 3][:, 0:nk], scalar=w, in1=sc, op0=ALU.mult,
                                                             op1=ALU.add).then_inc(item_masked, 1)
                                dve.wait_ge(item_masked, g + 1)
                        dve.wait_ge(unit_used, s_.end)
                        dve.tensor_copy((memk_rows if n == 0 else memv)[0][:, 1, :], bank_of(s_, 1)).then_inc(slab_dve, 1)

                    def best_keys(c):
                        nk = P * (c + 1)
                        sc = dsa_bias[:, c, 0:nk]
                        step(dve.tensor_tensor(sc, sc, causal[:, c, 0:nk], ALU.add))
                        for _ in range(TOPK // 8):
                            step(dve.max(best8, sc))
                            step(dve.match_replace(out=sc, in_to_replace=best8, in_values=sc, imm_value=TAKEN))
                        step(dve.tensor_scalar(sc, sc, TAKEN, NEG, ALU.not_equal, ALU.mult))
                        step(dve.tensor_tensor(sc, sc, causal[:, c, 0:nk], ALU.add))

                    split_to(M[0]["kv"][-1].end + RING)
                    for c in range(C):
                        best_keys(c)
                        product(M[1]["kv"][c:c + 1], lambda s_, c_: (memk_rows if s_.c0 == 0 else memv)[1][:, c_, :], scale=False)
                    attention(items0(), s["heads"], (2, 3, 0, 1))
                else:
                    product(s["cmp"] + s["gt"] + s["q0"], z1_dst, z1_src)
                    turns(s["cmpkvturn"], 2, lambda b: z[:, 5728 + 512 * b:6240 + 512 * b])
                    dve.memset(VBLK, 0.0)
                    dve.memset(HID, 0.0)
                    step(dve.memset(POST_GROUP, 0.0))
                    dve.wait_ge(turned, s["posturn"] + 1)
                    dve.tensor_copy(POST, TB[s["posturn"] % 2][:, 0:CMP_LEN]).then_inc(turn_dve, 1)
                    vq = [heads(Z1, NQ, 8, DH), heads(Z1, NQ + 512, 8, DH)]
                    vks, vkw = heads(Z1, KSEL, 4, DH), heads(Z1, KWIN, 4, DH)
                    head_norm([(SQ1["q0"], vq[0], [(vq[0], gains[:, N_NQ, :])])], DH, "q0")
                    dve.sem_inc(flag("q_plain1"), 1)
                    product(s["q1"], z1_dst, z1_src)
                    turns(s["q0turn"], 2, lambda b: feat[:, 512 * b:512 * b + 512])
                    head_norm([(SQ1["q1"], vq[1], [(vq[1], gains[:, N_NQ, :])])], DH, "q1")
                    dve.sem_inc(flag("q_plain1"), 1)
                    split_to(s["q1"][-1].end + RING)
                    dve.wait_ge(flag("cmp_w1_done"), 1)
                    dve.tensor_copy(s_t[0:DH, 0:1], SCB[0][0:DH, 60:61])
                    step(dve.tensor_copy(s_t[0:DH, 1:2], SCB[1][0:DH, 60:61]))
                    for n in range(2):
                        ins = dve.tensor_scalar(HID[:, n, :, 0:N_CMP],
                                                SCB[n][0:DH, 0:60].rearrange("p (g n) -> p g n", g=4),
                                                s_t[0:DH, n:n + 1], None, ALU.add)
                    ins.then_inc(flag("cmp_hidden"), 1)
                    dve.wait_ge(flag("cmp_tanh"), 1)
                    step(dve.scalar_tensor_tensor(out=HIT, in0=HIT, scalar=1.0, in1=HID, op0=ALU.add, op1=ALU.mult))
                    step(dve.tensor_scalar(HIT, HIT, 0.5, None, ALU.mult))
                    for j in range(4):
                        ins = dve.tensor_copy(HIV[:, :, j, :], HIT[:, 1, :, :])
                    ins.then_inc(flag("cmp_silu"), 1)
                    rope(vq[0], HALF, ROPET1)
                    product(s["sel"], z1_dst, z1_src)
                    turns(s["q1turn"], 2, lambda b: feat[:, 1024 + 512 * b:1536 + 512 * b])
                    head_norm([(SQ1["sel"], vks, [(vks, gains[:, N_KS, :])])], DH, "sel")
                    split_to(s["sel"][-1].end + RING)
                    dve.wait_ge(flag("cmp_w2_done"), 1)
                    bank = SCB[1]
                    step(dve.tensor_copy(KCN[:, 0, :], bank[:, 0:DH]))
                    step(dve.tensor_tensor(KCN[:, 1, :], KCN[:, 0, :], KCN[:, 0, :], ALU.mult))
                    step(dve.tensor_reduce(s_mean[:, 0:1], KCN[:, 1, :], AX, ALU.add))
                    rsqrt(1, DH)
                    step(dve.tensor_scalar(KCN[:, 0, :], KCN[:, 0, :], s_y[:, 0:1], None, ALU.mult))
                    step(dve.tensor_tensor(KCN[:, 0, :], KCN[:, 0, :], gains[:, N_KC, :], ALU.mult))
                    step(dve.tensor_copy(KCN[:, 1, :], KCN[:, 0, :]))
                    for j in range(4):
                        r = slice(32 * j, 32 * j + 32)
                        ins = dve.tensor_copy(VBLK[r, :, j, :], bank[r, 128:384].rearrange("p (g d) -> p g d", g=4))
                    ins.then_inc(flag("cmp_kv_ready"), 1)
                    rope(vq[1], HALF, ROPET1)
                    rope(vks, HALF, ROPET1)
                    dve.wait_ge(flag("gates_tanh"), 1)
                    step(dve.tensor_scalar(GATE, GATE, 0.5, 0.5, ALU.mult, ALU.add))
                    product(s["win"], z1_dst, z1_src)
                    head_norm([(SQ1["win"], vkw, [(vkw, gains[:, N_KW, :])])], DH, "win")
                    rope(vkw, HALF, ROPET1)
                    dve.sem_inc(flag("qk_ready1"), 1)
                    dve.wait_ge(turned, s["kcturn"] + 1)
                    dve.tensor_copy(KCT, TB[s["kcturn"] % 2][:, 0:P]).then_inc(turn_dve, 1)
                    turns(s["qrturn"], 6, lambda b: feat[:, 2048 + 512 * b:2560 + 512 * b] if b < 5 else KWT)
                    split_to(s["win"][-1].end + RING)
                    for c in range(C):
                        dve.wait_ge(flag("cmp_scored"), c + 1)
                        cs4, cp4 = (b_.rearrange("p (h n) -> p h n", h=16) for b_ in (CS, CP))
                        bias = cmp_bias[:, c, :].unsqueeze(1).broadcast_to([P, 16, 32])
                        keep = cmp_keep[:, c, :].unsqueeze(1).broadcast_to([P, 16, 32])
                        for n in range(2):
                            ins = dve.tensor_scalar(CS.rearrange("p (b a m) -> p b a m", b=2, a=2)[:, :, n, :],
                                                    SCB[n][:, 0:T].rearrange("p (b m) -> p b m", b=2), DH ** -0.5, None, ALU.mult)
                        step(ins)
                        step(dve.tensor_tensor(cs4, cs4, bias, ALU.add))
                        step(dve.tensor_reduce(s_t[:, 0:16], cs4, AX, ALU.max))
                        dve.tensor_tensor(cs4, cs4, s_t[:, 0:16].unsqueeze(2).broadcast_to([P, 16, 32]), ALU.subtract
                                          ).then_inc(flag("cmp_shifted"), 1)
                        dve.wait_ge(flag("cmp_exp"), c + 1)
                        step(dve.tensor_tensor(cp4, cp4, keep, ALU.mult))
                        step(dve.tensor_reduce(s_t[:, 0:16], cp4, AX, ALU.add))
                        step(dve.tensor_scalar(s_t[:, 0:16], s_t[:, 0:16], TINY, None, ALU.max))
                        step(dve.reciprocal(s_u[:, 0:16], s_t[:, 0:16]))
                        gate = GATE[:, c, :].rearrange("p (h b) -> p h b", b=3)[:, :, 0]
                        step(dve.tensor_tensor(s_u[:, 0:16], s_u[:, 0:16], gate, ALU.mult))
                        dve.tensor_tensor(cp4, cp4, s_u[:, 0:16].unsqueeze(2).broadcast_to([P, 16, 32]), ALU.mult
                                          ).then_inc(flag("cmp_prob"), 1)
                        dve.wait_ge(turned, s["cmpturn"] + c + 1)
                        dve.tensor_copy(CPT[c], TB[(s["cmpturn"] + c) % 2][:, :]).then_inc(turn_dve, 1)
                    attention(items1(), s["heads"], (0, 1, 2, 3))
                product(s["out"][0:1], None)
                to_t(s["mturn"], range(2), gain_of(G_MEM[l]), bhi, blo)
                if l == 0:
                    mk = [heads(memk_rows[m], 0, 4, P) for m in range(2)]
                    head_norm([(heads(zv(4944 + 1024 * m, 512), 0, 4, P), mk[m], [(mk[m], mem_k_gain[:, m, :])])
                               for m in range(2)], P, "mk")
                    dve.sem_inc(flag("mem_k_normed"), 1)
                product(s["out"][1:2], None)
                to_t(s["mturn"], range(2, 4), gain_of(G_MEM[l]), bhi, blo)
                row_scales(f"memq{l}")
                product(s["mq"], lambda s_, c: ZM[:, c, :])
                vm = heads(ZM, 0, 4, P)
                head_norm([(heads(zv(2048, 512), 0, 4, P), vm, [(vm, mem_q_gain[:, l, :])])], P, f"memq{l}")
                dve.sem_inc(flag(f"mem_q_ready{l}"), 1)
                turns(s["mqturn"], 2, lambda b: feat[:, 512 * b:512 * b + 512])
                split_to(s["mo"][-1].end)
                attention(items_mem(l), s["mheads"], (0, 1))
                product(s["mo"][0:1], None)
                to_t(s["fturn"], range(2), gain_of(G_FFN[l]), bhi, blo)
                product(s["mo"][1:2], None)
                to_t(s["fturn"], range(2, 4), gain_of(G_FFN[l]), bhi, blo)
                row_scales(f"ffn{l}")
                blocks(s["ff"])
                add_blocks(s["ff"], l)

            to_t(N["hturn"], range(4), gain_of(G_N1), ahi, alo)
            row_scales("mix2")
            lam = cols[:, 1, R_LAM:R_LAM + 8]
            l0, l1, l2, l3 = (LAM[:, i, :] for i in range(4))
            step(dve.tensor_scalar(l0, lam, -1.0, None, ALU.mult))
            dve.tensor_tensor(l1, l0, lam, ALU.min).then_inc(flag("minus_abs_lambda"), 1)
            dve.wait_ge(flag("exp_lambda"), 1)
            step(dve.tensor_scalar(l2, l1, 2.0, None, ALU.add))
            step(dve.reciprocal(l2, l2))
            step(dve.tensor_tensor(l1, l1, l2, ALU.mult))
            step(dve.tensor_tensor(l2, l1, l1, ALU.mult))
            step(dve.tensor_scalar(l3, l2, 1 / 17, 1 / 15, ALU.mult, ALU.add))
            for n in (13, 11, 9, 7, 5, 3, 1):
                step(dve.tensor_tensor(l3, l3, l2, ALU.mult))
                step(dve.tensor_scalar(l3, l3, 1 / n, None, ALU.add))
            step(dve.tensor_tensor(l3, l3, l1, ALU.mult))
            step(dve.tensor_scalar(l0, l0, 0.0, 0.5, ALU.max, ALU.mult))
            step(dve.tensor_tensor(l3, l3, l0, ALU.add))
            step(dve.tensor_scalar(SP4[:, 0:8], l3, 8.0, None, ALU.mult))
            for n, r in enumerate((R_BR, R_BI)):
                step(dve.tensor_scalar(HB[:, n, :], cols[:, 1, r:r + 8], 0.5, None, ALU.mult))
            product(N["in"], lambda s_, c: ZA[:, c, s_.c0:s_.c0 + s_.width])
            dve.sem_inc(flag("z_copied2"), 1)
            turns(N["uturn"], 10, lambda b: feat[:, 512 * b:512 * b + 512])
            split_to(N["in"][-1].end + RING)
            for k in range(8):
                wc = [cols[:, 1, 8 * n + k:8 * n + k + 1] for n in range(4)]
                step(dve.tensor_scalar(XC[:, k, :], ULT[:, k, :], wc[3], cols[:, 1, R_CB + k:R_CB + k + 1], ALU.mult, ALU.add))
                for n in (2, 1, 0):
                    back = 3 - n
                    ins = dve.scalar_tensor_tensor(out=XC[:, k, back:T], in0=ULT[:, k, 0:T - back], scalar=wc[n],
                                                   in1=XC[:, k, back:T], op0=ALU.mult, op1=ALU.add)
                    step(ins) if n else ins.then_inc(flag("convolved"), 1)
            product(N["gates"][0:2], lambda s_, c: ZG[:, c, s_.c0 - GA:s_.c0 - GA + 512])
            dve.wait_ge(turn_act, plan.turn_act[N["gturn"] + 8])
            for k in range(8):
                ins = dve.tensor_scalar(RG[:, k, :], RG[:, k, :], SP4[:, k:k + 1], SP4[:, k:k + 1], ALU.mult, ALU.add)
            ins.then_inc(flag("log_decay"), 1)
            dve.wait_ge(flag("convolved"), 8)
            step(dve.scalar_tensor_tensor(out=XC, in0=IG, scalar=1.0, in1=XC, op0=ALU.add, op1=ALU.mult))
            step(dve.tensor_tensor(IG, UGT, UGT, ALU.mult))
            step(dve.tensor_scalar(IG, IG, 0.044715, 1.0, ALU.mult, ALU.add))
            dve.tensor_tensor(IG, IG, UGT, ALU.mult).then_inc(flag("gelu_inner"), 1)
            product(N["gates"][2:4], lambda s_, c: ZG[:, c, s_.c0 - GA:s_.c0 - GA + 512])
            for g, w in enumerate(POOL_WINDOWS):
                p_, src, span = POOLT[:, g, :], UPT[:, g, :], 1
                tmp = pool_sum
                cur = src
                while span < w:
                    nxt = tmp[0] if cur is not tmp[0] else tmp[1]
                    dve.tensor_copy(nxt[:, 0:span], cur[:, 0:span])
                    step(dve.tensor_tensor(nxt[:, span:T], cur[:, span:T], cur[:, 0:T - span], ALU.add))
                    cur, span = nxt, 2 * span
                dve.tensor_tensor(p_[:, 0:w - 1], cur[:, 0:w - 1], numbers[:, 0:w - 1], ALU.mult)
                step(dve.tensor_scalar(p_[:, w - 1:T], cur[:, w - 1:T], 1.0 / w, None, ALU.mult))
                ins = dve.tensor_tensor(p_, p_, src, ALU.subtract)
                step(ins) if g < 3 else ins.then_inc(flag("pooled"), 1)
            dve.wait_ge(flag("gelu_tanh"), 1)
            step(dve.scalar_tensor_tensor(out=UGT, in0=IG, scalar=1.0, in1=UGT, op0=ALU.add, op1=ALU.mult))
            dve.wait_ge(flag("decay_tanh"), 1)
            step(dve.tensor_tensor(IG, ULT, ULT, ALU.mult))
            dve.scalar_tensor_tensor(out=RG, in0=IG, scalar=1.0, in1=RG, op0=ALU.add, op1=ALU.mult).then_inc(flag("drive_squared"), 1)
            to_t(N["yturn"], range(2), lambda k: cols[:, 1, R_PS + k:R_PS + k + 1], ahi, alo)
            dve.wait_ge(flag("drive_scale"), 1)
            step(dve.tensor_tensor(XC, XC, RG, ALU.mult))
            for k in range(8):
                ins = dve.tensor_tensor_scan(IG[:, k, :], ULT[:, k, :], XC[:, k, :], 0.0, ALU.mult, ALU.add)
            step(ins)
            dve.scalar_tensor_tensor(out=ULT, in0=IG, scalar=0.5, in1=UGT, op0=ALU.mult, op1=ALU.mult).then_inc(flag("lru_out"), 1)
            dve.wait_ge(flag("lru_hi"), 1)
            dve.tensor_tensor(blo[:, :, :], ULT, bhi[:, :, :].bitcast(F32), ALU.subtract).then_inc(flag("lru_done"), 1)
            dve.wait_ge(flag("mix_gates"), 1)

            def mix_a(s_, c):
                g_ = ZG[:, c, s_.c0:s_.c0 + 512]
                dve.scalar_tensor_tensor(out=g_, in0=g_, scalar=1.0, in1=bank_of(s_, c), op0=ALU.add, op1=ALU.mult
                                         ).then_inc(slab_dve, 1)

            def mix_b(s_, c):
                g_, y_ = ZG[:, c, D + s_.c0:D + s_.c0 + 512], ZG[:, c, s_.c0:s_.c0 + 512]
                step(dve.scalar_tensor_tensor(out=g_, in0=g_, scalar=1.0, in1=bank_of(s_, c), op0=ALU.add, op1=ALU.mult))
                dve.tensor_tensor(y_, y_, g_, ALU.add).then_inc(slab_dve, 1)

            product(N["pa"], mix_a)
            product(N["pb"][0:1], mix_b)
            to_t(N["oturn"], range(2), 0.5, ahi, alo)
            product(N["pb"][1:2], mix_b)
            to_t(N["oturn"], range(2, 4), 0.5, ahi, alo)
            product(N["out"][0:1], None)
            to_t(N["h2turn"], range(2), gain_of(G_N2), bhi, blo)
            product(N["out"][1:2], None)
            to_t(N["h2turn"], range(2, 4), gain_of(G_N2), bhi, blo)
            row_scales("moe")

            dve.wait_ge(flag("router_hi"), 1)
            dve.tensor_tensor(rlo[:, :, :], route_w, rhi[:, :, :].bitcast(F32), ALU.subtract).then_inc(flag("router_lo"), 1)
            split_to(N["moe"].base + RING)
            dve.wait_ge(flag("routed"), 1)
            gl, el = rt[:, 0, :, 0:N_GRP], rt[:, 2, :, :]
            lg = SCB[1][:, 0:40].rearrange("p (c n) -> p c n", c=C)
            for c in range(C):
                dve.scalar_tensor_tensor(out=gl[:, c, :], in0=lg[:, c, 0:N_GRP], scalar=row_scale[:, c:c + 1],
                                         in1=route_b[:, 0:N_GRP], op0=ALU.mult, op1=ALU.add)
                ins = dve.scalar_tensor_tensor(out=el[:, c, :], in0=lg[:, c, N_GRP:20], scalar=row_scale[:, c:c + 1],
                                               in1=route_b[:, N_GRP:20], op0=ALU.mult, op1=ALU.add)
            step(ins)
            iota = rt[:, 3, :, :]
            for e in range(N_EXP):
                ins = dve.memset(iota[:, :, e:e + 1], float(e - N_EXP))
            step(ins)

            def first_best(v, n, best, hot, t_):
                step(dve.tensor_reduce(best, v, AX, ALU.max))
                step(dve.tensor_tensor(t_, v, best.broadcast_to([P, C, n]), ALU.is_equal))
                step(dve.tensor_tensor(t_, t_, iota[:, :, 0:n], ALU.mult))
                step(dve.tensor_reduce(rt[:, 11, :, 0:1], t_, AX, ALU.min))
                step(dve.tensor_tensor(hot, iota[:, :, 0:n], rt[:, 11, :, 0:1].broadcast_to([P, C, n]), ALU.is_equal))

            gbest, ghot = rt[:, 4, :, 0:1], rt[:, 5, :, 0:N_GRP]
            first_best(gl, N_GRP, gbest, ghot, rt[:, 10, :, 0:N_GRP])
            dve.tensor_tensor(gl, gl, gbest.broadcast_to([P, C, N_GRP]), ALU.subtract).then_inc(flag("group_shifted"), 1)
            dve.wait_ge(flag("group_exp"), 1)
            step(dve.tensor_reduce(rt[:, 4, :, 1:2], rt[:, 1, :, 0:N_GRP], AX, ALU.add))
            p_top = rt[:, 4, :, 2:3]
            step(dve.reciprocal(p_top, rt[:, 4, :, 1:2]))
            g16 = rt[:, 6, :, :]
            for g in range(N_GRP):
                ins = dve.tensor_copy(g16[:, :, PER_GRP * g:PER_GRP * g + PER_GRP], ghot[:, :, g:g + 1].broadcast_to([P, C, PER_GRP]))
            step(ins)
            step(dve.tensor_tensor(el, el, g16, ALU.mult))
            step(dve.tensor_scalar(g16, g16, -NEG, NEG, ALU.mult, ALU.add))
            step(dve.tensor_tensor(el, el, g16, ALU.add))
            best1, hot1, best2, hot2 = rt[:, 4, :, 3:4], rt[:, 7, :, :], rt[:, 4, :, 4:5], rt[:, 6, :, :]
            first_best(el, N_EXP, best1, hot1, rt[:, 10, :, :])
            step(dve.tensor_scalar(hot2, hot1, 3 * NEG, None, ALU.mult))
            step(dve.tensor_tensor(el, el, hot2, ALU.add))
            first_best(el, N_EXP, best2, hot2, rt[:, 10, :, :])
            dve.tensor_tensor(rt[:, 8, :, 0:1], best2, best1, ALU.subtract).then_inc(flag("expert_gap"), 1)
            dve.wait_ge(flag("expert_exp"), 1)
            e_, w1, w2_ = rt[:, 9, :, 0:1], rt[:, 9, :, 1:2], rt[:, 9, :, 2:3]
            step(dve.tensor_scalar(w1, e_, 1.0, None, ALU.add))
            step(dve.reciprocal(w1, w1))
            step(dve.tensor_tensor(w1, w1, p_top, ALU.mult))
            step(dve.tensor_tensor(w2_, w1, e_, ALU.mult))
            step(dve.tensor_tensor(hot1, hot1, w1.broadcast_to([P, C, N_EXP]), ALU.mult))
            step(dve.tensor_tensor(hot2, hot2, w2_.broadcast_to([P, C, N_EXP]), ALU.mult))
            step(dve.tensor_tensor(hot1, hot1, hot2, ALU.add))
            for n in range(2):
                for c in range(C):
                    ins = dve.tensor_scalar(half_comb.rearrange("p c (e n) -> p c e n", n=2)[:, c, :, n], hot1[:, c, :],
                                            half_scale2[:, c:c + 1], None, ALU.mult)
            step(ins)
            blocks(N["moe"])
            add_blocks(N["moe"], 2)
            dve.wait_ge(flag("ff_added2"), 2)
            norm(x, "final")
            dve.wait_ge(flag("normed_final"), 1)
            dve.wait_ge(flag("final_gain_in"), 16)
            for c in range(C):
                dve.tensor_tensor(XN[:, c, :], XN[:, c, :], final_gain, ALU.mult).then_inc(flag("out_ready"), 1)

        @block.tensor
        def _(pe):
            def mm3(dst, lhi, llo, rhi_, rlo_, start, stop):
                pe.matmul(dst, lhi, rhi_, start=start, stop=False)
                pe.matmul(dst, lhi, rlo_, start=False, stop=False)
                return pe.matmul(dst, llo, rhi_, start=False, stop=stop)

            def unit_ready(u):
                pe.wait_ge(lo_dve, u + 1)
                pe.wait_ge(lo_pool, u + 1)

            def product(slabs, lhi, llo, between=None, left=None):
                group = 0
                for s in slabs:
                    if s.index >= 2:
                        before = plan.slabs[s.index - 2]
                        pe.wait_ge(slab_act, before.done_act)
                        pe.wait_ge(slab_dve, before.done_dve)
                    for i in range(s.units):
                        u, nk = s.unit + i, min(4, s.k)
                        unit_ready(u)
                        if left is not None:
                            emptied(left + 2 * i + 2)
                        wh, wl = (w[u % RING][:, 0:nk * s.width].rearrange("p (k n) -> p k n", k=nk) for w in (whi, wlo))
                        for c in range(C):
                            if between:
                                between(group)
                            group += 1
                            for k in range(nk):
                                kk = 4 * i + k
                                ins = mm3(bank_of(s, c), lhi[:, kk, P * c:P * c + P], llo[:, kk, P * c:P * c + P],
                                          wh[:, k, :], wl[:, k, :], kk == 0, kk == s.k - 1)
                        ins.then_inc(unit_used, 1)

            def turn_free(n):
                if n >= 2:
                    if plan.turn_act[n - 1]:
                        pe.wait_ge(turn_act, plan.turn_act[n - 1])
                    if plan.turn_dve[n - 1]:
                        pe.wait_ge(turn_dve, plan.turn_dve[n - 1])
                return turn_bank(n)

            def emptied(n):
                pe.wait_ge(turn_act, plan.turn_act[n]) if plan.turn_act[n] else None
                pe.wait_ge(turn_dve, plan.turn_dve[n]) if plan.turn_dve[n] else None

            def to_t(base, nk, src):
                for b in range(nk // 2):
                    bank = turn_free(base + b)
                    for n in range(2):
                        for c in range(C):
                            ins = pe.transpose(bank[:, T * n + P * c:T * n + P * c + P], src(c, 2 * b + n), ident[:, :])
                    ins.then_inc(turned, 1)
                emptied(base + nk // 2)

            def half_t(base, part, src, sem_, count):
                pe.wait_ge(sem_, count)
                for b in (2 * part, 2 * part + 1):
                    bank = turn_free(base + b)
                    for n in range(2):
                        for c in range(C):
                            ins = pe.transpose(bank[:, T * n + P * c:T * n + P * c + P], src(c, 2 * b + n), ident[:, :])
                    ins.then_inc(turned, 1)

            def turns(base, jobs):
                for b in range(len(jobs) // 2):
                    bank = turn_free(base + b)
                    for n in range(2):
                        for c in range(C):
                            ins = pe.transpose(bank[:, T * n + P * c:T * n + P * c + P], jobs[2 * b + n](c), ident[:, :])
                    ins.then_inc(turned, 1)
                emptied(base + len(jobs) // 2)

            def attention(items, run):
                n = run.n
                for t in range(n + 4):
                    if t < n:
                        it, g = items[t], run.first + t
                        if g >= 2:
                            pe.wait_ge(item_masked, g - 1)
                        for m, b_ in enumerate(it.branches):
                            ins = pe.matmul(SCB[g % 2][:, it.at[m]:it.at[m] + b_.nk], b_.q, b_.k, start=True, stop=True)
                        ins.then_inc(scored, 1)
                    if 0 <= t - 3 < n:
                        i = t - 3
                        pe.wait_ge(prob_scaled, run.outs + i + 1)
                        bank = turn_free(run.batch + i)
                        for b in range(items[i].width // P):
                            ins = pe.transpose(bank[:, P * b:P * b + P], run.prob[(run.first + i) % 4][:, P * b:P * b + P], ident[:, :])
                        ins.then_inc(turned, 1)
                    if 0 <= t - 4 < n:
                        i = t - 4
                        it = items[i]
                        pe.wait_ge(turn_dve, plan.turn_dve[run.batch + i + 1])
                        if it.first:
                            pe.matmul(it.branches[0].out, it.first[0], it.first[1], start=True, stop=False)
                        for m, b_ in enumerate(it.branches):
                            for b, v in enumerate(b_.v):
                                a_ = it.at[m] + P * b
                                ins = pe.matmul(b_.out, v, run.probt[i % 2][:, a_:a_ + P], start=b == 0 and not it.first,
                                                stop=b == len(b_.v) - 1 and (m == 1 or not it.first))
                        ins.then_inc(pved, 1)
                pe.wait_ge(heads_lo, run.banks + n // run.per)

            def ff_up(b, j, static=True, between=None):
                u0 = b.base + 3 * j - (0 if isinstance(j, int) and j == 0 else 1)
                s0 = b.base % RING if isinstance(j, int) and j == 0 else (b.base - 1) % RING
                if not static or b.start + j >= 1:
                    pe.wait_ge(ff_silu, b.start + j)
                for half_ in range(2):
                    unit_ready(u0 + half_)
                    if between and half_:
                        emptied(b.left + 4)
                    slot = (s0 + half_) % RING
                    for c in range(C):
                        if between and half_ == 0 and c == 1:
                            between()
                        for k in range(4):
                            kk = 4 * half_ + k
                            ins = mm3(TB[c][:, :], bhi[:, kk, P * c:P * c + P], blo[:, kk, P * c:P * c + P],
                                      whi[slot][:, 512 * k:512 * k + 512], wlo[slot][:, 512 * k:512 * k + 512],
                                      kk == 0, kk == KC - 1)
                    ins.then_inc(unit_used, 1)

            def ff_turn(b, j, static=True):
                n = b.start + j
                pe.wait_ge(ff_silu, n + 1)
                if not static or n >= 1:
                    pe.wait_ge(ff_lo, n)
                for f in range(2):
                    for c in range(C):
                        ins = pe.transpose(SCB[0][:, T * f + P * c:T * f + P * c + P], silu[:, c, 1, P * f:P * f + P], ident[:, :])
                ins.then_inc(ff_turned, 1)

            def ff_down(b, j, slot, first=False, last=False, u=None):
                pe.wait_ge(ff_lo, b.start + j + 1)
                unit_ready(u)
                for c in range(C):
                    for f in range(2):
                        for n in range(2):
                            w = slice(D * f + 512 * n, D * f + 512 * n + 512)
                            ins = mm3(G[2 * c + n][:, :], ahi[:, f, P * c:P * c + P], alo[:, f, P * c:P * c + P],
                                      whi[slot][:, w], wlo[slot][:, w], first and f == 0, last and f == 1)
                ins.then_inc(unit_used, 1)

            def blocks(b, between=None):
                s = (b.base + 1) % RING
                ff_up(b, 0, between=between)
                ff_turn(b, 0)
                ff_up(b, 1)
                ff_down(b, 0, s, first=True, u=b.base + 4)
                first, last, per = loop_turns(b)
                with pe.Fori(first, last) as i:
                    for n in range(per):
                        j = i * per + n
                        ff_turn(b, j - 1, False)
                        ff_up(b, j, False)
                        ff_down(b, j - 1, s, u=b.base + 3 * j + 1)
                for j in range(b.last, b.n):
                    ff_turn(b, j - 1)
                    ff_up(b, j)
                    ff_down(b, j - 1, s, u=b.base + 3 * j + 1)
                ff_turn(b, b.n - 1)
                ff_down(b, b.n - 1, (b.base + 3 * b.n - 1) % RING, last=True, u=b.base + 3 * b.n - 1)

            pe.wait_ge(flag("masks_ready"), 1)
            pe.wait_ge(flag("positions_float"), 1)
            pe.wait_ge(flag("rows_in"), 16 * 16)
            pe.transpose(SCB[0][:, 0:C], pos_r[:, :], ident[0:C, 0:C])
            pe.transpose(SCB[0][:, 128:208], rows[:, 0, :], ident[0:80, 0:80])
            pe.transpose(SCB[0][:, 256:324], rows[0:68, 1, :], ident[0:68, 0:68]).then_inc(flag("positions_turned"), 1)

            for l in range(2):
                s = L[l]
                if l == 0:
                    pe.wait_ge(flag("x_in"), 16)
                    to_t(s["hturn"], KC, xsrc)
                    product(s["in"], ahi, alo)
                    pe.wait_ge(flag("normed_mem"), 1)
                    to_t(mem_turn, KC, lambda c, k: MEMIN[:, c, P * k:P * k + P])
                    pe.wait_ge(flag("qk_ready0"), 1)
                    turns(s["qturn"], JOBS0)
                    index_item = [0]

                    def two_logits(group):
                        for i in range(index_item[0], index_item[0] + 2):
                            c, h, g = i // 8, i % 8, s["index"] + i
                            r = slice(32 * (h % 4), 32 * (h % 4) + 32)
                            if i >= 2:
                                pe.wait_ge(exped, g - 1)
                            pe.matmul(SCB[g % 2][:, 0:P * (c + 1)], feat[r, T * (h // 4) + P * c:T * (h // 4) + P * c + P],
                                      feat[r, 512:512 + P * (c + 1)], start=True, stop=True,
                                      tile_position=(32 * (h % 4), 0)).then_inc(scored, 1)
                        index_item[0] += 2

                    product(M[0]["kv"], bhi, blo, two_logits)
                    product(M[1]["kv"], ahi, alo)
                    pe.wait_ge(slab_act, M[1]["kv"][-1].done_act)
                    pe.wait_ge(slab_dve, M[1]["kv"][-1].done_dve)
                    attention(items0(), s["heads"])
                else:
                    half_t(s["hturn"], 0, xsrc, flag("ff_added0"), 1)
                    product(s["cmp"] + s["gt"] + s["q0"], ahi, alo, left=s["hturn"], between=lambda group:
                            half_t(s["hturn"], 1, xsrc, flag("ff_added0"), 2) if group == 1 else None)
                    pe.wait_ge(slab_act, s["cmp"][-1].done_act)
                    pe.wait_ge(slab_dve, s["cmp"][-1].done_dve)
                    turns(s["cmpkvturn"], JOBSC)
                    bank = turn_free(s["posturn"])
                    pe.transpose(bank[:, 0:CMP_LEN], pos_rows[:, :], ident[0:CMP_LEN, 0:CMP_LEN]).then_inc(turned, 1)
                    product(s["q1"], ahi, alo)
                    pe.wait_ge(flag("q_plain1"), 1)
                    turns(s["q0turn"], JOBSQ[0:4])
                    emptied(s["posturn"] + 1)
                    pe.wait_ge(flag("cmp_weights_in"), 32)
                    for n in range(2):
                        r = slice(DH * n, DH * n + DH)
                        for j in range(CMP_LEN):
                            ins = pe.matmul(SCB[n][0:DH, 0:75].rearrange("p (g n) -> p g n", g=5), CMPW[r, j, :],
                                            KCVT[r, :, j:j + CMP_STRIDE * (N_CMP - 1) + 1:CMP_STRIDE], start=j == 0, stop=j == CMP_LEN - 1)
                    ins.then_inc(flag("cmp_w1_done"), 1)
                    product(s["sel"], ahi, alo)
                    pe.wait_ge(flag("cmp_silu"), 1)
                    pe.matmul(SCB[1][:, 0:DH], HIT[:, 0, :, :].rearrange("p g n -> p (g n)"), w2[:, 0, :], start=True, stop=True)
                    for g in range(4):
                        ins = pe.matmul(SCB[1][:, 128 + DH * g:128 + DH * g + DH],
                                        HIV[:, g, :, :].rearrange("p j n -> p (j n)"), w2[:, 1, :], start=True, stop=True)
                    ins.then_inc(flag("cmp_w2_done"), 1)
                    pe.wait_ge(flag("q_plain1"), 2)
                    turns(s["q1turn"], JOBSQ[4:8])
                    product(s["win"], ahi, alo)
                    pe.wait_ge(flag("cmp_kv_ready"), 1)
                    bank = turn_free(s["kcturn"])
                    pe.transpose(bank[:, 0:P], KCN.rearrange("p a d -> p (a d)"), ident[:, :]).then_inc(turned, 1)
                    emptied(s["kcturn"] + 1)
                    pe.wait_ge(flag("qk_ready1"), 1)
                    turns(s["qrturn"], JOBSR)
                    for c in range(C):
                        if c:
                            pe.wait_ge(flag("cmp_shifted"), c)
                        for h in range(16):
                            (jq, half_), g = place1(h), h // 4
                            r = slice(DH * half_, DH * half_ + DH)
                            at_ = P * (g // 2) + 32 * (h % 4)
                            ins = pe.matmul(SCB[half_][:, at_:at_ + 32], feat[r, T * jq + P * c:T * jq + P * c + P],
                                            KCT[r, 32 * g:32 * g + 32], start=True, stop=True)
                        ins.then_inc(flag("cmp_scored"), 1)
                        pe.wait_ge(flag("cmp_prob"), c + 1)
                        bank = turn_free(s["cmpturn"] + c)
                        for g in range(4):
                            ins = pe.transpose(bank[:, P * g:P * g + P], CP[:, P * g:P * g + P], ident[:, :])
                        ins.then_inc(turned, 1)
                        emptied(s["cmpturn"] + c + 1)
                    attention(items1(), s["heads"])
                product(s["out"], ahi, alo, between=lambda group:
                        half_t(s["mturn"], 0, xsrc, slab_dve, s["out"][0].done_dve) if group == 6 else None)
                product(s["mq"], bhi, blo, left=s["mturn"], between=lambda group:
                        half_t(s["mturn"], 1, xsrc, slab_dve, s["out"][1].done_dve) if group == 1 else None)
                if l == 0:
                    pe.wait_ge(flag("mem_k_normed"), 1)
                    for m in range(2):
                        turns(M[m]["kturn"], [lambda c, h=h: memk_rows[m][:, c, P * h:P * h + P] for h in range(4)])
                pe.wait_ge(flag(f"mem_q_ready{l}"), 1)
                turns(s["mqturn"], JOBSM)
                attention(items_mem(l), s["mheads"])
                product(s["mo"], ahi, alo, between=lambda group:
                        half_t(s["fturn"], 0, xsrc, slab_dve, s["mo"][0].done_dve) if group == 3 else None)
                s["ff"].left = s["fturn"]
                emptied(s["fturn"] + 2)
                blocks(s["ff"], lambda: half_t(s["fturn"], 1, xsrc, slab_dve, s["mo"][1].done_dve))

            half_t(N["hturn"], 0, xsrc, flag("ff_added1"), 1)
            product(N["in"], ahi, alo, left=N["hturn"], between=lambda group:
                    half_t(N["hturn"], 1, xsrc, flag("ff_added1"), 2) if group == 1 else None)
            pe.wait_ge(flag("z_copied2"), 1)
            pe.wait_ge(slab_act, N["in"][-1].done_act)
            turns(N["uturn"], [lambda c, k=k: ZA[:, c, P * k:P * k + P] for k in [4, 5, 6, 7, 8, 9, 10, 11, 0, 1, 2, 3] + list(range(12, 20))])
            product(N["gates"][0:2], ahi, alo)
            pe.wait_ge(flag("gate_weights_in"), 80)
            for k in range(8):
                pe.wait_ge(flag("convolved"), k + 1)
                bank = turn_free(N["gturn"] + k)
                for n in range(2):
                    ins = pe.matmul(bank[:, T * n:T * n + T], GATEW[:, n, k, :], XC[:, k, :], start=True, stop=True)
                ins.then_inc(turned, 1)
            product(N["gates"][2:4], ahi, alo)
            pe.wait_ge(flag("pooled"), 1)
            for b in range(2):
                bank = turn_free(N["yturn"] + b)
                for n in range(2):
                    ins = pe.matmul(bank[:, T * n:T * n + T], POOLW[:, 2 * b + n, :], POOLT[:, 2 * b + n, :], start=True, stop=True)
                ins.then_inc(turned, 1)
            emptied(N["yturn"] + 2)
            product(N["pa"], ahi, alo)
            pe.wait_ge(flag("lru_done"), 1)
            product(N["pb"], bhi, blo, between=lambda group:
                    half_t(N["oturn"], 0, ysrc, slab_dve, N["pb"][0].done_dve) if group == 6 else None)

            def out2_between(group):
                if group == 1:
                    half_t(N["oturn"], 1, ysrc, slab_dve, N["pb"][1].done_dve)
                if group == 6:
                    half_t(N["h2turn"], 0, xsrc, slab_dve, N["out"][0].done_dve)

            product(N["out"], ahi, alo, left=N["oturn"], between=out2_between)
            half_t(N["h2turn"], 1, xsrc, slab_dve, N["out"][1].done_dve)
            emptied(N["h2turn"] + 4)
            pe.wait_ge(flag("router_lo"), 1)
            for c in range(C):
                for k in range(KC):
                    ins = mm3(SCB[1][:, 20 * c:20 * c + 20], bhi[:, k, P * c:P * c + P], blo[:, k, P * c:P * c + P],
                              rhi[:, k, :], rlo[:, k, :], k == 0, k == KC - 1)
            ins.then_inc(flag("routed"), 1)
            blocks(N["moe"])


_INS = ["x", "mem", "positions", "norm_mix", "norm_mem", "norm_mem_src", "norm_ffn", "ab_w_in", "ab_w_out",
        "dsa_q_norm", "dsa_k_norm", "moba_q_norm", "moba_k_norm", "nsa_w_in", "nsa_w_out", "nsa_q_norm",
        "nsa_kcmp_norm", "nsa_ksel_norm", "nsa_kwin_norm", "nsa_cmp_pos_k", "nsa_cmp_pos_v", "nsa_cmp_w1_k",
        "nsa_cmp_w2_k", "nsa_cmp_w1_v", "nsa_cmp_w2_v", "mem_w_q", "mem_w_kv", "mem_w_o", "mem_q_norm",
        "mem_k_norm", "ffn_w_in", "ffn_w_out", "norm1_g_2", "w_in_2", "pool_w_2", "pool_scale_2", "conv_w_2",
        "conv_b_2", "rg_w_r_2", "rg_b_r_2", "rg_w_i_2", "rg_b_i_2", "rg_lambda_2", "proj_a_2", "proj_b_2",
        "w_out_2", "norm2_g_2", "router_group_w_2", "router_group_b_2", "router_expert_w_2",
        "router_expert_b_2", "exp_w_gate_2", "exp_w_up_2", "exp_w_down_2", "norm_f_g_2"]


def kernel(**inputs):
    import concourse.bacc as bacc
    from concourse.bass_utils import run_bass_kernel_spmd

    nc = bacc.Bacc("TRN2", target_bir_lowering=False, num_devices=1)
    arrays, aps = {}, {}
    for name in _INS:
        v = np.ascontiguousarray(inputs[name])
        arrays[f"in_{name}"] = v
        aps[name] = nc.dram_tensor(f"in_{name}", v.shape, mybir.dt.from_np(v.dtype), kind="ExternalInput").ap()
    out = nc.dram_tensor("out_0", (1, T, D), F32, kind="ExternalOutput").ap()
    build(nc, aps, out)
    r = run_bass_kernel_spmd(nc, [arrays], core_ids=[0])
    return r.results[0]["out_0"]
```

```python
from contextlib import ExitStack
import math
import numpy as np
import concourse.bass as bass
from concourse import mybir

F32 = mybir.dt.float32
F32R = mybir.dt.float32r
I32 = mybir.dt.int32
ALU = mybir.AluOpType
ACT = mybir.ActivationFunctionType
AX = mybir.AxisListType.X

P = 128
T = 256
C = T // P
D = 1024
KC = D // P
DH = 64
FF = 2816
FB = 256
RING = 3
UNIT = 2048
LO_DVE = 768
EPS = 1e-6
NEG = -1e30
TAKEN = -3e38
TINY = 1e-20
ROPE_THETA = 500000.0
HALF = 8
N_CMP = 15
CMP_LEN, CMP_STRIDE = 32, 16
N_EXP, N_GRP, PER_GRP = 16, 4, 4
TOPK = 64
POOL_WINDOWS = (2, 4, 8, 16)

AQ, AK, AV, IQ, IK, IW, BQ, BK, BV, AB_W = 0, 512, 576, 640, 896, 928, 936, 1448, 1960, 2472
NQ, KCMP, VCMP, KSEL, VSEL, KWIN, VWIN, GT, C_W = 0, 1024, 1280, 1536, 1792, 2048, 2304, 2560, 2608
UL, UP, UG, GA, GB, IN_W = 512, 0, 1536, 2560, 3584, 4608

G_MIX, G_MEM, G_SRC, G_FFN, G_N1, G_N2 = (0, 1), (2, 3), (4, 5), (6, 7), 8, 9
R_CONV, R_CB, R_BR, R_BI, R_LAM, R_PS = 0, 32, 40, 48, 56, 64
N_AQ, N_AK, N_BQ, N_BK, N_NQ, N_KC, N_KS, N_KW = range(8)


class Chain:

    def __init__(self, eng, sem):
        self.eng, self.sem, self.n, self.turn = eng, sem, 0, 0

    def __call__(self, ins):
        self.n += 1
        ins.then_inc(self.sem, 1)
        self.eng.wait_ge(self.sem, self.n + self.turn)


class Slab:

    def __init__(self, w, c0, width, k, evac, unit, index, done_act, done_dve):
        self.w, self.c0, self.width, self.k, self.evac = w, c0, width, k, evac
        self.unit, self.units, self.index = unit, -(-k // 4), index
        self.end = unit + self.units
        self.done_act, self.done_dve = done_act, done_dve
        self.order = range(self.units)


class Plan:

    def __init__(self):
        self.slabs, self.loads, self.width, self.dmas = [], [], [], []
        self.act = self.dve = 0
        self.turns, self.turn_act, self.turn_dve = 0, [0], [0]
        self.turn_in_scores = set()
        self.items = self.outs = self.emptied = 0

    def product(self, w, width, k=KC, evac="both", first=0):
        out = []
        for c0 in range(first, first + width, 512):
            n = min(512, first + width - c0)
            self.act += evac == "both"
            self.dve += 1 if evac == "both" else 2
            s = Slab(w, c0, n, k, evac, len(self.width), len(self.slabs), self.act, self.dve)
            self.slabs.append(s)
            self.loads.append(s)
            self.width += [min(4, k) * n] * s.units
            self.dmas += [1] * s.units
            out.append(s)
        return out

    def blocks(self, n, per, dmas, load):
        b = Blocks(n, per, len(self.width), load, dmas)
        self.loads.append(b)
        self.width += [UNIT] * (3 * n)
        self.dmas += [dmas, dmas] + [dmas, dmas, 1] * (n - 1) + [1]
        return b

    def turn(self, n, act, dve):
        base = self.turns
        for _ in range(n):
            self.turn_act.append(self.turn_act[-1] + act)
            self.turn_dve.append(self.turn_dve[-1] + dve)
        self.turns += n
        return base

    def item(self, n):
        self.items += n
        return self.items - n

    def attention(self, n, per, tiles):
        run = Run(n, per, self.item(n), self.outs, self.turn(n, 0, 1), self.emptied, tiles)
        self.outs += n
        self.emptied += n // per
        return run

    def landed(self, u):
        return 16 * sum(self.dmas[v] for v in range(u % RING, u + 1, RING))


class Blocks:

    def __init__(self, n, per, base, load, dmas):
        self.n, self.per, self.base, self.load, self.dmas = n, per, base, load, dmas
        self.first, self.last = 2, n - per if (n - 2) % per == 0 and per > 1 else n - 1


class Run:

    def __init__(self, n, per, first, outs, batch, banks, tiles):
        self.prob, self.masked, self.probt = tiles
        self.n, self.per, self.first, self.outs, self.batch, self.banks = n, per, first, outs, batch, banks


class Branch:

    def __init__(self, q, k, nk, bias, v, out):
        self.q, self.k, self.nk, self.bias, self.v, self.out = q, k, nk, bias, v, out


class Item:

    def __init__(self, branches, scale, weight=None, first=None):
        self.branches, self.scale, self.weight, self.first = branches, scale, weight, first
        self.at = (0, branches[0].nk)
        self.width = branches[0].nk + branches[1].nk


def build(nc, a, out):
    ctx = ExitStack()
    with ctx:
        def sb(name, shape, dt=F32):
            return ctx.enter_context(nc.sbuf_tensor("t_" + name, shape, dt))

        def sem(name):
            return ctx.enter_context(nc.semaphore(name))

        flags = {}

        def flag(name):
            if name not in flags:
                flags[name] = sem(name)
            return flags[name]

        raw = [sb(f"raw{i}", [P, UNIT]) for i in range(RING)]
        whi = [sb(f"whi{i}", [P, UNIT], F32R) for i in range(RING)]
        wlo = [sb(f"wlo{i}", [P, UNIT], F32R) for i in range(RING)]
        x = sb("x", [P, C, D])
        ahi, alo = sb("ahi", [P, KC, T], F32R), sb("alo", [P, KC, T], F32R)
        bhi, blo = sb("bhi", [P, KC, T], F32R), sb("blo", [P, KC, T], F32R)
        z = sb("z", [P, 9216])
        feat = sb("feat", [P, 5120])
        memo = sb("memo", [P, 4096])
        rows = feat[0:80, 2560:2816].rearrange("r (a n) -> r a n", a=2)
        final_gain = feat[:, 0:D]
        cols = sb("cols", [P, 2, 80])
        ident = sb("ident", [P, P])
        causal = sb("causal", [P, C, T])
        zero = sb("zero", [P, T])
        cmp_bias, cmp_keep = sb("cmp_bias", [P, C, 32]), sb("cmp_keep", [P, C, 32])
        shared = sb("shared", [P, 2600])
        dsa_bias = shared[:, 0:512].rearrange("p (c t) -> p c t", c=C)
        relu_out = [shared[:, 1024 + T * i:1024 + T * (i + 1)] for i in range(3)]
        pool_sum = [shared[:, 512 + T * i:512 + T * (i + 1)] for i in range(2)]

        def tiles(buffer, first, n):
            return [buffer[:, first + 512 * i:first + 512 * i + 512] for i in range(n)]

        TILES = (tiles(z, 4944, 4), tiles(z, 6992, 2), tiles(feat, 4096, 2))
        TILES1 = (tiles(feat, 0, 4), tiles(z, 5728, 2), tiles(shared, 512, 2))
        best8 = shared[:, 2336:2344]
        item_min, item_sum, item_inv = (sb(n, [P, 64]) for n in ("item_min", "item_sum", "item_inv"))
        s_mean, s_y, s_t, s_u = (sb(n, [P, 64]) for n in ("s_mean", "s_y", "s_t", "s_u"))
        row_scale, half_scale, half_scale2 = (sb(n, [P, C]) for n in ("row_scale", "half_scale", "half_scale2"))
        mem_scale = sb("mem_scale", [P, C])
        s_bits = sb("s_bits", [P, 64], I32)
        cosine, sine = sb("cosine", [P, C, HALF]), sb("sine", [P, C, HALF])
        pos_i, pos_r, pos_f = sb("pos_i", [C, P], I32), sb("pos_r", [C, P]), sb("pos_f", [P, C])
        angle = sb("angle", [P, 5, C, HALF])
        gains = sb("gains", [P, 8, DH])
        mem_q_gain, mem_k_gain = sb("mem_q_gain", [P, 2, P]), sb("mem_k_gain", [P, 2, P])
        silu = shared[:, 0:1024].rearrange("p (c a f) -> p c a f", c=C, a=2)
        route_w = shared[:, 1024:1184].rearrange("p (k n) -> p k n", k=KC)
        rt = shared[:, 1184:1568].rearrange("p (a c n) -> p a c n", a=12, c=C)
        half_comb = shared[:, 1568:1632].rearrange("p (c n) -> p c n", c=C)
        route_b = shared[:, 1632:1652]
        rhi, rlo = sb("rhi", [P, KC, 20], F32R), sb("rlo", [P, KC, 20], F32R)
        w2 = shared[0:DH, 2344:2472].rearrange("p (a e) -> p a e", a=2)
        pos_rows = shared[0:CMP_LEN, 2472:2600]
        numbers, sumsq = sb("numbers", [P, 16]), sb("sumsq", [P, 2 * C])

        psum = [ctx.enter_context(nc.psum_tensor(f"bank{i}", [P, 512], F32)) for i in range(8)]
        G, TB, SCB = psum[0:4], psum[4:6], psum[6:8]
        memk = [memo[:, 2048 * i:2048 * i + 1024].rearrange("p (h t) -> p h t", h=4) for i in range(2)]
        memk_rows = [memo[:, 2048 * i:2048 * i + 1024].rearrange("p (c n) -> p c n", c=C) for i in range(2)]
        memv = [memo[:, 2048 * i + 1024:2048 * i + 2048].rearrange("p (c n) -> p c n", c=C) for i in range(2)]

        def zv(off, width):
            return z[:, off:off + C * width].rearrange("p (c n) -> p c n", c=C)

        def heads(view, first, n, d):
            return view[:, :, first:first + n * d].rearrange("p c (h d) -> p c h d", d=d)

        raw_loaded = [sem(f"raw_loaded{i}") for i in range(RING)]
        hi_done, lo_dve, lo_pool, unit_used = (sem(n) for n in ("hi_done", "lo_dve_done", "lo_pool_done", "unit_used"))
        slab_act, slab_dve = sem("slab_emptied_act"), sem("slab_emptied_dve")
        turned, turn_act, turn_dve = sem("turned"), sem("turn_emptied_act"), sem("turn_emptied_dve")
        scored, item_masked, exped = sem("scored"), sem("item_masked"), sem("exped")
        item_weighed, prob_scaled, pved = sem("item_weighed"), sem("prob_scaled"), sem("pved")
        heads_hi, heads_lo = sem("heads_hi"), sem("heads_lo")
        dve_step, act_step, pool_step = sem("dve_step"), sem("act_step"), sem("pool_step")
        ff_tanh, ff_silu, ff_turned, ff_hi, ff_lo = (sem(n) for n in ("ff_tanh", "ff_silu", "ff_turned", "ff_hi", "ff_lo"))

        plan = Plan()
        L = [{}, {}]
        M = [{}, {}]
        for l in range(2):
            s = L[l]
            s["hturn"] = plan.turn(4, 1, 1)
            if l == 0:
                s["in"] = plan.product(a["ab_w_in"][0], AB_W)
            else:
                w = a["nsa_w_in"][0]
                s["cmp"] = plan.product(w, 512, first=KCMP)
                s["keys"] = plan.product(w, 512, first=VSEL) + plan.product(w, 256, first=KSEL)
                s["q0"], s["q1"] = plan.product(w, 512), plan.product(w, 512, first=512)
                s["vg"] = plan.product(w, C_W - VWIN, first=VWIN)
            if l == 0:
                mem_turn = plan.turn(4, 1, 1)
                s["qturn"] = plan.turn(8, 0, 1)
                s["index"] = plan.item(16)
                for m in range(2):
                    M[m]["kv"] = plan.product(a["mem_w_kv"][m], 1024)
                s["heads"] = plan.attention(16, 4, TILES)
            else:
                s["cmpkvturn"] = plan.turn(2, 0, 1)
                s["posturn"] = plan.turn(1, 0, 1)
                s["q0turn"], s["q1turn"] = plan.turn(2, 0, 1), plan.turn(2, 0, 1)
                s["qrturn"] = plan.turn(4, 0, 1)
                s["kcturn"] = plan.turn(1, 0, 1)
                s["qrturn2"] = plan.turn(2, 0, 1)
                s["cmpturn"] = plan.turn(2, 0, 1)
                s["heads"] = plan.attention(32, 8, TILES1)
            s["out"] = plan.product(a["ab_w_out" if l == 0 else "nsa_w_out"][0], D, evac="dve")
            for o in s["out"]:
                o.order = (1, 0)
            s["mturn"] = plan.turn(4, 1, 1)
            s["mq"] = plan.product(a["mem_w_q"][l], 256) + plan.product(a["mem_w_q"][l], 256, first=256)
            M[l]["kturn"] = plan.turn(2, 1, 0)
            s["mqturn"] = plan.turn(2, 0, 1)
            s["mheads"] = plan.attention(4, 2, TILES)
            s["mo"] = plan.product(a["mem_w_o"][l], D, k=4, evac="dve")
            s["fturn"] = plan.turn(4, 1, 1)
            plan.turn_in_scores |= {s["fturn"] + 2, s["fturn"] + 3}
            s["ff"] = plan.blocks(FF // FB, 1, 2, ("ffn", l))
            s["ff"].start = sum(b["ff"].n for b in L[:l])
        N = {}
        N["hturn"] = plan.turn(4, 1, 1)
        N["in"] = (plan.product(a["w_in_2"][0], 1024, first=UL) + plan.product(a["w_in_2"][0], 512, first=UP)
                   + plan.product(a["w_in_2"][0], 1024, first=UG))
        N["gates"] = plan.product(a["w_in_2"][0], 2048, first=GA)
        N["uturn"] = plan.turn(10, 0, 1)
        N["gturn"] = plan.turn(8, 1, 0)
        N["yturn"] = plan.turn(2, 1, 1)
        N["pa"] = plan.product(a["proj_a_2"][0], D, k=4, evac="dve")
        N["pb"] = plan.product(a["proj_b_2"][0], D, evac="dve")
        N["oturn"] = plan.turn(4, 1, 1)
        N["out"] = plan.product(a["w_out_2"][0], D, evac="dve")
        N["h2turn"] = plan.turn(4, 1, 1)
        N["moe"] = plan.blocks(N_EXP * 2, 2, 2, ("moe", 0))
        N["moe"].start = 2 * (FF // FB)
        n_units = len(plan.width)

        XN = zv(0, D)
        SQA, SQQ, SQK = (z[:, a_:a_ + C * n * DH].rearrange("p (c h d) -> p c h d", c=C, d=DH)
                         for a_, n in ((4944, 9), (6096, 8), (7120, 8)))
        ROPET = feat[:, 4096:4672]
        COPIES = z[:, 8144:8656].rearrange("p (c n) -> p c n", c=C)
        MEMIN = feat[:, 0:2 * D].rearrange("p (c n) -> p c n", c=C)
        Z0, Z1, ZM = zv(0, AB_W), zv(0, C_W), zv(0, 512)
        KWT = z[:, 5216:5728]
        KCVT = z[:, 5728:7008].rearrange("p (g t) -> p g t", g=5)
        POST_GROUP, POST = z[:, 6752:7008], z[:, 6752:6784]
        HIV = z[0:DH, 6752:7264].rearrange("p (g j n) -> p g j n", g=4, j=4)
        VBLK = z[:, 7264:8288].rearrange("p (g j d) -> p g j d", g=4, j=4)
        CMPW = memo[:, 0:2048].rearrange("p (j e) -> p j e", e=DH)
        HID = z[0:DH, 8320:8576].rearrange("p (a g n) -> p a g n", a=2, g=4)
        HIT = z[0:DH, 8576:8832].rearrange("p (a g n) -> p a g n", a=2, g=4)
        KCN = z[:, 8832:8960].rearrange("p (a d) -> p a d", a=2)
        KCT = z[:, 8960:9088]
        GATE = z[:, 9088:9184].rearrange("p (c n) -> p c n", c=C)
        CS, CP = (shared[:, 512:1024], z[:, 5728:6240]), (shared[:, 1024:1536], z[:, 6240:6752])
        CPT = [shared[:, 1536:2048], shared[:, 0:512]]
        U = feat[:, :].rearrange("p (k t) -> p k t", t=T)
        ULT, UPT, UGT = U[:, 0:8, :], U[:, 8:12, :], U[:, 12:20, :]
        ZA = z[:, 0:5120].rearrange("p (s c n) -> p s c n", s=5, c=C)
        ZG = z[:, 5120:9216].rearrange("p (c n) -> p c n", c=C)
        XC = z[:, 0:2048].rearrange("p (k t) -> p k t", t=T)
        RG = z[:, 2048:4096].rearrange("p (k t) -> p k t", t=T)
        POOLT = z[:, 4096:5120].rearrange("p (k t) -> p k t", t=T)
        IG = memo[:, 0:2048].rearrange("p (k t) -> p k t", t=T)
        GATEW = memo[:, 2048:4096].rearrange("p (a k n) -> p a k n", a=2, k=8)
        POOLW = shared[:, 1664:2176].rearrange("p (g n) -> p g n", g=4)
        SP4 = shared[:, 2176:2192]
        LAM = shared[:, 2192:2256].rearrange("p (a k) -> p a k", a=8)
        HB = shared[:, 2256:2272].rearrange("p (a k) -> p a k", a=2)
        GELU = [z[:, a_:a_ + 1024].rearrange("p (k t) -> p k t", t=T) for a_ in (6144, 8192)]
        FHI, FLO = ahi[:, 0:2, :], alo[:, 0:2, :]

        def bank_of(s, c):
            return G[2 * (s.index % 2) + c][:, 0:s.width]

        def turn_bank(n):
            return (SCB if n in plan.turn_in_scores else TB)[n % 2]

        def gain_of(g):
            return lambda k: cols[:, 0, 8 * g + k:8 * g + k + 1]

        def pair(view, first):
            return lambda c: view[:, c, first:first + P]

        def place1(h):
            return 4 * (h // 8) + h % 4, h // 4 % 2

        def z1_dst(s, c):
            v = Z1[:, c, s.c0:s.c0 + s.width]
            if s.c0 < KCMP:
                return v.rearrange("p (i g d) -> p g i d", g=2, d=DH)
            if s.c0 == KCMP:
                return v.rearrange("p (g a d) -> p a g d", a=2, d=DH)
            return v

        def z1_src(s, c):
            v = bank_of(s, c)
            if s.c0 < KCMP:
                return v.rearrange("p (g i d) -> p g i d", g=2, d=DH)
            if s.c0 == KCMP:
                return v.rearrange("p (a g d) -> p a g d", a=2, d=DH)
            return v

        JOBS0 = ([pair(Z0, IQ), pair(Z0, IQ + P), pair(COPIES, 0), pair(COPIES, P)]
                 + [pair(Z0, AQ + P * i) for i in range(4)] + [pair(Z0, BQ + P * i) for i in range(4)]
                 + [pair(Z0, BK + P * i) for i in range(4)])
        JOBSQ = [pair(Z1, NQ + P * i) for i in range(8)]
        JOBSK = [pair(Z1, KSEL + P * i) for i in range(2)] + [pair(Z1, KWIN + P * i) for i in range(2)]
        JOBSC = [pair(Z1, KCMP + P * g) for g in range(4)]
        SQ1 = {name: feat[:, a_:a_ + C * n * DH].rearrange("p (c h d) -> p c h d", c=C, d=DH)
               for name, a_, n in (("q0", 2048, 8), ("q1", 3072, 8), ("sel", 4096, 4), ("win", 4608, 4))}
        ROPET1 = feat[:, 4608:5120]
        JOBSM = [pair(ZM, P * i) for i in range(4)]

        def head_out(k, half_, c):
            return G[k // 2][DH * half_:DH * half_ + DH, T * (k % 2) + P * c:T * (k % 2) + P * c + P]

        def items0():
            out_ = []
            for q0, k0, one_key, bias, v0, dv, chunk in ((2048, 3072, False, causal, BV, DH, 4), (1024, 768, True, dsa_bias, AV, 0, 0)):
                for h in range(8):
                    r = slice(DH * (h % 2), DH * (h % 2) + DH)
                    branches = []
                    for c in range(C):
                        nk = P * (c + 1)
                        q, k = q0 + T * (h // 2) + P * c, k0 + (0 if one_key else T * (h // 2))
                        branches.append(Branch(feat[r, q:q + P], feat[r, k:k + nk], nk, bias[:, c, 0:nk],
                                               [Z0[:, b, v0 + dv * h:v0 + dv * h + DH] for b in range(c + 1)],
                                               head_out(chunk + h // 2, h % 2, c)))
                    out_.append(Item(branches, DH ** -0.5))
            return out_

        def items1():
            out_ = []
            for h in list(range(8, 16)) + list(range(8)):
                (jq, half_), g = place1(h), h // 4
                r = slice(DH * half_, DH * half_ + DH)
                for c in range(C):
                    nk, q = P * (c + 1), 2048 + T * jq + P * c
                    branches = [Branch(feat[r, q:q + P], keys[r, T * (g // 2):T * (g // 2) + nk], nk, causal[:, c, 0:nk],
                                       [Z1[:, b, v0 + DH * g:v0 + DH * g + DH] for b in range(c + 1)],
                                       head_out(h // 2, h % 2, c))
                                for keys, v0 in ((feat[:, 4096:4608], VSEL), (KWT, VWIN))]
                    out_.append(Item(branches, DH ** -0.5, GATE[:, c, 3 * h + 1:3 * h + 3],
                                     (VBLK[:, g, h % 4, :], CPT[c][:, P * g:P * g + P])))
            return out_

        def items_mem(l):
            return [Item([Branch(feat[:, T * h + P * c:T * h + P * (c + 1)], memk[l][:, h, :], T, zero[:, :],
                                 [memv[l][:, b, P * h:P * h + P] for b in range(C)],
                                 G[h // 2][:, T * (h % 2) + P * c:T * (h % 2) + P * c + P]) for c in range(C)], P ** -0.5)
                    for h in range(4)]

        def xsrc(c, k):
            return x[:, c, P * k:P * k + P]

        def ysrc(c, k):
            return ZG[:, c, P * k:P * k + P]

        def dve_share(n):
            return LO_DVE if n == UNIT else n * 3 // 16 * 2

        def loop_turns(b):
            return b.first // b.per, b.last // b.per, b.per

        def landed_at(b, j, c):
            ref = b.base + 3 * b.first + c
            return plan.landed(ref) + 16 * plan.dmas[ref] * (j - b.first)

        block = ctx.enter_context(nc.Block())

        @block.sync
        def _(sp):
            def slot_free(u, static=True):
                if not static or u >= RING:
                    sp.wait_ge(lo_dve, u - RING + 1)
                    sp.wait_ge(lo_pool, u - RING + 1)

            def load_slab(s):
                for i in range(s.units):
                    u, nk, part = s.unit + i, min(4, s.k), s.order[i]
                    slot_free(u)
                    sp.dma_start(raw[u % RING][:, 0:nk * s.width].rearrange("p (k n) -> p k n", k=nk),
                                 s.w[512 * part:512 * part + P * nk, s.c0:s.c0 + s.width].rearrange("(k p) n -> p k n", p=P)
                                 ).then_inc(raw_loaded[u % RING], 16)

            def load_up(b, j, half, u, slot, static, e=None, h=None):
                slot_free(u, static)
                kind, l = b.load
                dst = raw[slot][:, :].rearrange("p (k a f) -> p k a f", k=4, a=2)
                if kind == "ffn":
                    for n in range(2):
                        src = a["ffn_w_in"][l, 512 * half:512 * half + 512, FF * n:FF * n + FF].rearrange("(k p) f -> p k f", p=P)
                        sp.dma_start(dst[:, :, n, :], src[:, :, bass.ds(j * FB, FB)]).then_inc(raw_loaded[slot], 16)
                else:
                    for n, w in enumerate(("exp_w_gate_2", "exp_w_up_2")):
                        src = a[w][0, bass.ds(e, 1), 512 * half:512 * half + 512, FB * h:FB * h + FB]
                        src = src.rearrange("e (k p) f -> p (e k) f", p=P)
                        sp.dma_start(dst[:, :, n, :], src).then_inc(raw_loaded[slot], 16)

            def load_down(b, j, u, slot, static):
                slot_free(u, static)
                kind, l = b.load
                w = a["ffn_w_out"][l] if kind == "ffn" else a["exp_w_down_2"][0].rearrange("e f n -> (e f) n")
                src = w[bass.ds(j * FB, FB), :].rearrange("(r p) n -> p r n", p=P)
                sp.dma_start(raw[slot][:, :].rearrange("p (r n) -> p r n", r=2), src).then_inc(raw_loaded[slot], 16)

            def load_block(b, j, static, e=None, h=None):
                u = b.base + 3 * j - 1
                s = (b.base - 1) % RING
                load_up(b, j, 0, u, s, static, e, h)
                load_up(b, j, 1, u + 1, (s + 1) % RING, static, e, h)
                load_down(b, j - 1, u + 2, (s + 2) % RING, static)

            def load_blocks(b):
                halves = 2 if b.per == 2 else 1
                where = (lambda j: (j // 2, j % 2)) if halves == 2 else (lambda j: (None, None))
                load_up(b, 0, 0, b.base, b.base % RING, True, *where(0))
                load_up(b, 0, 1, b.base + 1, (b.base + 1) % RING, True, *where(0))
                load_block(b, 1, True, *where(1))
                first, last, per = loop_turns(b)
                with sp.Fori(first, last) as i:
                    for n in range(per):
                        load_block(b, i * per + n, False, i, n)
                for j in range(b.last, b.n):
                    load_block(b, j, True, *where(j))
                load_down(b, b.n - 1, b.base + 3 * b.n - 1, (b.base + 3 * b.n - 1) % RING, True)

            sp.dma_start(x[:, :, :], a["x"][0].rearrange("(c p) n -> p c n", p=P)).then_inc(flag("x_in"), 16)
            for n, s in enumerate(plan.loads):
                if n == 0:
                    sp.wait_ge(flag("rows_in"), 16 * 16)
                    sp.wait_ge(flag("positions_in"), 16)
                if n == 1:
                    sp.dma_start(MEMIN, a["mem"][0].rearrange("(c p) n -> p c n", p=P)).then_inc(flag("mem_in"), 16)
                load_blocks(s) if isinstance(s, Blocks) else load_slab(s)
                if s is L[1]["keys"][0]:
                    sp.wait_ge(pved, L[0]["mheads"].outs + 4)
                    for n_, w in enumerate(("nsa_cmp_w1_k", "nsa_cmp_w1_v")):
                        sp.dma_start(CMPW[DH * n_:DH * n_ + DH], a[w][0].rearrange("(j d) e -> d j e", d=DH)
                                     ).then_inc(flag("cmp_weights_in"), 16)
                if s is N["in"][0]:
                    sp.wait_ge(pved, L[1]["mheads"].outs + 4)
                    sp.wait_ge(flag("gate_weights_zeroed"), 1)
                    for n_, w in enumerate(("rg_w_r_2", "rg_w_i_2")):
                        src = a[w][0].rearrange("(k h) c d -> h c k d", h=2)
                        for h in range(2):
                            r = slice(DH * h, DH * h + DH)
                            sp.dma_start(GATEW[r, n_, :, DH * h:DH * h + DH], src[h]).then_inc(flag("gate_weights_in"), 16)
                    sp.dma_start(POOLW, a["pool_w_2"][0].rearrange("g c d -> c g d")).then_inc(flag("gate_weights_in"), 16)
                if s is N["pb"][-1]:
                    sp.wait_ge(flag("lru_done"), 1)
                    wide = route_w
                    sp.dma_start(wide[:, :, 0:N_GRP], a["router_group_w_2"][0].rearrange("(k p) n -> p k n", p=P)).then_inc(flag("router_in"), 16)
                    sp.dma_start(wide[:, :, N_GRP:20], a["router_expert_w_2"][0].rearrange("(k p) n -> p k n", p=P)).then_inc(flag("router_in"), 16)
                    sp.dma_start(route_b[:, 0:N_GRP], a["router_group_b_2"].broadcast_to([P, N_GRP])).then_inc(flag("router_in"), 16)
                    sp.dma_start(route_b[:, N_GRP:20], a["router_expert_b_2"].broadcast_to([P, N_EXP])).then_inc(flag("router_in"), 16)
                    sp.dma_start(final_gain, a["norm_f_g_2"].rearrange("(a n) -> a n", a=1).broadcast_to([P, D])).then_inc(flag("final_gain_in"), 16)
            for c in range(C):
                sp.wait_ge(flag("out_ready"), c + 1)
                sp.dma_start(out[0, P * c:P * c + P, :], XN[:, c, :]).then_inc(flag("stored"), 16)
            sp.wait_ge(flag("stored"), 32)

        @block.gpsimd
        def _(pool):
            step = Chain(pool, pool_step)
            at = [0]

            def lo(u, slot, n):
                s = dve_share(n)
                pool.wait_ge(hi_done, u + 1)
                pool.tensor_tensor(wlo[slot][:, s:n], raw[slot][:, s:n], whi[slot][:, s:n].bitcast(F32),
                                   ALU.subtract).then_inc(lo_pool, 1)

            def split_to(end):
                while at[0] < min(end, n_units):
                    lo(at[0], at[0] % RING, plan.width[at[0]])
                    at[0] += 1

            def blocks(b):
                first, last, per = loop_turns(b)
                split_to(b.base + 3 * b.first + 1)
                with pool.Fori(first, last) as i:
                    for n in range(per):
                        for c in range(1, 4):
                            lo(b.base + 3 * (i * per + n) + c, (b.base + c) % RING, UNIT)
                at[0] = b.base + 3 * b.last + 1

            step(pool.memset(ident[:, :], 0.0))
            step(pool.affine_select(out=ident[:, :], in_=ident[:, :], compare_op=ALU.not_equal, fill=1.0,
                                    base=0, pattern=[[-1, P]], channel_multiplier=1))
            step(pool.memset(zero[:, :], 0.0))
            for c in range(C):
                step(pool.affine_select(out=causal[:, c, :], in_=zero[:, :], compare_op=ALU.is_ge, fill=NEG,
                                        base=P * c, pattern=[[-1, T]], channel_multiplier=1))
            for c in range(C):
                step(pool.affine_select(out=cmp_bias[:, c, :], in_=zero[:, 0:32], compare_op=ALU.is_ge, fill=NEG,
                                        base=P * c - (CMP_LEN - 1), pattern=[[-CMP_STRIDE, 32]], channel_multiplier=1))
            step(pool.memset(cmp_keep[:, :, :], 1.0))
            for c in range(C):
                step(pool.affine_select(out=cmp_keep[:, c, :], in_=cmp_keep[:, c, :], compare_op=ALU.is_ge, fill=0.0,
                                        base=P * c - (CMP_LEN - 1), pattern=[[-CMP_STRIDE, 32]], channel_multiplier=1))
            for t in range(16):
                ins = pool.memset(numbers[:, t:t + 1], 1.0 / (t + 1))
            ins.then_inc(flag("masks_ready"), 1)

            def scale_probs(items, run):
                for t, it in enumerate(items):
                    p_ = run.prob[(run.first + t) % 4]
                    pool.wait_ge(item_weighed, run.outs + t + 1)
                    for n in range(2):
                        nk = it.branches[n].nk
                        pn = p_[:, it.at[n]:it.at[n] + nk]
                        ins = pool.tensor_tensor(pn, pn, item_inv[:, 2 * t + n:2 * t + n + 1].broadcast_to([P, nk]), ALU.mult)
                    ins.then_inc(prob_scaled, 1)

            for l in range(2):
                split_to(L[l]["out"][0].unit + 2)
                scale_probs(items1() if l else items0(), L[l]["heads"])
                split_to(L[l]["mo"][0].unit + 2)
                scale_probs(items_mem(l), L[l]["mheads"])
                split_to(L[l]["ff"].base)
                blocks(L[l]["ff"])
            split_to(N["in"][0].unit + 2)
            pool.wait_ge(pved, L[1]["mheads"].outs + 4)
            pool.memset(GATEW, 0.0).then_inc(flag("gate_weights_zeroed"), 1)

            split_to(N["gates"][0].unit + 2)
            pool.wait_ge(turned, N["uturn"] + 10)
            pool.wait_ge(turn_dve, plan.turn_dve[N["uturn"] + 6])
            for g, w in enumerate(POOL_WINDOWS):
                p_, src, span = POOLT[:, g, :], UPT[:, g, :], 1
                cur = src
                while span < w:
                    nxt = pool_sum[0] if cur is not pool_sum[0] else pool_sum[1]
                    pool.tensor_copy(nxt[:, 0:span], cur[:, 0:span])
                    step(pool.tensor_tensor(nxt[:, span:T], cur[:, span:T], cur[:, 0:T - span], ALU.add))
                    cur, span = nxt, 2 * span
                pool.tensor_tensor(p_[:, 0:w - 1], cur[:, 0:w - 1], numbers[:, 0:w - 1], ALU.mult)
                step(pool.tensor_tensor(p_[:, w - 1:T], cur[:, w - 1:T], numbers[:, w - 1:w].broadcast_to([P, T - w + 1]), ALU.mult))
                ins = pool.tensor_tensor(p_, p_, src, ALU.subtract)
                step(ins) if g < 3 else ins.then_inc(flag("pooled"), 1)
                split_to(N["gates"][0].unit + 3 + g)
            split_to(N["moe"].base)
            blocks(N["moe"])
            split_to(n_units)

        @block.scalar
        def _(act):
            step = Chain(act, act_step)
            at = [0]

            def hi(u, slot, n, landed, static=True):
                act.wait_ge(raw_loaded[slot], landed)
                if not static or u >= RING:
                    act.wait_ge(unit_used, u - RING + 1)
                act.activation(whi[slot][:, 0:n], raw[slot][:, 0:n], ACT.Copy).then_inc(hi_done, 1)

            def split_to(end):
                while at[0] < min(end, n_units):
                    u = at[0]
                    hi(u, u % RING, plan.width[u], plan.landed(u))
                    at[0] += 1

            def product(slabs, dst, src=bank_of, scale=True):
                for s in slabs:
                    split_to(s.end + 2)
                    if s.evac == "both":
                        act.wait_ge(unit_used, s.end)
                        act.activation(dst(s, 0), src(s, 0), ACT.Copy, scale=row_scale[:, 0:1] if scale is True else scale
                                       ).then_inc(slab_act, 1)

            def to_t(base, batches, gain, dst):
                for b in batches:
                    act.wait_ge(turned, base + b + 1)
                    bank = turn_bank(base + b)
                    for n in range(2):
                        k = 2 * b + n
                        ins = act.activation(dst[:, k, :], bank[:, T * n:T * n + T], ACT.Copy,
                                             scale=gain(k) if callable(gain) else gain)
                    ins.then_inc(turn_act, 1)

            def squares(src, tag, scratch=2048, first=0):
                for c in range(C):
                    ins = act.activation(z[:, scratch + D * c:scratch + D * c + D], src[:, c, :], ACT.Square,
                                         accum_out=sumsq[:, first + c:first + c + 1])
                ins.then_inc(flag("squared_" + tag), 1)

            def head_squares(parts, slabs, tag):
                act.wait_ge(slab_act, slabs[-1].done_act)
                act.wait_ge(slab_dve, slabs[-1].done_dve)
                for src, dst in parts:
                    ins = act.activation(dst, src, ACT.Square)
                ins.then_inc(flag("head_squares_" + tag), 1)

            def attention(items, run, banks):
                n, per = run.n, run.per
                for t in range(n + 5 + 1):
                    if t < n:
                        it, g = items[t], run.first + t
                        act.wait_ge(item_masked, g + 1)
                        if t >= 4:
                            act.wait_ge(turned, run.batch + t - 3)
                        for m in range(2):
                            a_, b_ = it.at[m], it.at[m] + it.branches[m].nk
                            ins = act.activation(run.prob[g % 4][:, a_:b_], run.masked[g % 2][:, a_:b_], ACT.Exp, scale=-1.0,
                                                 bias=item_min[:, 2 * t + m:2 * t + m + 1],
                                                 accum_out=item_sum[:, 2 * t + m:2 * t + m + 1])
                        ins.then_inc(exped, 1)
                    if t >= 5 and (t - 4) % per == 0:
                        k = banks[(t - 4) // per - 1]
                        act.wait_ge(pved, run.outs + t - 4)
                        act.activation(ahi[:, 2 * k:2 * k + 2, :], G[k][:, :].rearrange("p (k t) -> p k t", k=2),
                                       ACT.Copy).then_inc(heads_hi, 1)

            def ff_up_out(j, static=True):
                for c in range(C):
                    if c == 0:
                        act.wait_ge(unit_used, ff_gu_unit(j))
                        if not static or ff_n(j) >= 1:
                            act.wait_ge(ff_silu, ff_n(j))
                    act.activation(silu[:, c, 0, :], TB[c][:, 0:FB], ACT.Tanh, scale=half_scale[:, c:c + 1]).then_inc(ff_tanh, 1)

            def ff_hidden(j):
                act.wait_ge(ff_turned, ff_n(j) + 1)
                act.activation(FHI, SCB[0][:, :].rearrange("p (f t) -> p f t", f=2), ACT.Copy).then_inc(ff_hi, 1)

            def blocks(b):
                nonlocal ff_n, ff_gu_unit
                ff_n = lambda j: b.start + j
                ff_gu_unit = lambda j: b.base + 2 if isinstance(j, int) and j == 0 else b.base + 3 * j + 1
                split_to(b.base + 3)
                ff_up_out(0)
                split_to(b.base + 4)
                ff_hidden(0)
                split_to(b.base + 6)
                ff_up_out(1)
                split_to(b.base + 7)
                first, last, per = loop_turns(b)
                with act.Fori(first, last) as i:
                    for n in range(per):
                        j = i * per + n
                        ff_hidden(j - 1)
                        for c in (1, 2):
                            hi(b.base + 3 * j + c, (b.base + c) % RING, UNIT, landed_at(b, j, c), False)
                        ff_up_out(j, False)
                        hi(b.base + 3 * j + 3, (b.base + 3) % RING, UNIT, landed_at(b, j, 3), False)
                at[0] = b.base + 3 * b.last + 1
                for j in range(b.last, b.n):
                    ff_hidden(j - 1)
                    split_to(b.base + min(3 * j + 3, 3 * b.n))
                    ff_up_out(j)
                    split_to(b.base + min(3 * j + 4, 3 * b.n))
                ff_hidden(b.n - 1)

            ff_n = ff_gu_unit = None

            def load(dst, src, name):
                act.dma_start(dst, src).then_inc(flag(name), 16)

            for l in range(2):
                for g, name in ((G_MIX, "norm_mix"), (G_MEM, "norm_mem"), (G_SRC, "norm_mem_src"), (G_FFN, "norm_ffn")):
                    load(rows[8 * g[l]:8 * g[l] + 8, 0, :], a[name][l].rearrange("(k p) -> k p", p=P), "rows_in")
            for g, name in ((G_N1, "norm1_g_2"), (G_N2, "norm2_g_2")):
                load(rows[8 * g:8 * g + 8, 0, :], a[name][0].rearrange("(k p) -> k p", p=P), "rows_in")
            load(rows[0:32, 1, :], a["conv_w_2"][0].rearrange("w (k p) -> (w k) p", p=P), "rows_in")
            for r, name in ((R_CB, "conv_b_2"), (R_BR, "rg_b_r_2"), (R_BI, "rg_b_i_2"), (R_LAM, "rg_lambda_2")):
                load(rows[r:r + 8, 1, :], a[name][0].rearrange("(k p) -> k p", p=P), "rows_in")
            load(rows[R_PS:R_PS + 4, 1, :], a["pool_scale_2"][0].rearrange("(k p) -> k p", p=P), "rows_in")
            load(pos_i[:, :], a["positions"].rearrange("a (c p) -> (a c) p", p=P), "positions_in")
            act.wait_ge(flag("x_in"), 16)
            squares(x, "x")
            act.wait_ge(flag("cols_ready"), 1)
            to_t(L[0]["hturn"], range(4), gain_of(G_MIX[0]), ahi)
            split_to(RING)
            act.wait_ge(flag("mem_in"), 16)
            squares(MEMIN, "mix0", 4944, C)
            for n, name in enumerate(("dsa_q_norm", "dsa_k_norm", "moba_q_norm", "moba_k_norm", "nsa_q_norm",
                                      "nsa_kcmp_norm", "nsa_ksel_norm", "nsa_kwin_norm")):
                load(gains[:, n, :], a[name].broadcast_to([P, DH]), "gains_in")
            for l in range(2):
                load(mem_q_gain[:, l, :], a["mem_q_norm"][l:l + 1, :].broadcast_to([P, P]), "gains_in")
                load(mem_k_gain[:, l, :], a["mem_k_norm"][l:l + 1, :].broadcast_to([P, P]), "gains_in")
            load(pos_rows[:, 0:DH], a["nsa_cmp_pos_k"][0], "gains_in")
            load(pos_rows[:, DH:P], a["nsa_cmp_pos_v"][0], "gains_in")
            load(w2[:, 0, :], a["nsa_cmp_w2_k"][0], "gains_in")
            load(w2[:, 1, :], a["nsa_cmp_w2_v"][0], "gains_in")

            for l in range(2):
                s = L[l]
                if l:
                    to_t(s["hturn"], range(4), gain_of(G_MIX[l]), ahi)
                    act.wait_ge(flag("ff_added0"), 2)
                    squares(x, "mix1")
                    split_to(at[0] + 1)
                act.wait_ge(flag(f"row_scale_mix{l}"), 1)
                if l == 0:

                    def z0(s_, c):
                        return Z0[:, c, s_.c0:s_.c0 + s_.width]

                    product(s["in"][0:1], z0)
                    act.wait_ge(flag("angles"), 1)
                    act.activation(sine[:, :, :], angle[:, 3], ACT.Sin)
                    act.activation(cosine[:, :, :], angle[:, 4], ACT.Sin).then_inc(flag("rotation"), 1)
                    product(s["in"][1:2], z0)
                    head_squares([(heads(Z0, AQ, 9, DH), SQA)], s["in"][0:2], "a")
                    product(s["in"][2:3], z0)
                    head_squares([(heads(Z0, BQ, 8, DH), SQQ)], s["in"][0:3], "bq")
                    product(s["in"][3:4], z0)
                    head_squares([(heads(Z0, BK, 8, DH), SQK)], s["in"][0:4], "bk")
                    product(s["in"][4:5], z0)
                    for b in range(4):
                        act.wait_ge(turned, mem_turn + b + 1)
                        for m, dst in enumerate((bhi, ahi)):
                            for n in range(2):
                                ins = act.activation(dst[:, 2 * b + n, :], TB[(mem_turn + b) % 2][:, T * n:T * n + T],
                                                     ACT.Copy, scale=gain_of(G_SRC[m])(2 * b + n))
                        ins.then_inc(turn_act, 1)
                    kv = M[0]["kv"] + M[1]["kv"]
                    dsts = (memk_rows[0], memv[0], memk_rows[1], memv[1])
                    product(kv[0:1], lambda s_, c: dsts[0][:, c, :], scale=mem_scale[:, 0:1])
                    for n in (1, 2):
                        for v in range(2):
                            split_to(kv[n].unit + v + RING)
                            for i in range(8 * n - 8 + 4 * v, 8 * n - 4 + 4 * v):
                                g, nk = s["index"] + i, P * (i // 8 + 1)
                                act.wait_ge(scored, g + 1)
                                if i >= 3:
                                    act.wait_ge(item_masked, g - 2)
                                act.activation(relu_out[g % 3][:, 0:nk], SCB[g % 2][:, 0:nk], ACT.Relu).then_inc(exped, 1)
                        product(kv[n:n + 1], lambda s_, c: dsts[n][:, c, :], scale=mem_scale[:, 0:1])
                    product(kv[3:4], lambda s_, c: dsts[3][:, c, :], scale=mem_scale[:, 0:1])
                    attention(items0(), s["heads"], (2, 3, 0, 1))
                else:
                    product(s["cmp"] + s["keys"], z1_dst, z1_src)
                    head_squares([(heads(Z1, KSEL, 4, DH), SQ1["sel"]), (heads(Z1, KWIN, 4, DH), SQ1["win"])], s["keys"], "keys")
                    for name, first, n in (("q0", NQ, 8), ("q1", NQ + 512, 8)):
                        product(s[name], z1_dst, z1_src)
                        head_squares([(heads(Z1, first, n, DH), SQ1[name])], s[name], name)
                        if name == "q1":
                            split_to(s["q1"][-1].end + RING)
                            act.wait_ge(flag("cmp_hidden"), 1)
                            act.activation(HIT, HID, ACT.Tanh, scale=0.5).then_inc(flag("cmp_tanh"), 1)
                    product(s["vg"], z1_dst, z1_src)
                    act.wait_ge(slab_act, s["vg"][-1].done_act)
                    act.wait_ge(slab_dve, s["vg"][-1].done_dve)
                    act.activation(GATE, Z1[:, :, GT:C_W], ACT.Tanh, scale=0.5).then_inc(flag("gates_tanh"), 1)
                    for c in range(C):
                        act.wait_ge(flag("cmp_shifted"), c + 1)
                        act.activation(CP[c], CS[c], ACT.Exp).then_inc(flag("cmp_exp"), 1)
                    attention(items1(), s["heads"], (2, 3, 0, 1))
                act.wait_ge(slab_dve, M[l]["kv"][-1].done_dve)
                act.activation(zv(4944, 512), memk_rows[l], ACT.Square).then_inc(flag(f"head_squares_mk{l}"), 1)
                product(s["out"][0:1], None)
                to_t(s["mturn"], range(2), gain_of(G_MEM[l]), bhi)
                product(s["out"][1:2], None)
                to_t(s["mturn"], range(2, 4), gain_of(G_MEM[l]), bhi)
                act.wait_ge(slab_dve, s["out"][-1].done_dve)
                squares(x, f"memq{l}")
                split_to(at[0] + 1)
                act.wait_ge(flag(f"row_scale_memq{l}"), 1)
                for n in range(2):
                    product(s["mq"][n:n + 1], lambda s_, c: ZM[:, c, s_.c0:s_.c0 + 256])
                    head_squares([(heads(ZM, 256 * n, 2, P), heads(zv(2048, 512), 256 * n, 2, P))], s["mq"][n:n + 1], f"memq{l}")
                act.wait_ge(turned, M[l]["kturn"] + 2)
                for b in range(2):
                    act.activation(memo[:, 2048 * l + 512 * b:2048 * l + 512 * b + 512],
                                   TB[(M[l]["kturn"] + b) % 2][:, :], ACT.Copy).then_inc(turn_act, 1)
                split_to(s["mo"][-1].end)
                attention(items_mem(l), s["mheads"], (0, 1))
                product(s["mo"][0:1], None)
                to_t(s["fturn"], range(2), gain_of(G_FFN[l]), bhi)
                product(s["mo"][1:2], None)
                to_t(s["fturn"], range(2, 4), gain_of(G_FFN[l]), bhi)
                act.wait_ge(slab_dve, s["mo"][-1].done_dve)
                squares(x, f"ffn{l}")
                split_to(at[0] + 1)
                act.wait_ge(flag(f"row_scale_ffn{l}"), 1)
                blocks(s["ff"])
                split_to(s["ff"].base + 3 * s["ff"].n + 2)

            to_t(N["hturn"], range(4), gain_of(G_N1), ahi)
            act.wait_ge(flag("ff_added1"), 2)
            squares(x, "mix2")
            split_to(at[0] + 1)
            act.wait_ge(flag("row_scale_mix2"), 1)
            for n in range(5):
                product(N["in"][n:n + 1], lambda s_, c: ZA[:, n, c, :])
                if n == 3:
                    act.wait_ge(flag("minus_abs_lambda"), 1)
                    act.activation(LAM[:, 1, :], LAM[:, 1, :], ACT.Exp).then_inc(flag("exp_lambda"), 1)
            product(N["gates"][0:1], lambda s_, c: ZG[:, c, s_.c0 - GA:s_.c0 - GA + 512])
            act.wait_ge(flag("gelu_inner"), 2)
            for n in range(2):
                ins = act.activation(GELU[n], GELU[n], ACT.Tanh, scale=math.sqrt(2 / math.pi))
            ins.then_inc(flag("gelu_tanh"), 1)
            for k in range(8):
                act.wait_ge(turned, N["gturn"] + k + 1)
                if k == 4:
                    split_to(N["gates"][1].end + 1)
                bank = TB[(N["gturn"] + k) % 2]
                act.activation(RG[:, k, :], bank[:, 0:T], ACT.Tanh, scale=0.5, bias=HB[:, 0, k:k + 1])
                act.activation(IG[:, k, :], bank[:, T:2 * T], ACT.Tanh, scale=0.5, bias=HB[:, 1, k:k + 1]).then_inc(turn_act, 1)
            product(N["gates"][1:2], lambda s_, c: ZG[:, c, s_.c0 - GA:s_.c0 - GA + 512])
            split_to(N["gates"][1].end + RING)
            act.wait_ge(flag("log_decay"), 1)
            act.activation(ULT, RG, ACT.Exp, scale=-1.0).then_inc(flag("decay"), 1)
            act.wait_ge(flag("decay"), 1)
            act.activation(RG, RG, ACT.Tanh).then_inc(flag("decay_tanh"), 1)
            product(N["gates"][2:4], lambda s_, c: ZG[:, c, s_.c0 - GA:s_.c0 - GA + 512])
            act.wait_ge(slab_act, N["gates"][-1].done_act)
            act.wait_ge(slab_dve, N["gates"][-1].done_dve)
            act.activation(ZG, ZG, ACT.Tanh, scale=0.5).then_inc(flag("mix_gates"), 1)
            to_t(N["yturn"], range(2), lambda k: cols[:, 1, R_PS + k:R_PS + k + 1], ahi)
            act.wait_ge(flag("drive_squared"), 1)
            act.activation(RG, RG, ACT.Sqrt, scale=0.25).then_inc(flag("drive_scale"), 1)
            act.wait_ge(flag("lru_out"), 1)
            act.activation(bhi[:, :, :], ULT, ACT.Copy).then_inc(flag("lru_hi"), 1)
            product(N["pa"], None)
            product(N["pb"][0:1], None)
            to_t(N["oturn"], range(2), 0.5, ahi)
            product(N["pb"][1:2], None)
            to_t(N["oturn"], range(2, 4), 0.5, ahi)
            act.wait_ge(flag("router_in"), 64)
            act.activation(rhi[:, :, :], route_w, ACT.Copy).then_inc(flag("router_hi"), 1)
            product(N["out"][0:1], None)
            to_t(N["h2turn"], range(2), gain_of(G_N2), bhi)
            product(N["out"][1:2], None)
            to_t(N["h2turn"], range(2, 4), gain_of(G_N2), bhi)
            act.wait_ge(slab_dve, N["out"][-1].done_dve)
            squares(x, "moe")
            split_to(at[0] + 1)
            act.wait_ge(flag("row_scale_moe"), 1)
            split_to(N["moe"].base + RING)
            act.wait_ge(flag("group_shifted"), 1)
            act.activation(rt[:, 1, :, 0:N_GRP], rt[:, 0, :, 0:N_GRP], ACT.Exp).then_inc(flag("group_exp"), 1)
            act.wait_ge(flag("expert_gap"), 1)
            act.activation(rt[:, 9, :, 0:1], rt[:, 8, :, 0:1], ACT.Exp).then_inc(flag("expert_exp"), 1)
            blocks(N["moe"])
            act.wait_ge(flag("ff_added2"), 2)
            squares(x, "final")

        @block.vector
        def _(dve):
            step = Chain(dve, dve_step)
            at = [0]

            def lo(u, slot, n):
                s = dve_share(n)
                dve.wait_ge(hi_done, u + 1)
                dve.tensor_tensor(wlo[slot][:, 0:s], raw[slot][:, 0:s], whi[slot][:, 0:s].bitcast(F32),
                                  ALU.subtract).then_inc(lo_dve, 1)

            def split_to(end):
                while at[0] < min(end, n_units):
                    lo(at[0], at[0] % RING, plan.width[at[0]])
                    at[0] += 1

            def product(slabs, dst, src=bank_of, scale=True):
                for s in slabs:
                    split_to(s.end + 2)
                    dve.wait_ge(unit_used, s.end)
                    if s.evac == "both":
                        dve.tensor_scalar(dst(s, 1), src(s, 1), (row_scale if scale is True else scale)[:, 1:2], None,
                                          ALU.mult).then_inc(slab_dve, 1)
                    else:
                        for c in range(C):
                            if dst is None:
                                xs = x[:, c, s.c0:s.c0 + s.width]
                                dve.tensor_tensor(xs, xs, bank_of(s, c), ALU.add).then_inc(slab_dve, 1)
                            else:
                                dst(s, c)
                if slabs[-1].evac == "dve":
                    dve.wait_ge(slab_dve, slabs[-1].done_dve)

            def rsqrt(n, d):
                m, y, t, u = (s_[:, 0:n] for s_ in (s_mean, s_y, s_t, s_u))
                step(dve.tensor_scalar(m, m, 1.0 / d, EPS, ALU.mult, ALU.add))
                step(dve.tensor_scalar(s_bits[:, 0:n], m.bitcast(I32), 1, None, ALU.logical_shift_right))
                step(dve.tensor_scalar(y.bitcast(I32), s_bits[:, 0:n], -1.0, 1597463007.0, ALU.mult, ALU.add))
                dve.tensor_scalar(m, m, -0.5, None, ALU.mult)
                for _ in range(3):
                    step(dve.tensor_tensor(t, y, y, ALU.mult))
                    step(dve.tensor_tensor(u, t, m, ALU.mult))
                    step(dve.scalar_tensor_tensor(out=y, in0=u, scalar=1.5, in1=y, op0=ALU.add, op1=ALU.mult))

            def row_scales(tag):
                dve.wait_ge(flag("squared_" + tag), 1)
                n = 2 * C if tag == "mix0" else C
                step(dve.tensor_copy(s_mean[:, 0:n], sumsq[:, 0:n]))
                rsqrt(n, D)
                if n > C:
                    dve.tensor_copy(mem_scale[:, :], s_y[:, C:n])
                dve.tensor_scalar(half_scale[:, :], s_y[:, 0:C], 0.5, None, ALU.mult)
                step(dve.tensor_copy(row_scale[:, :], s_y[:, 0:C]))
                step(dve.tensor_tensor(half_scale2[:, :], half_scale[:, :], row_scale[:, :], ALU.mult))
                dve.sem_inc(flag("row_scale_" + tag), 1)
                if tag != "mix0":
                    split_to(at[0] + 1)

            def to_t(base, batches, gain, hi_, dst):
                for b in batches:
                    dve.wait_ge(turn_act, plan.turn_act[base + b + 1])
                    bank = turn_bank(base + b)
                    for n in range(2):
                        k = 2 * b + n
                        ins = dve.scalar_tensor_tensor(out=dst[:, k, :], in0=bank[:, T * n:T * n + T],
                                                       scalar=gain(k) if callable(gain) else gain,
                                                       in1=hi_[:, k, :].bitcast(F32), op0=ALU.mult, op1=ALU.subtract)
                    ins.then_inc(turn_dve, 1)

            def turns(base, n, dst):
                for b in range(n):
                    dve.wait_ge(turned, base + b + 1)
                    dve.tensor_copy(dst(b), turn_bank(base + b)[:, :]).then_inc(turn_dve, 1)
                dve.wait_ge(turn_dve, plan.turn_dve[base + n])

            def head_norm(parts, d, tag):
                dve.wait_ge(flag("head_squares_" + tag), 1)
                at_ = 0
                for sq, v, _ in parts:
                    n = v.shape[2]
                    step(dve.tensor_reduce(s_mean[:, at_:at_ + C * n].rearrange("p (c h) -> p c h", c=C), sq, AX, ALU.add))
                    at_ += C * n
                rsqrt(at_, d)
                at_ = 0
                for _, v, _ in parts:
                    n = v.shape[2]
                    r = s_y[:, at_:at_ + C * n].rearrange("p (c h) -> p c h", c=C).unsqueeze(3).broadcast_to([P, C, n, d])
                    ins = dve.tensor_tensor(v, v, r, ALU.mult)
                    at_ += C * n
                step(ins)
                for _, _, gs in parts:
                    for v, g in gs:
                        n = v.shape[2]
                        ins = dve.tensor_tensor(v, v, g.unsqueeze(1).unsqueeze(1).broadcast_to([P, C, n, d]), ALU.mult)
                step(ins)

            def rope(v, hf, scratch):
                n = v.shape[2]
                w = C * n * hf
                v1, v2 = v[:, :, :, 0:hf], v[:, :, :, hf:2 * hf]
                co, si = (t_[:, :, 0:HALF:HALF // hf].unsqueeze(2).broadcast_to([P, C, n, hf]) for t_ in (cosine, sine))
                t = [scratch[:, w * i:w * i + w].rearrange("p (c h d) -> p c h d", c=C, h=n) for i in range(4)]
                dve.tensor_tensor(t[0], v1, co, ALU.mult)
                dve.tensor_tensor(t[1], v2, si, ALU.mult)
                dve.tensor_tensor(t[2], v2, co, ALU.mult)
                step(dve.tensor_tensor(t[3], v1, si, ALU.mult))
                dve.tensor_tensor(v1, t[0], t[1], ALU.subtract)
                step(dve.tensor_tensor(v2, t[2], t[3], ALU.add))

            def attention(items, run, banks):
                n, per = run.n, run.per
                for t in range(n + 5 + 1):
                    if t < n:
                        it, g = items[t], run.first + t
                        dve.wait_ge(scored, g + 1)
                        if t >= 2:
                            dve.wait_ge(exped, g - 1)
                        for m, b_ in enumerate(it.branches):
                            s_ = slice(it.at[m], it.at[m] + b_.nk)
                            ins = dve.tensor_tensor_reduce(run.masked[g % 2][:, s_], SCB[g % 2][:, s_], b_.bias, -it.scale,
                                                           -TAKEN, ALU.add, ALU.min, item_min[:, 2 * t + m:2 * t + m + 1])
                        ins.then_inc(item_masked, 1)
                    if 0 <= t - 1 < n:
                        i = t - 1
                        inv = item_inv[:, 2 * i:2 * i + 2]
                        dve.wait_ge(exped, run.first + i + 1)
                        ins = dve.reciprocal(inv, item_sum[:, 2 * i:2 * i + 2])
                        if items[i].weight is not None:
                            step(ins)
                            ins = dve.tensor_tensor(inv, inv, items[i].weight, ALU.mult)
                        ins.then_inc(item_weighed, 1)
                    if 0 <= t - 3 < n:
                        i = t - 3
                        dve.wait_ge(turned, run.batch + i + 1)
                        if i >= 2:
                            dve.wait_ge(pved, run.outs + i - 1)
                        w = items[i].width
                        dve.tensor_copy(run.probt[i % 2][:, 0:w], TB[(run.batch + i) % 2][:, 0:w]).then_inc(turn_dve, 1)
                    if t >= 5 and (t - 4) % per == 0:
                        bank_ = (t - 4) // per
                        k = banks[bank_ - 1]
                        dve.wait_ge(heads_hi, run.banks + bank_)
                        dve.tensor_tensor(alo[:, 2 * k:2 * k + 2, :], G[k][:, :].rearrange("p (k t) -> p k t", k=2),
                                          ahi[:, 2 * k:2 * k + 2, :].bitcast(F32), ALU.subtract).then_inc(heads_lo, 1)

            def ff_silu_(b, j, static=True):
                n = b.start + j
                for c in range(C):
                    dve.wait_ge(ff_tanh, 2 * n + c + 1)
                    if c == 0 and (not static or n >= 1):
                        dve.wait_ge(ff_turned, n)
                    gate, up, t1 = TB[c][:, 0:FB], TB[c][:, FB:2 * FB], silu[:, c, 1, :]
                    dve.scalar_tensor_tensor(out=t1, in0=silu[:, c, 0, :], scalar=1.0, in1=gate, op0=ALU.add,
                                             op1=ALU.mult).then_inc(flag("silu_half"), 1)
                    dve.wait_ge(flag("silu_half"), 2 * n + c + 1)
                    w = half_scale2[:, c:c + 1] if b.load[0] == "ffn" else half_comb[:, c, bass.ds(j, 1)]
                    ins = dve.scalar_tensor_tensor(out=t1, in0=t1, scalar=w, in1=up, op0=ALU.mult, op1=ALU.mult)
                ins.then_inc(ff_silu, 1)

            def ff_hidden(b, j):
                dve.wait_ge(ff_hi, b.start + j + 1)
                dve.tensor_tensor(FLO, SCB[0][:, :].rearrange("p (f t) -> p f t", f=2), FHI.bitcast(F32),
                                  ALU.subtract).then_inc(ff_lo, 1)

            def blocks(b):
                split_to(b.base + 3)
                ff_silu_(b, 0)
                split_to(b.base + 4)
                ff_hidden(b, 0)
                split_to(b.base + 6)
                ff_silu_(b, 1)
                split_to(b.base + 7)
                first, last, per = loop_turns(b)
                with dve.Fori(first, last) as i:
                    for n in range(per):
                        j = i * per + n
                        ff_hidden(b, j - 1)
                        for c in (1, 2):
                            lo(b.base + 3 * j + c, (b.base + c) % RING, UNIT)
                        ff_silu_(b, j, False)
                        lo(b.base + 3 * j + 3, (b.base + 3) % RING, UNIT)
                at[0] = b.base + 3 * b.last + 1
                for j in range(b.last, b.n):
                    ff_hidden(b, j - 1)
                    split_to(b.base + min(3 * j + 3, 3 * b.n))
                    ff_silu_(b, j)
                    split_to(b.base + min(3 * j + 4, 3 * b.n))
                ff_hidden(b, b.n - 1)

            def add_blocks(b, l):
                split_to(b.base + 3 * b.n + 2)
                dve.wait_ge(unit_used, b.base + 3 * b.n)
                for n in range(2):
                    for c in range(C):
                        xs = x[:, c, 512 * n:512 * n + 512]
                        ins = dve.tensor_tensor(xs, xs, G[2 * c + n][:, :], ALU.add)
                    ins.then_inc(flag(f"ff_added{l}"), 1)

            dve.wait_ge(flag("positions_in"), 16)
            dve.tensor_copy(pos_r[:, :], pos_i[:, :]).then_inc(flag("positions_float"), 1)
            dve.wait_ge(flag("positions_turned"), 1)
            step(dve.tensor_copy(pos_f[:, :], SCB[0][:, 0:C]))
            dve.tensor_copy(cols[:, 0, :], SCB[0][:, 128:208])
            dve.tensor_copy(cols[:, 1, 0:68], SCB[0][:, 256:324]).then_inc(flag("cols_ready"), 1)

            def angles():
                raw_angle = angle[:, 0]
                for i in range(HALF):
                    freq = float(np.float32(ROPE_THETA) ** np.float32(-2.0 * i / (2 * HALF)))
                    ins = dve.tensor_scalar(raw_angle[:, :, i], pos_f[:, :], freq, None, ALU.mult)
                step(ins)
                two_pi = 2 * math.pi
                part1 = 6.28125
                part2 = round((two_pi - part1) * 2 ** 20) / 2 ** 20
                part3 = two_pi - part1 - part2
                turn_, r = angle[:, 1:3], angle[:, 3:5]
                both = raw_angle.unsqueeze(1).broadcast_to([P, 2, C, HALF])
                for n, quarter in ((0, 0.0), (1, 0.25)):
                    ins = dve.tensor_scalar(turn_[:, n], raw_angle, 1 / two_pi, quarter, ALU.mult, ALU.add)
                step(ins)
                step(dve.tensor_scalar(turn_, turn_, 12582912.0, None, ALU.add))
                step(dve.tensor_scalar(turn_, turn_, -12582912.0, None, ALU.add))
                step(dve.scalar_tensor_tensor(out=r, in0=turn_, scalar=-part1, in1=both, op0=ALU.mult, op1=ALU.add))
                for part in (part2, part3):
                    step(dve.scalar_tensor_tensor(out=r, in0=turn_, scalar=-part, in1=r, op0=ALU.mult, op1=ALU.add))
                step(dve.tensor_scalar(r[:, 1], r[:, 1], two_pi / 4, None, ALU.add))
                dve.tensor_scalar(r, r, 3.1415925, -3.1415925, ALU.min, ALU.max).then_inc(flag("angles"), 1)

            for l in range(2):
                s = L[l]
                to_t(s["hturn"], range(4), gain_of(G_MIX[l]), ahi, alo)
                if l == 0:
                    split_to(2)
                row_scales(f"mix{l}")
                if l == 0:

                    def z0(s_, c):
                        return Z0[:, c, s_.c0:s_.c0 + s_.width]

                    in_ = s["in"]
                    va, vq, vk = heads(Z0, AQ, 9, DH), heads(Z0, BQ, 8, DH), heads(Z0, BK, 8, DH)
                    product(in_[0:1], z0)
                    angles()
                    product(in_[1:2], z0)
                    dve.wait_ge(flag("gains_in"), 16 * 16)
                    dve.wait_ge(flag("masks_ready"), 1)
                    dve.wait_ge(flag("rotation"), 1)
                    head_norm([(SQA, va, [(va[:, :, 0:8, :], gains[:, N_AQ, :]), (va[:, :, 8:9, :], gains[:, N_AK, :])])],
                              DH, "a")
                    split_to(in_[1].end + RING)
                    rope(heads(Z0, IQ, 9, 32), 4, ROPET)
                    rope(va, HALF, ROPET)
                    product(in_[2:3], z0)
                    head_norm([(SQQ, vq, [(vq, gains[:, N_BQ, :])])], DH, "bq")
                    split_to(in_[2].end + RING)
                    rope(vq, HALF, ROPET)
                    for n in range(4):
                        dve.tensor_copy(COPIES[:, :, 32 * n:32 * n + 32], Z0[:, :, IK:IW])
                    for n in range(2):
                        dve.tensor_copy(COPIES[:, :, P + DH * n:P + DH * n + DH], Z0[:, :, AK:AV])
                    product(in_[3:4], z0)
                    product(in_[4:5], z0)
                    for b in range(4):
                        dve.wait_ge(turn_act, plan.turn_act[mem_turn + b + 1])
                        for m, (hi_, dst) in enumerate(((bhi, blo), (ahi, alo))):
                            for n in range(2):
                                k = 2 * b + n
                                ins = dve.scalar_tensor_tensor(out=dst[:, k, :], in0=TB[(mem_turn + b) % 2][:, T * n:T * n + T],
                                                               scalar=gain_of(G_SRC[m])(k), in1=hi_[:, k, :].bitcast(F32),
                                                               op0=ALU.mult, op1=ALU.subtract)
                        ins.then_inc(turn_dve, 1)
                    head_norm([(SQK, vk, [(vk, gains[:, N_BK, :])])], DH, "bk")
                    split_to(in_[4].end + RING)
                    rope(vk, HALF, ROPET)
                    dve.sem_inc(flag("qk_ready0"), 1)
                    kv = M[0]["kv"] + M[1]["kv"]
                    dsts = (memk_rows[0], memv[0], memk_rows[1], memv[1])
                    product(kv[0:1], lambda s_, c: dsts[0][:, c, :], scale=mem_scale)
                    turns(s["qturn"], 8, lambda b: feat[:, 512 * b:512 * b + 512])
                    for n in (1, 2):
                        for v in range(2):
                            split_to(kv[n].unit + v + RING)
                            for i in range(8 * n - 8 + 4 * v, 8 * n - 4 + 4 * v):
                                c, h, g = i // 8, i % 8, s["index"] + i
                                nk = P * (c + 1)
                                dve.wait_ge(exped, g + 1)
                                sc, w = dsa_bias[:, c, 0:nk], Z0[:, c, IW + h:IW + h + 1]
                                if h == 0:
                                    dve.tensor_scalar(sc, relu_out[g % 3][:, 0:nk], w, None, ALU.mult).then_inc(item_masked, 1)
                                else:
                                    dve.scalar_tensor_tensor(out=sc, in0=relu_out[g % 3][:, 0:nk], scalar=w, in1=sc, op0=ALU.mult,
                                                             op1=ALU.add).then_inc(item_masked, 1)
                                dve.wait_ge(item_masked, g + 1)
                        product(kv[n:n + 1], lambda s_, c: dsts[n][:, c, :], scale=mem_scale)

                    def best_keys(c):
                        nk = P * (c + 1)
                        sc = dsa_bias[:, c, 0:nk]
                        step(dve.tensor_tensor(sc, sc, causal[:, c, 0:nk], ALU.add))
                        for _ in range(TOPK // 8):
                            step(dve.max(best8, sc))
                            step(dve.match_replace(out=sc, in_to_replace=best8, in_values=sc, imm_value=TAKEN))
                        step(dve.tensor_scalar(sc, sc, TAKEN, NEG, ALU.not_equal, ALU.mult))
                        step(dve.tensor_tensor(sc, sc, causal[:, c, 0:nk], ALU.add))

                    best_keys(0)
                    split_to(kv[2].end + RING)
                    best_keys(1)
                    product(kv[3:4], lambda s_, c: dsts[3][:, c, :], scale=mem_scale)
                    attention(items0(), s["heads"], (2, 3, 0, 1))
                else:
                    product(s["cmp"] + s["keys"][0:1], z1_dst, z1_src)
                    dve.memset(VBLK, 0.0)
                    dve.memset(HID, 0.0)
                    step(dve.memset(POST_GROUP, 0.0))
                    turns(s["cmpkvturn"], 2, lambda b: z[:, 5728 + 512 * b:6240 + 512 * b])
                    dve.wait_ge(turned, s["posturn"] + 1)
                    dve.tensor_copy(POST, TB[s["posturn"] % 2][:, 0:CMP_LEN]).then_inc(turn_dve, 1)
                    vq = [heads(Z1, NQ, 8, DH), heads(Z1, NQ + 512, 8, DH)]
                    vks, vkw = heads(Z1, KSEL, 4, DH), heads(Z1, KWIN, 4, DH)
                    product(s["keys"][1:2], z1_dst, z1_src)
                    head_norm([(SQ1["sel"], vks, [(vks, gains[:, N_KS, :])]), (SQ1["win"], vkw, [(vkw, gains[:, N_KW, :])])],
                              DH, "keys")
                    rope(vks, HALF, ROPET1)
                    rope(vkw, HALF, ROPET1)
                    product(s["q0"], z1_dst, z1_src)
                    head_norm([(SQ1["q0"], vq[0], [(vq[0], gains[:, N_NQ, :])])], DH, "q0")
                    dve.sem_inc(flag("q_plain1"), 1)
                    split_to(s["q0"][-1].end + RING)
                    turns(s["q0turn"], 2, lambda b: feat[:, 512 * b:512 * b + 512])
                    rope(vq[0], HALF, ROPET1)
                    dve.sem_inc(flag("qk_ready1"), 1)
                    product(s["q1"], z1_dst, z1_src)
                    head_norm([(SQ1["q1"], vq[1], [(vq[1], gains[:, N_NQ, :])])], DH, "q1")
                    dve.sem_inc(flag("q_plain1"), 1)
                    split_to(s["q1"][-1].end + RING)
                    dve.wait_ge(flag("cmp_w1_done"), 1)
                    dve.tensor_copy(s_t[0:DH, 0:1], SCB[0][0:DH, 60:61])
                    step(dve.tensor_copy(s_t[0:DH, 1:2], SCB[1][0:DH, 60:61]))
                    for n in range(2):
                        ins = dve.tensor_scalar(HID[:, n, :, 0:N_CMP],
                                                SCB[n][0:DH, 0:60].rearrange("p (g n) -> p g n", g=4),
                                                s_t[0:DH, n:n + 1], None, ALU.add)
                    ins.then_inc(flag("cmp_hidden"), 1)
                    dve.wait_ge(flag("cmp_tanh"), 1)
                    step(dve.scalar_tensor_tensor(out=HIT, in0=HIT, scalar=1.0, in1=HID, op0=ALU.add, op1=ALU.mult))
                    step(dve.tensor_scalar(HIT, HIT, 0.5, None, ALU.mult))
                    for j in range(4):
                        ins = dve.tensor_copy(HIV[:, :, j, :], HIT[:, 1, :, :])
                    ins.then_inc(flag("cmp_silu"), 1)
                    turns(s["q1turn"], 2, lambda b: feat[:, 1024 + 512 * b:1536 + 512 * b])
                    turns(s["qrturn"], 4, lambda b: (feat[:, 2048:2560], feat[:, 2560:3072], feat[:, 4096:4608], KWT)[b])
                    dve.wait_ge(flag("cmp_w2_done"), 1)
                    bank = SCB[1]
                    step(dve.tensor_copy(KCN[:, 0, :], bank[:, 0:DH]))
                    step(dve.tensor_tensor(KCN[:, 1, :], KCN[:, 0, :], KCN[:, 0, :], ALU.mult))
                    step(dve.tensor_reduce(s_mean[:, 0:1], KCN[:, 1, :], AX, ALU.add))
                    rsqrt(1, DH)
                    step(dve.tensor_scalar(KCN[:, 0, :], KCN[:, 0, :], s_y[:, 0:1], None, ALU.mult))
                    step(dve.tensor_tensor(KCN[:, 0, :], KCN[:, 0, :], gains[:, N_KC, :], ALU.mult))
                    step(dve.tensor_copy(KCN[:, 1, :], KCN[:, 0, :]))
                    for j in range(4):
                        r = slice(32 * j, 32 * j + 32)
                        ins = dve.tensor_copy(VBLK[r, :, j, :], bank[r, 128:384].rearrange("p (g d) -> p g d", g=4))
                    ins.then_inc(flag("cmp_kv_ready"), 1)
                    rope(vq[1], HALF, ROPET1)
                    dve.sem_inc(flag("qk_ready1"), 1)
                    product(s["vg"], z1_dst, z1_src)
                    dve.wait_ge(turned, s["kcturn"] + 1)
                    dve.tensor_copy(KCT, TB[s["kcturn"] % 2][:, 0:P]).then_inc(turn_dve, 1)
                    dve.wait_ge(flag("gates_tanh"), 1)
                    step(dve.tensor_scalar(GATE, GATE, 0.5, 0.5, ALU.mult, ALU.add))
                    def by_head(b_):
                        return b_.rearrange("p (h n) -> p h n", h=16)

                    for c in range(C):
                        dve.wait_ge(flag("cmp_scored"), c + 1)
                        bias = cmp_bias[:, c, :].unsqueeze(1).broadcast_to([P, 4, 32])
                        for n in range(2):
                            for b in range(2):
                                ins = dve.scalar_tensor_tensor(
                                    out=CS[c][:, T * b + P * n:T * b + P * n + P].rearrange("p (h m) -> p h m", h=4),
                                    in0=SCB[n][:, P * b:P * b + P].rearrange("p (h m) -> p h m", h=4), scalar=DH ** -0.5,
                                    in1=bias, op0=ALU.mult, op1=ALU.add)
                        ins.then_inc(flag("cmp_read"), 1)
                        dve.wait_ge(flag("cmp_read"), c + 1)
                        step(dve.tensor_reduce(s_t[:, 16 * c:16 * c + 16], by_head(CS[c]), AX, ALU.max))
                        dve.tensor_tensor(by_head(CS[c]), by_head(CS[c]),
                                          s_t[:, 16 * c:16 * c + 16].unsqueeze(2).broadcast_to([P, 16, 32]), ALU.subtract
                                          ).then_inc(flag("cmp_shifted"), 1)
                    turns(s["qrturn2"], 2, lambda b: feat[:, 3072 + 512 * b:3584 + 512 * b])
                    for c in range(C):
                        cp4 = by_head(CP[c])
                        keep = cmp_keep[:, c, :].unsqueeze(1).broadcast_to([P, 16, 32])
                        dve.wait_ge(flag("cmp_exp"), c + 1)
                        step(dve.tensor_tensor(cp4, cp4, keep, ALU.mult))
                        step(dve.tensor_reduce(s_t[:, 0:16], cp4, AX, ALU.add))
                        step(dve.tensor_scalar(s_t[:, 0:16], s_t[:, 0:16], TINY, None, ALU.max))
                        step(dve.reciprocal(s_u[:, 0:16], s_t[:, 0:16]))
                        gate = GATE[:, c, :].rearrange("p (h b) -> p h b", b=3)[:, :, 0]
                        step(dve.tensor_tensor(s_u[:, 0:16], s_u[:, 0:16], gate, ALU.mult))
                        dve.tensor_tensor(cp4, cp4, s_u[:, 0:16].unsqueeze(2).broadcast_to([P, 16, 32]), ALU.mult
                                          ).then_inc(flag("cmp_prob"), 1)
                    turns(s["cmpturn"], 2, lambda b: CPT[b])
                    attention(items1(), s["heads"], (2, 3, 0, 1))
                product(s["out"][0:1], None)
                mk = heads(memk_rows[l], 0, 4, P)
                head_norm([(heads(zv(4944, 512), 0, 4, P), mk, [(mk, mem_k_gain[:, l, :])])], P, f"mk{l}")
                dve.sem_inc(flag("mem_k_normed"), 1)
                to_t(s["mturn"], range(2), gain_of(G_MEM[l]), bhi, blo)
                product(s["out"][1:2], None)
                to_t(s["mturn"], range(2, 4), gain_of(G_MEM[l]), bhi, blo)
                row_scales(f"memq{l}")
                for n in range(2):
                    product(s["mq"][n:n + 1], lambda s_, c: ZM[:, c, s_.c0:s_.c0 + 256])
                    vm = heads(ZM, 256 * n, 2, P)
                    dve.wait_ge(flag(f"head_squares_memq{l}"), n + 1)
                    head_norm([(heads(zv(2048, 512), 256 * n, 2, P), vm, [(vm, mem_q_gain[:, l, :])])], P, f"memq{l}")
                dve.sem_inc(flag(f"mem_q_ready{l}"), 1)
                turns(s["mqturn"], 2, lambda b: feat[:, 512 * b:512 * b + 512])
                split_to(s["mo"][-1].end)
                attention(items_mem(l), s["mheads"], (0, 1))
                product(s["mo"][0:1], None)
                to_t(s["fturn"], range(2), gain_of(G_FFN[l]), bhi, blo)
                product(s["mo"][1:2], None)
                to_t(s["fturn"], range(2, 4), gain_of(G_FFN[l]), bhi, blo)
                row_scales(f"ffn{l}")
                blocks(s["ff"])
                add_blocks(s["ff"], l)

            to_t(N["hturn"], range(4), gain_of(G_N1), ahi, alo)
            row_scales("mix2")
            def decay_rates():
                lam = cols[:, 1, R_LAM:R_LAM + 8]
                l0, l1, l2, l3 = (LAM[:, i, :] for i in range(4))
                step(dve.tensor_scalar(l0, lam, -1.0, None, ALU.mult))
                dve.tensor_tensor(l1, l0, lam, ALU.min).then_inc(flag("minus_abs_lambda"), 1)
                dve.wait_ge(flag("exp_lambda"), 1)
                step(dve.tensor_scalar(l2, l1, 2.0, None, ALU.add))
                step(dve.reciprocal(l2, l2))
                step(dve.tensor_tensor(l1, l1, l2, ALU.mult))
                step(dve.tensor_tensor(l2, l1, l1, ALU.mult))
                step(dve.tensor_scalar(l3, l2, 1 / 17, 1 / 15, ALU.mult, ALU.add))
                for n in (13, 11, 9, 7, 5, 3, 1):
                    step(dve.tensor_tensor(l3, l3, l2, ALU.mult))
                    step(dve.tensor_scalar(l3, l3, 1 / n, None, ALU.add))
                step(dve.tensor_tensor(l3, l3, l1, ALU.mult))
                step(dve.tensor_scalar(l0, l0, 0.0, 0.5, ALU.max, ALU.mult))
                step(dve.tensor_tensor(l3, l3, l0, ALU.add))
                step(dve.tensor_scalar(SP4[:, 0:8], l3, 8.0, None, ALU.mult))
                for n, r in enumerate((R_BR, R_BI)):
                    step(dve.tensor_scalar(HB[:, n, :], cols[:, 1, r:r + 8], 0.5, None, ALU.mult))

            def convolve(k):
                wc = [cols[:, 1, 8 * n + k:8 * n + k + 1] for n in range(4)]
                step(dve.tensor_scalar(XC[:, k, :], ULT[:, k, :], wc[3], cols[:, 1, R_CB + k:R_CB + k + 1], ALU.mult, ALU.add))
                for n in (2, 1, 0):
                    back = 3 - n
                    ins = dve.scalar_tensor_tensor(out=XC[:, k, back:T], in0=ULT[:, k, 0:T - back], scalar=wc[n],
                                                   in1=XC[:, k, back:T], op0=ALU.mult, op1=ALU.add)
                    step(ins) if n else ins.then_inc(flag("convolved"), 1)

            for n in range(5):
                product(N["in"][n:n + 1], lambda s_, c: ZA[:, n, c, :])
                if n == 3:
                    decay_rates()
                if n == 4:
                    split_to(N["in"][4].end + RING)
                turns(N["uturn"] + 2 * n, 2, lambda b: feat[:, 1024 * n + 512 * b:1024 * n + 512 * b + 512])
                if n < 2:
                    convolve(4 * n)
                    convolve(4 * n + 1)
                    split_to(N["in"][n].end + RING)
                    convolve(4 * n + 2)
                    convolve(4 * n + 3)
            for n in range(2):
                ug = UGT[:, 4 * n:4 * n + 4, :]
                step(dve.tensor_tensor(GELU[n], ug, ug, ALU.mult))
                step(dve.tensor_scalar(GELU[n], GELU[n], 0.044715, 1.0, ALU.mult, ALU.add))
                dve.tensor_tensor(GELU[n], GELU[n], ug, ALU.mult).then_inc(flag("gelu_inner"), 1)
            product(N["gates"][0:1], lambda s_, c: ZG[:, c, s_.c0 - GA:s_.c0 - GA + 512])
            dve.wait_ge(flag("gelu_tanh"), 1)
            for n in range(2):
                ug = UGT[:, 4 * n:4 * n + 4, :]
                dve.scalar_tensor_tensor(out=ug, in0=GELU[n], scalar=1.0, in1=ug, op0=ALU.add, op1=ALU.mult).then_inc(flag("gelu"), 1)
            product(N["gates"][1:2], lambda s_, c: ZG[:, c, s_.c0 - GA:s_.c0 - GA + 512])
            dve.wait_ge(turn_act, plan.turn_act[N["gturn"] + 8])
            for k in range(8):
                ins = dve.tensor_scalar(RG[:, k, :], RG[:, k, :], SP4[:, k:k + 1], SP4[:, k:k + 1], ALU.mult, ALU.add)
            ins.then_inc(flag("log_decay"), 1)
            dve.wait_ge(flag("convolved"), 8)
            step(dve.scalar_tensor_tensor(out=XC, in0=IG, scalar=1.0, in1=XC, op0=ALU.add, op1=ALU.mult))
            split_to(N["gates"][1].end + RING)
            product(N["gates"][2:4], lambda s_, c: ZG[:, c, s_.c0 - GA:s_.c0 - GA + 512])
            dve.wait_ge(flag("decay_tanh"), 1)
            step(dve.tensor_tensor(IG, ULT, ULT, ALU.mult))
            dve.scalar_tensor_tensor(out=RG, in0=IG, scalar=1.0, in1=RG, op0=ALU.add, op1=ALU.mult).then_inc(flag("drive_squared"), 1)
            to_t(N["yturn"], range(2), lambda k: cols[:, 1, R_PS + k:R_PS + k + 1], ahi, alo)
            dve.wait_ge(flag("drive_scale"), 1)
            step(dve.tensor_tensor(XC, XC, RG, ALU.mult))
            for k in range(8):
                ins = dve.tensor_tensor_scan(IG[:, k, :], ULT[:, k, :], XC[:, k, :], 0.0, ALU.mult, ALU.add)
            step(ins)
            dve.wait_ge(flag("gelu"), 2)
            dve.scalar_tensor_tensor(out=ULT, in0=IG, scalar=0.5, in1=UGT, op0=ALU.mult, op1=ALU.mult).then_inc(flag("lru_out"), 1)
            dve.wait_ge(flag("lru_hi"), 1)
            dve.tensor_tensor(blo[:, :, :], ULT, bhi[:, :, :].bitcast(F32), ALU.subtract).then_inc(flag("lru_done"), 1)
            dve.wait_ge(flag("mix_gates"), 1)

            def mix_a(s_, c):
                g_ = ZG[:, c, s_.c0:s_.c0 + 512]
                dve.scalar_tensor_tensor(out=g_, in0=g_, scalar=1.0, in1=bank_of(s_, c), op0=ALU.add, op1=ALU.mult
                                         ).then_inc(slab_dve, 1)

            def mix_b(s_, c):
                g_, y_ = ZG[:, c, D + s_.c0:D + s_.c0 + 512], ZG[:, c, s_.c0:s_.c0 + 512]
                step(dve.scalar_tensor_tensor(out=g_, in0=g_, scalar=1.0, in1=bank_of(s_, c), op0=ALU.add, op1=ALU.mult))
                dve.tensor_tensor(y_, y_, g_, ALU.add).then_inc(slab_dve, 1)

            product(N["pa"], mix_a)
            product(N["pb"][0:1], mix_b)
            to_t(N["oturn"], range(2), 0.5, ahi, alo)
            product(N["pb"][1:2], mix_b)
            to_t(N["oturn"], range(2, 4), 0.5, ahi, alo)
            dve.wait_ge(flag("router_hi"), 1)
            dve.tensor_tensor(rlo[:, :, :], route_w, rhi[:, :, :].bitcast(F32), ALU.subtract).then_inc(flag("router_lo"), 1)
            product(N["out"][0:1], None)
            to_t(N["h2turn"], range(2), gain_of(G_N2), bhi, blo)
            product(N["out"][1:2], None)
            to_t(N["h2turn"], range(2, 4), gain_of(G_N2), bhi, blo)
            row_scales("moe")

            split_to(N["moe"].base + RING)
            dve.wait_ge(flag("routed"), 1)
            gl, el = rt[:, 0, :, 0:N_GRP], rt[:, 2, :, :]
            lg = SCB[1][:, 0:40].rearrange("p (c n) -> p c n", c=C)
            for c in range(C):
                dve.scalar_tensor_tensor(out=gl[:, c, :], in0=lg[:, c, 0:N_GRP], scalar=row_scale[:, c:c + 1],
                                         in1=route_b[:, 0:N_GRP], op0=ALU.mult, op1=ALU.add)
                ins = dve.scalar_tensor_tensor(out=el[:, c, :], in0=lg[:, c, N_GRP:20], scalar=row_scale[:, c:c + 1],
                                               in1=route_b[:, N_GRP:20], op0=ALU.mult, op1=ALU.add)
            step(ins)
            iota = rt[:, 3, :, :]
            for e in range(N_EXP):
                ins = dve.memset(iota[:, :, e:e + 1], float(e - N_EXP))
            step(ins)

            def first_best(v, n, best, hot, t_):
                step(dve.tensor_reduce(best, v, AX, ALU.max))
                step(dve.tensor_tensor(t_, v, best.broadcast_to([P, C, n]), ALU.is_equal))
                step(dve.tensor_tensor(t_, t_, iota[:, :, 0:n], ALU.mult))
                step(dve.tensor_reduce(rt[:, 11, :, 0:1], t_, AX, ALU.min))
                step(dve.tensor_tensor(hot, iota[:, :, 0:n], rt[:, 11, :, 0:1].broadcast_to([P, C, n]), ALU.is_equal))

            gbest, ghot = rt[:, 4, :, 0:1], rt[:, 5, :, 0:N_GRP]
            first_best(gl, N_GRP, gbest, ghot, rt[:, 10, :, 0:N_GRP])
            dve.tensor_tensor(gl, gl, gbest.broadcast_to([P, C, N_GRP]), ALU.subtract).then_inc(flag("group_shifted"), 1)
            dve.wait_ge(flag("group_exp"), 1)
            step(dve.tensor_reduce(rt[:, 4, :, 1:2], rt[:, 1, :, 0:N_GRP], AX, ALU.add))
            p_top = rt[:, 4, :, 2:3]
            step(dve.reciprocal(p_top, rt[:, 4, :, 1:2]))
            g16 = rt[:, 6, :, :]
            for g in range(N_GRP):
                ins = dve.tensor_copy(g16[:, :, PER_GRP * g:PER_GRP * g + PER_GRP], ghot[:, :, g:g + 1].broadcast_to([P, C, PER_GRP]))
            step(ins)
            step(dve.tensor_tensor(el, el, g16, ALU.mult))
            step(dve.tensor_scalar(g16, g16, -NEG, NEG, ALU.mult, ALU.add))
            step(dve.tensor_tensor(el, el, g16, ALU.add))
            best1, hot1, best2, hot2 = rt[:, 4, :, 3:4], rt[:, 7, :, :], rt[:, 4, :, 4:5], rt[:, 6, :, :]
            first_best(el, N_EXP, best1, hot1, rt[:, 10, :, :])
            step(dve.tensor_scalar(hot2, hot1, 3 * NEG, None, ALU.mult))
            step(dve.tensor_tensor(el, el, hot2, ALU.add))
            first_best(el, N_EXP, best2, hot2, rt[:, 10, :, :])
            dve.tensor_tensor(rt[:, 8, :, 0:1], best2, best1, ALU.subtract).then_inc(flag("expert_gap"), 1)
            dve.wait_ge(flag("expert_exp"), 1)
            e_, w1, w2_ = rt[:, 9, :, 0:1], rt[:, 9, :, 1:2], rt[:, 9, :, 2:3]
            step(dve.tensor_scalar(w1, e_, 1.0, None, ALU.add))
            step(dve.reciprocal(w1, w1))
            step(dve.tensor_tensor(w1, w1, p_top, ALU.mult))
            step(dve.tensor_tensor(w2_, w1, e_, ALU.mult))
            step(dve.tensor_tensor(hot1, hot1, w1.broadcast_to([P, C, N_EXP]), ALU.mult))
            step(dve.tensor_tensor(hot2, hot2, w2_.broadcast_to([P, C, N_EXP]), ALU.mult))
            step(dve.tensor_tensor(hot1, hot1, hot2, ALU.add))
            for n in range(2):
                for c in range(C):
                    ins = dve.tensor_scalar(half_comb.rearrange("p c (e n) -> p c e n", n=2)[:, c, :, n], hot1[:, c, :],
                                            half_scale2[:, c:c + 1], None, ALU.mult)
            step(ins)
            blocks(N["moe"])
            add_blocks(N["moe"], 2)
            dve.wait_ge(flag("ff_added2"), 2)
            dve.wait_ge(flag("squared_final"), 1)
            step(dve.tensor_copy(s_mean[:, 0:C], sumsq[:, 0:C]))
            rsqrt(C, D)
            dve.wait_ge(flag("final_gain_in"), 16)
            for c in range(C):
                dve.scalar_tensor_tensor(out=XN[:, c, :], in0=x[:, c, :], scalar=s_y[:, c:c + 1], in1=final_gain,
                                         op0=ALU.mult, op1=ALU.mult).then_inc(flag("out_ready"), 1)

        @block.tensor
        def _(pe):
            def mm3(dst, lhi, llo, rhi_, rlo_, start, stop):
                pe.matmul(dst, lhi, rhi_, start=start, stop=False)
                pe.matmul(dst, lhi, rlo_, start=False, stop=False)
                return pe.matmul(dst, llo, rhi_, start=False, stop=stop)

            def unit_ready(u):
                pe.wait_ge(lo_dve, u + 1)
                pe.wait_ge(lo_pool, u + 1)

            def product(slabs, lhi, llo, between=None, left=None, ready=None):
                group = 0
                for s in slabs:
                    if s.index >= 2:
                        before = plan.slabs[s.index - 2]
                        pe.wait_ge(slab_act, before.done_act)
                        pe.wait_ge(slab_dve, before.done_dve)
                    for i in range(s.units):
                        u, nk = s.unit + i, min(4, s.k)
                        unit_ready(u)
                        if left is not None:
                            emptied(left + 2 * i + 2)
                        if ready:
                            ready(i)
                        wh, wl = (w[u % RING][:, 0:nk * s.width].rearrange("p (k n) -> p k n", k=nk) for w in (whi, wlo))
                        for c in range(C):
                            if between:
                                between(group)
                            group += 1
                            for k in range(nk):
                                kk = 4 * s.order[i] + k
                                ins = mm3(bank_of(s, c), lhi[:, kk, P * c:P * c + P], llo[:, kk, P * c:P * c + P],
                                          wh[:, k, :], wl[:, k, :], i + k == 0, 4 * i + k == s.k - 1)
                        ins.then_inc(unit_used, 1)

            def turn_free(n):
                if n >= 2:
                    if plan.turn_act[n - 1]:
                        pe.wait_ge(turn_act, plan.turn_act[n - 1])
                    if plan.turn_dve[n - 1]:
                        pe.wait_ge(turn_dve, plan.turn_dve[n - 1])
                return turn_bank(n)

            def emptied(n):
                pe.wait_ge(turn_act, plan.turn_act[n]) if plan.turn_act[n] else None
                pe.wait_ge(turn_dve, plan.turn_dve[n]) if plan.turn_dve[n] else None

            def to_t(base, nk, src):
                for b in range(nk // 2):
                    bank = turn_free(base + b)
                    for n in range(2):
                        for c in range(C):
                            ins = pe.transpose(bank[:, T * n + P * c:T * n + P * c + P], src(c, 2 * b + n), ident[:, :])
                    ins.then_inc(turned, 1)
                emptied(base + nk // 2)

            def half_t(base, part, src, sem_, count):
                pe.wait_ge(sem_, count)
                for b in (2 * part, 2 * part + 1):
                    bank = turn_free(base + b)
                    for n in range(2):
                        for c in range(C):
                            ins = pe.transpose(bank[:, T * n + P * c:T * n + P * c + P], src(c, 2 * b + n), ident[:, :])
                    ins.then_inc(turned, 1)

            def turns(base, jobs, drain=True):
                for b in range(len(jobs) // 2):
                    bank = turn_free(base + b)
                    for n in range(2):
                        for c in range(C):
                            ins = pe.transpose(bank[:, T * n + P * c:T * n + P * c + P], jobs[2 * b + n](c), ident[:, :])
                    ins.then_inc(turned, 1)
                if drain:
                    emptied(base + len(jobs) // 2)

            def attention(items, run):
                n = run.n
                for t in range(n + 4):
                    if t < n:
                        it, g = items[t], run.first + t
                        if g >= 2:
                            pe.wait_ge(item_masked, g - 1)
                        for m, b_ in enumerate(it.branches):
                            ins = pe.matmul(SCB[g % 2][:, it.at[m]:it.at[m] + b_.nk], b_.q, b_.k, start=True, stop=True)
                        ins.then_inc(scored, 1)
                    if 0 <= t - 3 < n:
                        i = t - 3
                        pe.wait_ge(prob_scaled, run.outs + i + 1)
                        bank = turn_free(run.batch + i)
                        for b in range(items[i].width // P):
                            ins = pe.transpose(bank[:, P * b:P * b + P], run.prob[(run.first + i) % 4][:, P * b:P * b + P], ident[:, :])
                        ins.then_inc(turned, 1)
                    if 0 <= t - 4 < n:
                        i = t - 4
                        it = items[i]
                        pe.wait_ge(turn_dve, plan.turn_dve[run.batch + i + 1])
                        if it.first:
                            pe.matmul(it.branches[0].out, it.first[0], it.first[1], start=True, stop=False)
                        for m, b_ in enumerate(it.branches):
                            for b, v in enumerate(b_.v):
                                a_ = it.at[m] + P * b
                                ins = pe.matmul(b_.out, v, run.probt[i % 2][:, a_:a_ + P], start=b == 0 and not it.first,
                                                stop=b == len(b_.v) - 1 and (m == 1 or not it.first))
                        ins.then_inc(pved, 1)

            def ff_up(b, j, static=True, between=None):
                u0 = b.base + 3 * j - (0 if isinstance(j, int) and j == 0 else 1)
                s0 = b.base % RING if isinstance(j, int) and j == 0 else (b.base - 1) % RING
                if not static or b.start + j >= 1:
                    pe.wait_ge(ff_silu, b.start + j)
                for half_ in range(2):
                    unit_ready(u0 + half_)
                    if between and half_:
                        emptied(b.left + 4)
                    slot = (s0 + half_) % RING
                    for c in range(C):
                        if between and half_ == 0 and c == 1:
                            between()
                        for k in range(4):
                            kk = 4 * half_ + k
                            ins = mm3(TB[c][:, :], bhi[:, kk, P * c:P * c + P], blo[:, kk, P * c:P * c + P],
                                      whi[slot][:, 512 * k:512 * k + 512], wlo[slot][:, 512 * k:512 * k + 512],
                                      kk == 0, kk == KC - 1)
                    ins.then_inc(unit_used, 1)

            def ff_turn(b, j, static=True):
                n = b.start + j
                pe.wait_ge(ff_silu, n + 1)
                if not static or n >= 1:
                    pe.wait_ge(ff_lo, n)
                for f in range(2):
                    for c in range(C):
                        ins = pe.transpose(SCB[0][:, T * f + P * c:T * f + P * c + P], silu[:, c, 1, P * f:P * f + P], ident[:, :])
                ins.then_inc(ff_turned, 1)

            def ff_down(b, j, slot, first=False, last=False, u=None):
                pe.wait_ge(ff_lo, b.start + j + 1)
                unit_ready(u)
                for c in range(C):
                    for f in range(2):
                        for n in range(2):
                            w = slice(D * f + 512 * n, D * f + 512 * n + 512)
                            ins = mm3(G[2 * c + n][:, :], ahi[:, f, P * c:P * c + P], alo[:, f, P * c:P * c + P],
                                      whi[slot][:, w], wlo[slot][:, w], first and f == 0, last and f == 1)
                ins.then_inc(unit_used, 1)

            def blocks(b, between=None):
                s = (b.base + 1) % RING
                ff_up(b, 0, between=between)
                ff_turn(b, 0)
                ff_up(b, 1)
                ff_down(b, 0, s, first=True, u=b.base + 4)
                first, last, per = loop_turns(b)
                with pe.Fori(first, last) as i:
                    for n in range(per):
                        j = i * per + n
                        ff_turn(b, j - 1, False)
                        ff_up(b, j, False)
                        ff_down(b, j - 1, s, u=b.base + 3 * j + 1)
                for j in range(b.last, b.n):
                    ff_turn(b, j - 1)
                    ff_up(b, j)
                    ff_down(b, j - 1, s, u=b.base + 3 * j + 1)
                ff_turn(b, b.n - 1)
                ff_down(b, b.n - 1, (b.base + 3 * b.n - 1) % RING, last=True, u=b.base + 3 * b.n - 1)

            pe.wait_ge(flag("masks_ready"), 1)
            pe.wait_ge(flag("positions_float"), 1)
            pe.wait_ge(flag("rows_in"), 16 * 16)
            pe.transpose(SCB[0][:, 0:C], pos_r[:, :], ident[0:C, 0:C])
            pe.transpose(SCB[0][:, 128:208], rows[:, 0, :], ident[0:80, 0:80])
            pe.transpose(SCB[0][:, 256:324], rows[0:68, 1, :], ident[0:68, 0:68]).then_inc(flag("positions_turned"), 1)

            for l in range(2):
                s = L[l]
                if l == 0:
                    pe.wait_ge(flag("x_in"), 16)
                    to_t(s["hturn"], KC, xsrc)
                    product(s["in"], ahi, alo)
                    pe.wait_ge(flag("mem_in"), 16)
                    to_t(mem_turn, KC, lambda c, k: MEMIN[:, c, P * k:P * k + P])
                    product(M[0]["kv"][0:1], bhi, blo)
                    pe.wait_ge(flag("qk_ready0"), 1)
                    turns(s["qturn"], JOBS0)
                    index_item = [0]

                    def two_logits(group):
                        for i in range(index_item[0], index_item[0] + 2):
                            c, h, g = i // 8, i % 8, s["index"] + i
                            r = slice(32 * (h % 4), 32 * (h % 4) + 32)
                            if i >= 2:
                                pe.wait_ge(exped, g - 1)
                            pe.matmul(SCB[g % 2][:, 0:P * (c + 1)], feat[r, T * (h // 4) + P * c:T * (h // 4) + P * c + P],
                                      feat[r, 512:512 + P * (c + 1)], start=True, stop=True,
                                      tile_position=(32 * (h % 4), 0)).then_inc(scored, 1)
                        index_item[0] += 2

                    product(M[0]["kv"][1:2], bhi, blo, two_logits)
                    product(M[1]["kv"][0:1], ahi, alo, two_logits)
                    product(M[1]["kv"][1:2], ahi, alo)
                    pe.wait_ge(slab_act, M[1]["kv"][-1].done_act)
                    pe.wait_ge(slab_dve, M[1]["kv"][-1].done_dve)
                    attention(items0(), s["heads"])
                else:
                    half_t(s["hturn"], 0, xsrc, flag("ff_added0"), 1)

                    def keys_between(group):
                        if group == 1:
                            half_t(s["hturn"], 1, xsrc, flag("ff_added0"), 2)
                        if group == 9:
                            turns(s["cmpkvturn"], JOBSC, drain=False)
                            bank = turn_free(s["posturn"])
                            pe.transpose(bank[:, 0:CMP_LEN], pos_rows[:, :], ident[0:CMP_LEN, 0:CMP_LEN]).then_inc(turned, 1)

                    def q1_between(group):
                        if group == 3:
                            pe.wait_ge(flag("q_plain1"), 1)
                            turns(s["q0turn"], JOBSQ[0:4], drain=False)

                    product(s["cmp"] + s["keys"] + s["q0"], ahi, alo, left=s["hturn"], between=keys_between)
                    product(s["q1"], ahi, alo, between=q1_between)
                    emptied(s["posturn"] + 1)
                    pe.wait_ge(flag("cmp_weights_in"), 32)
                    for n in range(2):
                        r = slice(DH * n, DH * n + DH)
                        for j in range(CMP_LEN):
                            ins = pe.matmul(SCB[n][0:DH, 0:75].rearrange("p (g n) -> p g n", g=5), CMPW[r, j, :],
                                            KCVT[r, :, j:j + CMP_STRIDE * (N_CMP - 1) + 1:CMP_STRIDE], start=j == 0, stop=j == CMP_LEN - 1)
                    ins.then_inc(flag("cmp_w1_done"), 1)
                    pe.wait_ge(flag("q_plain1"), 2)
                    turns(s["q1turn"], JOBSQ[4:8], drain=False)

                    def vg_between(group):
                        if group == 0:
                            pe.wait_ge(flag("qk_ready1"), 1)
                            turns(s["qrturn"], JOBSQ[0:4] + JOBSK, drain=False)
                        if group == 2:
                            pe.wait_ge(flag("cmp_silu"), 1)
                            pe.matmul(SCB[1][:, 0:DH], HIT[:, 0, :, :].rearrange("p g n -> p (g n)"), w2[:, 0, :],
                                      start=True, stop=True)
                            for g in range(4):
                                ins = pe.matmul(SCB[1][:, 128 + DH * g:128 + DH * g + DH],
                                                HIV[:, g, :, :].rearrange("p j n -> p (j n)"), w2[:, 1, :], start=True, stop=True)
                            ins.then_inc(flag("cmp_w2_done"), 1)

                    product(s["vg"], ahi, alo, between=vg_between)
                    pe.wait_ge(flag("cmp_kv_ready"), 1)
                    bank = turn_free(s["kcturn"])
                    pe.transpose(bank[:, 0:P], KCN.rearrange("p a d -> p (a d)"), ident[:, :]).then_inc(turned, 1)
                    emptied(s["kcturn"] + 1)
                    for c in range(C):
                        if c:
                            pe.wait_ge(flag("cmp_read"), c)
                        for h in range(16):
                            (jq, half_), g = place1(h), h // 4
                            r = slice(DH * half_, DH * half_ + DH)
                            at_ = P * (g // 2) + 32 * (h % 4)
                            ins = pe.matmul(SCB[half_][:, at_:at_ + 32], feat[r, T * jq + P * c:T * jq + P * c + P],
                                            KCT[r, 32 * g:32 * g + 32], start=True, stop=True)
                        ins.then_inc(flag("cmp_scored"), 1)
                    pe.wait_ge(flag("qk_ready1"), 2)
                    turns(s["qrturn2"], JOBSQ[4:8], drain=False)
                    for c in range(C):
                        pe.wait_ge(flag("cmp_prob"), c + 1)
                        bank = turn_free(s["cmpturn"] + c)
                        for g in range(4):
                            ins = pe.transpose(bank[:, P * g:P * g + P], CP[c][:, P * g:P * g + P], ident[:, :])
                        ins.then_inc(turned, 1)
                    emptied(s["cmpturn"] + 2)
                    attention(items1(), s["heads"])
                product(s["out"], ahi, alo, ready=lambda i: pe.wait_ge(heads_lo, s["heads"].banks + 2 * i + 2),
                        between=lambda group:
                        half_t(s["mturn"], 0, xsrc, slab_dve, s["out"][0].done_dve) if group == 6 else None)
                product(s["mq"], bhi, blo, left=s["mturn"], between=lambda group:
                        half_t(s["mturn"], 1, xsrc, slab_dve, s["out"][1].done_dve) if group == 1 else None)
                pe.wait_ge(flag("mem_k_normed"), l + 1)
                turns(M[l]["kturn"], [lambda c, h=h: memk_rows[l][:, c, P * h:P * h + P] for h in range(4)])
                pe.wait_ge(flag(f"mem_q_ready{l}"), 1)
                turns(s["mqturn"], JOBSM)
                attention(items_mem(l), s["mheads"])
                pe.wait_ge(heads_lo, s["mheads"].banks + 2)
                product(s["mo"], ahi, alo, between=lambda group:
                        half_t(s["fturn"], 0, xsrc, slab_dve, s["mo"][0].done_dve) if group == 3 else None)
                s["ff"].left = s["fturn"]
                emptied(s["fturn"] + 2)
                blocks(s["ff"], lambda: half_t(s["fturn"], 1, xsrc, slab_dve, s["mo"][1].done_dve))

            half_t(N["hturn"], 0, xsrc, flag("ff_added1"), 1)

            def slab_turns(n):
                s_ = N["in"][n]
                pe.wait_ge(slab_act, s_.done_act)
                pe.wait_ge(slab_dve, s_.done_dve)
                turns(N["uturn"] + 2 * n, [lambda c, k=k: ZA[:, n, c, P * k:P * k + P] for k in range(4)], drain=False)

            def in2_between(group):
                if group == 1:
                    half_t(N["hturn"], 1, xsrc, flag("ff_added1"), 2)
                elif group % 4 == 1:
                    slab_turns(group // 4 - 1)

            product(N["in"], ahi, alo, left=N["hturn"], between=in2_between)

            def gate_matmuls(k):
                pe.wait_ge(flag("convolved"), k + 1)
                bank = turn_free(N["gturn"] + k)
                for n in range(2):
                    ins = pe.matmul(bank[:, T * n:T * n + T], GATEW[:, n, k, :], XC[:, k, :], start=True, stop=True)
                ins.then_inc(turned, 1)

            def gates_between(group):
                if group == 1:
                    slab_turns(4)
                    pe.wait_ge(flag("gate_weights_in"), 80)
                if group >= 4:
                    for k in (2 * group - 8, 2 * group - 7):
                        gate_matmuls(k)

            product(N["gates"][0:2], ahi, alo, between=gates_between)
            product(N["gates"][2:4], ahi, alo)
            pe.wait_ge(flag("pooled"), 1)
            for b in range(2):
                bank = turn_free(N["yturn"] + b)
                for n in range(2):
                    ins = pe.matmul(bank[:, T * n:T * n + T], POOLW[:, 2 * b + n, :], POOLT[:, 2 * b + n, :], start=True, stop=True)
                ins.then_inc(turned, 1)
            emptied(N["yturn"] + 2)
            product(N["pa"], ahi, alo)
            pe.wait_ge(flag("lru_done"), 1)
            product(N["pb"], bhi, blo, between=lambda group:
                    half_t(N["oturn"], 0, ysrc, slab_dve, N["pb"][0].done_dve) if group == 6 else None)

            def out2_between(group):
                if group == 1:
                    half_t(N["oturn"], 1, ysrc, slab_dve, N["pb"][1].done_dve)
                if group == 6:
                    half_t(N["h2turn"], 0, xsrc, slab_dve, N["out"][0].done_dve)

            product(N["out"], ahi, alo, left=N["oturn"], between=out2_between)
            half_t(N["h2turn"], 1, xsrc, slab_dve, N["out"][1].done_dve)
            emptied(N["h2turn"] + 4)
            pe.wait_ge(flag("router_lo"), 1)
            for c in range(C):
                for k in range(KC):
                    ins = mm3(SCB[1][:, 20 * c:20 * c + 20], bhi[:, k, P * c:P * c + P], blo[:, k, P * c:P * c + P],
                              rhi[:, k, :], rlo[:, k, :], k == 0, k == KC - 1)
            ins.then_inc(flag("routed"), 1)
            blocks(N["moe"])


_INS = ["x", "mem", "positions", "norm_mix", "norm_mem", "norm_mem_src", "norm_ffn", "ab_w_in", "ab_w_out",
        "dsa_q_norm", "dsa_k_norm", "moba_q_norm", "moba_k_norm", "nsa_w_in", "nsa_w_out", "nsa_q_norm",
        "nsa_kcmp_norm", "nsa_ksel_norm", "nsa_kwin_norm", "nsa_cmp_pos_k", "nsa_cmp_pos_v", "nsa_cmp_w1_k",
        "nsa_cmp_w2_k", "nsa_cmp_w1_v", "nsa_cmp_w2_v", "mem_w_q", "mem_w_kv", "mem_w_o", "mem_q_norm",
        "mem_k_norm", "ffn_w_in", "ffn_w_out", "norm1_g_2", "w_in_2", "pool_w_2", "pool_scale_2", "conv_w_2",
        "conv_b_2", "rg_w_r_2", "rg_b_r_2", "rg_w_i_2", "rg_b_i_2", "rg_lambda_2", "proj_a_2", "proj_b_2",
        "w_out_2", "norm2_g_2", "router_group_w_2", "router_group_b_2", "router_expert_w_2",
        "router_expert_b_2", "exp_w_gate_2", "exp_w_up_2", "exp_w_down_2", "norm_f_g_2"]


def kernel(**inputs):
    import concourse.bacc as bacc
    from concourse.bass_utils import run_bass_kernel_spmd

    nc = bacc.Bacc("TRN2", target_bir_lowering=False, num_devices=1)
    arrays, aps = {}, {}
    for name in _INS:
        v = np.ascontiguousarray(inputs[name])
        arrays[f"in_{name}"] = v
        aps[name] = nc.dram_tensor(f"in_{name}", v.shape, mybir.dt.from_np(v.dtype), kind="ExternalInput").ap()
    out = nc.dram_tensor("out_0", (1, T, D), F32, kind="ExternalOutput").ap()
    build(nc, aps, out)
    r = run_bass_kernel_spmd(nc, [arrays], core_ids=[0])
    return r.results[0]["out_0"]
```
